# Optimizing a Trainium2 kernel written in Bass

```python
import math
import jax, jax.numpy as jnp
from jax import lax
import numpy as np

D_MODEL = 1024
BATCH = 1
SEQ = 1024
DEPTH = 1

PLE_DIM = 256
D_POOL = D_MODEL // 2
POOL_WINDOWS = (2, 4, 8, 16)
N_POOL_GROUPS = len(POOL_WINDOWS)
POOL_GROUP_DIM = D_POOL // N_POOL_GROUPS
SB_HEADS = 8
SB_HEAD_DIM = 64
D_SB = SB_HEADS * SB_HEAD_DIM
Q_BLOCK = 128
D_FF = ((8 * D_MODEL // 3 + 255) // 256) * 256
D_IN = D_POOL + 3 * D_SB + 2 * D_MODEL
RMS_EPS = 1e-6


def rms_norm(x, gain):
    xf = x.astype(jnp.float32)
    inv = lax.rsqrt(jnp.mean(xf * xf, axis=-1, keepdims=True) + RMS_EPS)
    return (xf * inv * gain.astype(jnp.float32)).astype(x.dtype)

def pool_mixer(u, w_pool, pool_scale):
    B, S, _ = u.shape
    uf = u.astype(jnp.float32)
    csum = jnp.cumsum(uf, axis=1)
    t = jnp.arange(S, dtype=jnp.int32)
    outs = []
    for g, w in enumerate(POOL_WINDOWS):
        sl = slice(g * POOL_GROUP_DIM, (g + 1) * POOL_GROUP_DIM)
        cg = csum[..., sl]
        prev = jnp.pad(cg, ((0, 0), (w, 0), (0, 0)))[:, :S]
        count = jnp.minimum(t + 1, w).astype(jnp.float32)[None, :, None]
        outs.append((cg - prev) / count - uf[..., sl])
    pooled = jnp.stack(outs, axis=2).astype(u.dtype)
    mixed = jnp.einsum('bsgc,gcd->bsgd', pooled, w_pool).reshape(B, S, D_POOL)
    return mixed * pool_scale

def stick_breaking_attention(q, k, v):
    B, H, S, dh = q.shape
    n_blk = S // Q_BLOCK
    scale = 1.0 / math.sqrt(dh)
    q_blocks = q.reshape(B, H, n_blk, Q_BLOCK, dh).transpose(2, 0, 1, 3, 4)
    starts = jnp.arange(n_blk, dtype=jnp.int32) * Q_BLOCK
    k_pos = jnp.arange(S, dtype=jnp.int32)

    def one_block(args):
        q_i, start = args
        z = jnp.einsum('bhqd,bhkd->bhqk', q_i, k).astype(jnp.float32) * scale
        t_pos = start + jnp.arange(Q_BLOCK, dtype=jnp.int32)
        mask = k_pos[None, :] < t_pos[:, None]
        log_fail = jnp.where(mask, jax.nn.log_sigmoid(-z), 0.0)
        suffix = lax.cumsum(log_fail, axis=3, reverse=True) - log_fail
        a = jnp.where(mask, jnp.exp(jax.nn.log_sigmoid(z) + suffix), 0.0)
        return jnp.einsum('bhqk,bhkd->bhqd', a.astype(v.dtype), v)

    out = lax.map(one_block, (q_blocks, starts))
    return out.transpose(1, 2, 0, 3, 4).reshape(B, H, S, dh)

def first_inputs(seed: int = 0) -> dict:
    key = jax.random.key(seed)
    ks = jax.random.split(key, 20)
    f32 = jnp.float32

    def nrm(k, shape, fan_in):
        return jax.random.normal(k, shape, f32) * (fan_in ** -0.5)

    def gain(k, shape):
        return jnp.ones(shape, f32) + 0.02 * jax.random.normal(k, shape, f32)

    return {
        "x": jax.random.normal(ks[0], (BATCH, SEQ, D_MODEL), f32),
        "p": jax.random.normal(ks[1], (DEPTH, BATCH, SEQ, PLE_DIM), f32),
        "norm_mix": gain(ks[2], (DEPTH, D_MODEL)),
        "w_in": nrm(ks[3], (DEPTH, D_MODEL, D_IN), D_MODEL),
        "w_pool": nrm(ks[4], (DEPTH, N_POOL_GROUPS, POOL_GROUP_DIM, POOL_GROUP_DIM), POOL_GROUP_DIM),
        "pool_scale": gain(ks[5], (DEPTH, D_POOL)),
        "w_branch_a": nrm(ks[6], (DEPTH, D_POOL, D_MODEL), D_POOL),
        "w_branch_b": nrm(ks[7], (DEPTH, D_SB, D_MODEL), D_SB),
        "w_out": nrm(ks[8], (DEPTH, D_MODEL, D_MODEL), D_MODEL),
        "norm_ffn": gain(ks[9], (DEPTH, D_MODEL)),
        "w_ffn_gate": nrm(ks[10], (DEPTH, D_MODEL, D_FF), D_MODEL),
        "w_ffn_up": nrm(ks[11], (DEPTH, D_MODEL, D_FF), D_MODEL),
        "w_ffn_down": nrm(ks[12], (DEPTH, D_FF, D_MODEL), D_FF),
        "norm_ple": gain(ks[13], (DEPTH, D_MODEL)),
        "w_ple_gate": nrm(ks[14], (DEPTH, D_MODEL, D_MODEL), D_MODEL),
        "w_ple_proj": nrm(ks[15], (DEPTH, PLE_DIM, D_MODEL), PLE_DIM),
        "norm_final": gain(ks[16], (D_MODEL,)),
    }

def first_block(x, p, norm_mix, w_in, w_pool, pool_scale, w_branch_a, w_branch_b, w_out,
              norm_ffn, w_ffn_gate, w_ffn_up, w_ffn_down, norm_ple, w_ple_gate, w_ple_proj,
              norm_final):
    B, S, _ = x.shape
    split_at = [D_POOL, D_POOL + D_SB, D_POOL + 2 * D_SB, D_POOL + 3 * D_SB,
                D_POOL + 3 * D_SB + D_MODEL]
    for i in range(DEPTH):
        h = rms_norm(x, norm_mix[i])
        proj = h @ w_in[i]
        u_pool, q, k, v, g_a, g_b = jnp.split(proj, split_at, axis=-1)
        y_a = pool_mixer(u_pool, w_pool[i], pool_scale[i])
        to_heads = lambda t: t.reshape(B, S, SB_HEADS, SB_HEAD_DIM).transpose(0, 2, 1, 3)
        y_b = stick_breaking_attention(to_heads(q), to_heads(k), to_heads(v))
        y_b = y_b.transpose(0, 2, 1, 3).reshape(B, S, D_SB)
        merged = (jax.nn.sigmoid(g_a) * (y_a @ w_branch_a[i])
                  + jax.nn.sigmoid(g_b) * (y_b @ w_branch_b[i]))
        x = x + merged @ w_out[i]
        h = rms_norm(x, norm_ffn[i])
        x = x + (jax.nn.silu(h @ w_ffn_gate[i]) * (h @ w_ffn_up[i])) @ w_ffn_down[i]
        gate = jax.nn.sigmoid(rms_norm(x, norm_ple[i]) @ w_ple_gate[i])
        x = x + gate * (p[i] @ w_ple_proj[i])
    return rms_norm(x, norm_final)


A_HEADS = 8
A_HEAD_DIM = 64
A_WIDTH = A_HEADS * A_HEAD_DIM
DECAY_LORA = 64
ICLR_LORA = 64
DECAY_SCALE = 0.6065306597
GN_EPS = 64e-5
B_HEADS = 8
QK_NOPE_DIM = 64
QK_ROPE_DIM = 32
V_HEAD_DIM = 64
Q_LORA_RANK = 256
KV_LORA_RANK = 128
B_WIDTH = B_HEADS * V_HEAD_DIM
ROPE_THETA = 10000.0
NORM_EPS = 1e-6
N_BRANCHES = 2
SHIFT_COLS = 3 * A_WIDTH + DECAY_LORA + ICLR_LORA
IN_COLS = SHIFT_COLS + A_WIDTH + Q_LORA_RANK + KV_LORA_RANK + QK_ROPE_DIM + B_WIDTH + N_BRANCHES * D_MODEL


def rmsnorm(x, g, eps=NORM_EPS):
    xf = x.astype(jnp.float32)
    y = xf * lax.rsqrt(jnp.mean(xf * xf, axis=-1, keepdims=True) + eps)
    return (y * g.astype(jnp.float32)).astype(x.dtype)

def split_cols(t, sizes):
    idx = np.cumsum(sizes)[:-1].tolist()
    return jnp.split(t, idx, axis=-1)

def token_shift(feat, mu):
    prev = jnp.pad(feat, ((0, 0), (1, 0), (0, 0)))[:, :-1, :]
    return feat + mu * (prev - feat)

def rwkv7_branch(feat, z, mu_shift, w0, w_decay_up, a0, w_iclr_up, k_k, k_a, r_k, gn_gain, gn_bias, w_out_a):
    bsz, seq, _ = feat.shape
    dt = feat.dtype
    f = token_shift(feat, mu_shift)
    r, k, v, wd, ad = split_cols(f, [A_WIDTH, A_WIDTH, A_WIDTH, DECAY_LORA, ICLR_LORA])
    w_logit = (w0 + jnp.tanh(wd) @ w_decay_up).astype(jnp.float32)
    w = jnp.exp(-DECAY_SCALE * jax.nn.sigmoid(w_logit))
    a = jax.nn.sigmoid((a0 + ad @ w_iclr_up).astype(jnp.float32))
    hs = lambda t: t.reshape(bsz, seq, A_HEADS, A_HEAD_DIM).astype(jnp.float32)
    r, k, v, w, a = hs(r), hs(k), hs(v), hs(w), hs(a)
    kk = k * k_k.reshape(A_HEADS, A_HEAD_DIM)
    kk = kk / jnp.maximum(jnp.linalg.norm(kk, axis=-1, keepdims=True), 1e-12)
    k = k * (1.0 + (a - 1.0) * k_a.reshape(A_HEADS, A_HEAD_DIM))

    def step(S, inp):
        r_t, w_t, k_t, v_t, kk_t, a_t = inp
        sa = jnp.einsum('bhvk,bhk->bhv', S, -kk_t)
        S = S * w_t[:, :, None, :] + sa[..., None] * (kk_t * a_t)[:, :, None, :] + v_t[..., None] * k_t[:, :, None, :]
        return S, jnp.einsum('bhvk,bhk->bhv', S, r_t)

    tm = lambda t: jnp.moveaxis(t, 1, 0)
    S0 = jnp.zeros((bsz, A_HEADS, A_HEAD_DIM, A_HEAD_DIM), jnp.float32)
    _, y = lax.scan(step, S0, (tm(r), tm(w), tm(k), tm(v), tm(kk), tm(a)))
    y = jnp.moveaxis(y, 0, 1)
    mean = jnp.mean(y, axis=-1, keepdims=True)
    var = jnp.mean(jnp.square(y - mean), axis=-1, keepdims=True)
    y = (y - mean) * lax.rsqrt(var + GN_EPS)
    y = y * gn_gain.reshape(A_HEADS, A_HEAD_DIM) + gn_bias.reshape(A_HEADS, A_HEAD_DIM)
    y = y + jnp.sum(r * k * r_k, axis=-1, keepdims=True) * v
    y = y.reshape(bsz, seq, A_WIDTH).astype(dt) * jax.nn.silu(z)
    return y @ w_out_a

def rope(t, cos, sin):
    t1, t2 = jnp.split(t, 2, axis=-1)
    return jnp.concatenate([t1 * cos - t2 * sin, t2 * cos + t1 * sin], axis=-1)

def mla_branch(c_q, c_kv, k_pe, z, positions, g_q, w_uq, g_kv, w_ukv, w_out_b):
    bsz, seq, _ = c_q.shape
    dt = c_q.dtype
    q = (rmsnorm(c_q, g_q) @ w_uq).reshape(bsz, seq, B_HEADS, QK_NOPE_DIM + QK_ROPE_DIM)
    q_nope, q_pe = q[..., :QK_NOPE_DIM], q[..., QK_NOPE_DIM:]
    kv = (rmsnorm(c_kv, g_kv) @ w_ukv).reshape(bsz, seq, B_HEADS, QK_NOPE_DIM + V_HEAD_DIM)
    k_nope, v = kv[..., :QK_NOPE_DIM], kv[..., QK_NOPE_DIM:]
    inv_freq = ROPE_THETA ** (-jnp.arange(0, QK_ROPE_DIM, 2, dtype=jnp.float32) / QK_ROPE_DIM)
    ang = positions.astype(jnp.float32)[..., None] * inv_freq
    cos, sin = jnp.cos(ang).astype(dt), jnp.sin(ang).astype(dt)
    q_pe = rope(q_pe, cos[:, :, None, :], sin[:, :, None, :])
    k_pe = rope(k_pe, cos, sin)
    scale = 1.0 / math.sqrt(QK_NOPE_DIM + QK_ROPE_DIM)
    nb = seq // Q_BLOCK
    blk = lambda t: jnp.moveaxis(t.reshape(bsz, nb, Q_BLOCK, *t.shape[2:]), 1, 0)
    key_idx = jnp.arange(seq)

    def attend(args):
        qn, qp, b = args
        s = jnp.einsum('bqhd,bkhd->bhqk', qn, k_nope) + jnp.einsum('bqhr,bkr->bhqk', qp, k_pe)
        s = s.astype(jnp.float32) * scale
        q_idx = b * Q_BLOCK + jnp.arange(Q_BLOCK)
        s = jnp.where(key_idx[None, :] <= q_idx[:, None], s, jnp.finfo(jnp.float32).min)
        p = jax.nn.softmax(s, axis=-1).astype(dt)
        return jnp.einsum('bhqk,bkhd->bqhd', p, v)

    o = lax.map(attend, (blk(q_nope), blk(q_pe), jnp.arange(nb)))
    o = jnp.moveaxis(o, 0, 1).reshape(bsz, seq, B_WIDTH)
    return (o * jax.nn.silu(z)) @ w_out_b

def second_inputs(seed: int = 0) -> dict:
    key = jax.random.key(seed)
    ks = jax.random.split(key, 24)
    n = lambda i, shape, s=1.0: s * jax.random.normal(ks[i], shape, jnp.float32)
    x = n(0, (BATCH, SEQ, D_MODEL))
    positions = (jnp.arange(SEQ, dtype=jnp.int32)[None, :]
                 + jax.random.randint(ks[1], (BATCH, 1), 0, 1024, dtype=jnp.int32))
    return {
        'x': x,
        'positions': positions,
        'g_pre': 1.0 + n(2, (D_MODEL,), 0.05),
        'w_in': n(3, (D_MODEL, IN_COLS), D_MODEL ** -0.5),
        'b_gate': n(4, (N_BRANCHES * D_MODEL,), 0.01),
        'mu_shift': jax.random.uniform(ks[5], (SHIFT_COLS,), jnp.float32),
        'w0': n(6, (A_WIDTH,), 0.5),
        'w_decay_up': n(7, (DECAY_LORA, A_WIDTH), 0.1),
        'a0': n(8, (A_WIDTH,), 0.5),
        'w_iclr_up': n(9, (ICLR_LORA, A_WIDTH), 0.5 * ICLR_LORA ** -0.5),
        'k_k': 0.85 + n(10, (A_WIDTH,), 0.05),
        'k_a': 1.0 + n(11, (A_WIDTH,), 0.05),
        'r_k': n(12, (A_HEADS, A_HEAD_DIM), 0.1),
        'gn_gain': 1.0 + n(13, (A_WIDTH,), 0.05),
        'gn_bias': n(14, (A_WIDTH,), 0.01),
        'w_out_a': n(15, (A_WIDTH, D_MODEL), A_WIDTH ** -0.5),
        'g_q': 1.0 + n(16, (Q_LORA_RANK,), 0.05),
        'w_uq': n(17, (Q_LORA_RANK, B_HEADS * (QK_NOPE_DIM + QK_ROPE_DIM)), Q_LORA_RANK ** -0.5),
        'g_kv': 1.0 + n(18, (KV_LORA_RANK,), 0.05),
        'w_ukv': n(19, (KV_LORA_RANK, B_HEADS * (QK_NOPE_DIM + V_HEAD_DIM)), KV_LORA_RANK ** -0.5),
        'w_out_b': n(20, (B_WIDTH, D_MODEL), B_WIDTH ** -0.5),
        'w_o': n(21, (D_MODEL, D_MODEL), D_MODEL ** -0.5),
        'g_post': 1.0 + n(22, (D_MODEL,), 0.05),
    }

def second_block(x, positions, g_pre, w_in, b_gate, mu_shift, w0, w_decay_up, a0, w_iclr_up, k_k, k_a, r_k,
              gn_gain, gn_bias, w_out_a, g_q, w_uq, g_kv, w_ukv, w_out_b, w_o, g_post):
    h = x
    for _ in range(DEPTH):
        u = rmsnorm(h, g_pre)
        proj = u @ w_in
        feat_a, z_a, c_q, c_kv, k_pe, z_b, gate_logits = split_cols(
            proj, [SHIFT_COLS, A_WIDTH, Q_LORA_RANK, KV_LORA_RANK, QK_ROPE_DIM, B_WIDTH, N_BRANCHES * D_MODEL])
        y_a = rwkv7_branch(feat_a, z_a, mu_shift, w0, w_decay_up, a0, w_iclr_up, k_k, k_a, r_k,
                           gn_gain, gn_bias, w_out_a)
        y_b = mla_branch(c_q, c_kv, k_pe, z_b, positions, g_q, w_uq, g_kv, w_ukv, w_out_b)
        gates = jax.nn.sigmoid(gate_logits + b_gate)
        g_a, g_b = gates[..., :D_MODEL], gates[..., D_MODEL:]
        merged = g_a * y_a + g_b * y_b
        h = h + rmsnorm(merged @ w_o, g_post)
    return h


def setup_inputs(seed=0):
    out = dict(first_inputs(seed))
    for name, value in second_inputs(seed + 1).items():
        if name != "x":
            out[name + "_2"] = value
    return out


def reference(
    x, p, norm_mix, w_in, w_pool, pool_scale, w_branch_a, w_branch_b, w_out, norm_ffn,
    w_ffn_gate, w_ffn_up, w_ffn_down, norm_ple, w_ple_gate, w_ple_proj, norm_final, positions_2,
    g_pre_2, w_in_2, b_gate_2, mu_shift_2, w0_2, w_decay_up_2, a0_2, w_iclr_up_2, k_k_2, k_a_2,
    r_k_2, gn_gain_2, gn_bias_2, w_out_a_2, g_q_2, w_uq_2, g_kv_2, w_ukv_2, w_out_b_2, w_o_2,
    g_post_2,
):
    x = first_block(
        x, p, norm_mix, w_in, w_pool, pool_scale, w_branch_a, w_branch_b, w_out, norm_ffn,
        w_ffn_gate, w_ffn_up, w_ffn_down, norm_ple, w_ple_gate, w_ple_proj, norm_final,
    )
    return second_block(
        x, positions_2, g_pre_2, w_in_2, b_gate_2, mu_shift_2, w0_2, w_decay_up_2, a0_2,
        w_iclr_up_2, k_k_2, k_a_2, r_k_2, gn_gain_2, gn_bias_2, w_out_a_2, g_q_2, w_uq_2,
        g_kv_2, w_ukv_2, w_out_b_2, w_o_2, g_post_2,
    )


_drawn_inputs = setup_inputs


def setup_inputs(seed=0):
    import zlib

    import numpy as np

    out = dict(_drawn_inputs(seed))
    spreads = {}
    factors = {'pool_scale': 3.754,
     'norm_ple': 8.0,
     'b_gate_2': 8.0,
     'k_k_2': 48.2,
     'gn_bias_2': 57.728,
     'g_q_2': 8.0,
     'g_kv_2': 7.702,
     'w0_2': 3.371,
     'w_decay_up_2': 6.325,
     'w_iclr_up_2': 2.88,
     'k_a_2': 8.0,
     'gn_gain_2': 8.0}
    for name, (base, spread) in spreads.items():
        noise = np.random.default_rng([zlib.crc32(name.encode()), seed]).standard_normal(out[name].shape)
        drawn = base * np.exp(spread * noise) if base else spread * noise
        out[name] = __import__('jax').numpy.asarray(drawn.astype(out[name].dtype))
    for name, factor in factors.items():
        out[name] = (out[name] * factor).astype(out[name].dtype)
    return out
```

```python
from contextlib import ExitStack

import numpy as np

import concourse.bass as bass
from concourse import mybir

F32 = mybir.dt.float32
F32R = mybir.dt.float32r
I32 = mybir.dt.int32
ACT = mybir.ActivationFunctionType
ALU = mybir.AluOpType
AX = mybir.AxisListType

P = 128
D = 1024
S = 1024
HALF = 512
KT = D // P
SUB = 8
NEG = -1.0e30
EPS = 1e-6

POOL_GROUPS = 4
WINDOWS = (2, 4, 8, 16)
PAIRS = 4
HD = 64
FF = 2816
FF_TILES = FF // P
FF_CHUNKS = (8, 8, 6)
assert sum(FF_CHUNKS) == FF_TILES

GN_EPS = 64e-5
DECAY = 0.6065306597
CH = 64
NC = HALF // CH
LEVELS = 5
ROPE = 32
ROPE_THETA = 10000.0
MLA_SCALE = (HD + ROPE) ** -0.5
ROUND = 1.5 * 2.0 ** 23
TWO_PI = (6.28125, 1.93500518798828125e-3, 3.0199159819e-07)
PI_BELOW = 3.1415925

CONST = {}
_at = 0
for _name, _width in (("ident", P), ("mean", P), ("headsum", P), ("neg_tri", P), ("neg_ones", P),
                      ("sb_mask", P), ("mla_mask", P), ("pair_ident", HD), ("strict_t", HD), ("strict", HD),
                      ("incl_t", HD), ("lev0", HD), ("lev0_t", HD), ("lev1", HD), ("lev2", HD), ("lev3", HD),
                      ("lev4", HD), ("lev5", HD), ("rope_sum", P), ("pool_count", 64), ("reset", HALF),
                      ("rope", 8)):
    CONST[_name] = (_at, _at + _width)
    _at += _width
N_CONST = _at

VEC = {}
_at = 0
for _name, _width in (("norm_mix", 8), ("norm_ffn", 8), ("norm_ple", 8), ("norm_final", 8), ("pool_scale", 4),
                      ("g_pre", 8), ("g_post", 8), ("b_gate", 16), ("mu", 13), ("w0", 4), ("a0", 4), ("k_k", 4),
                      ("k_a", 4), ("r_k", 4), ("gn_gain", 4), ("gn_bias", 4), ("g_q", 2), ("g_kv", 1)):
    VEC[_name] = _at
    _at += _width
N_VEC = _at

BLK = {"pool": 0}
TILE = {"pool": 0}


def _stage(name, after, blocks, tiles):
    BLK[name] = BLK[after] + blocks
    TILE[name] = TILE[after] + tiles


_stage("sb", "pool", 4, 4)
_stage("merge", "sb", 16, 16)
_stage("out", "merge", 24, 32)
_stage("ffn", "out", 8, 8)
_stage("ple", "ffn", 2 * FF_TILES + KT * len(FF_CHUNKS), 2 * FF_TILES + KT * len(FF_CHUNKS))
_stage("mla", "ple", 16, 16)
_stage("rwkv", "mla", 4 + 2 * 4, 4 + 6 * 4)
_stage("merge2", "rwkv", 2 + 4 * 4, 2 + 6 * 4)
_stage("out2", "merge2", 24, 32)
_stage("end", "out2", 8, 8)


class Core:

    def __init__(self, nc, ctx):
        self.nc, self.ctx, self.sems = nc, ctx, {}

    def sem(self, name):
        if name not in self.sems:
            self.sems[name] = self.ctx.enter_context(self.nc.semaphore(name))
        return self.sems[name]

    def at(self, name, offset, shape, dt=F32):
        return self.nc.alloc_sbuf_tensor_at(name, [P, *shape], dt, offset=offset)


def layout(nc, ctx):
    k = Core(nc, ctx)
    kb = 1024
    W = 16512
    K = W + 24 * kb
    H = K + 10 * kb
    X = H + 64 * kb
    C = X + 32 * kb
    V = C + 64 * kb
    k.w_raw = k.at("w_raw", W, [2, SUB, P])
    k.w_hi = k.at("w_hi", W + 8 * kb, [2, SUB, P], F32R)
    k.w_lo = k.at("w_lo", W + 16 * kb, [2, SUB, P], F32R)
    k.const = k.at("const", K, [N_CONST])
    k.vec = k.at("vec", V + 12 * kb, [N_VEC])
    k.one = k.at("one", V + 12 * kb + 4 * N_VEC, [1])
    k.h_hi = k.at("h_hi", H, [KT, S], F32R)
    k.h_lo = k.at("h_lo", H + 32 * kb, [KT, S], F32R)
    k.x = k.at("x_res", X, [KT, S])
    k.inv = k.at("inv", V, [S])
    k.tmp0 = k.at("tmp0", V + 4 * kb, [S])
    k.tmp1 = k.at("tmp1", V + 8 * kb, [S])
    k.tmp = [k.tmp0, k.tmp1]
    k.sq = [k.tmp0, k.tmp1]
    k.sq_ple = [k.at(f"sq_ple{n}", C + (24 + 4 * n) * kb, [S]) for n in range(2)]
    k.sumsq = k.at("sumsq", C + 56 * kb, [S])
    k.std = k.at("std", C + 60 * kb, [S])
    k.u_pad = k.at("u_pad", X, [16 + S])
    k.win = [k.at(f"win{n}", X + (n + 1) * 4160, [16 + S]) for n in range(2)]
    k.pooled = k.at("pooled", X + 3 * 4160, [S])
    k.ya_hi = k.at("ya_hi", C, [4, S], F32R)
    k.ya_lo = k.at("ya_lo", C + 16 * kb, [4, S], F32R)
    k.yb_hi = k.at("yb_hi", C + 32 * kb, [4, S], F32R)
    k.yb_lo = k.at("yb_lo", C + 48 * kb, [4, S], F32R)
    k.sb_q = k.at("sb_q", X, [S])
    k.sb_k = k.at("sb_k", X + 4 * kb, [S])
    k.sb_v = k.at("sb_v", X + 8 * kb, [KT, P])
    k.sb_e = k.at("sb_e", X + 12 * kb, [2, HALF])
    k.sb_sp = k.at("sb_sp", X + 16 * kb, [3, HALF])
    k.sb_acc = k.at("sb_acc", X + 22 * kb, [2, 2, HALF])
    k.sb_o = k.at("sb_o", X + 30 * kb, [4, P])
    k.sb_vt = k.at("sb_vt", V + 4 * kb, [S])
    k.sb_a = k.at("sb_a", V + 8 * kb, [2, HALF])
    k.merged = k.at("merged", X, [KT, S])
    k.x_again = k.at("x_again", C, [KT, S])
    k.hid_hi = k.at("hid_hi", C, [SUB, S], F32R)
    k.hid_lo = k.at("hid_lo", C + 32 * kb, [SUB, S], F32R)
    k.p_raw = k.at("p_raw", C + 16 * kb, [2, S])
    k.p_hi = k.at("p_hi", C, [2, S], F32R)
    k.p_lo = k.at("p_lo", C + 8 * kb, [2, S], F32R)
    k.cq_hi = k.at("cq_hi", X, [2, S], F32R)
    k.cq_lo = k.at("cq_lo", X + 8 * kb, [2, S], F32R)
    k.ckv_hi = k.at("ckv_hi", X + 16 * kb, [1, S], F32R)
    k.ckv_lo = k.at("ckv_lo", X + 20 * kb, [1, S], F32R)
    k.trig = k.at("trig", X + 24 * kb, [S])
    k.inv_q = k.at("inv_q", X + 28 * kb, [S])
    k.inv_kv = k.at("inv_kv", C, [S])
    k.mla_k = k.at("mla_k", C + 4 * kb, [S])
    k.mla_q = k.at("mla_q", C + 8 * kb, [S])
    k.mla_v = k.at("mla_v", C + 12 * kb, [2, KT, HD])
    k.mla_p = k.at("mla_p", C + 16 * kb, [2, S])
    k.mla_o = k.at("mla_o", C + 24 * kb, [KT, P])
    k.mla_gate = k.at("mla_gate", C + 28 * kb, [S])
    k.mla_vt = k.at("mla_vt", V + 4 * kb, [S])
    k.mla_out = k.at("mla_out", C + 32 * kb, [4, S])
    k.mla_pt = k.at("mla_pt", V + 8 * kb, [2, HALF])
    k.latent = k.at("latent", C + 32 * kb, [3, S])
    k.latent_sq = k.at("latent_sq", C + 44 * kb, [3, S])
    k.latent_std = k.at("latent_std", C + 56 * kb, [2, S])
    k.pos = k.at("pos", V + 4 * kb, [S], I32)
    k.angle = k.at("angle", V + 8 * kb, [S])
    k.turns = k.at("turns", X + 16 * kb, [S])
    k.pe_raw = k.at("pe_raw", X + 20 * kb, [S])
    free = V + 12 * kb + 4 * N_VEC + 32
    k.mla_max = k.at("mla_max", free, [2, 2])
    k.mla_sum = k.at("mla_sum", free + 32, [2, 2])
    k.rw_pad = [k.at(f"rw_{name}", X + 4128 * n, [S + 1]) for n, name in enumerate("rkv")]
    k.rw_r, k.rw_k, k.rw_v = (t[:, 1:S + 1] for t in k.rw_pad)
    at = X + 3 * 4128
    k.rw_z = k.at("rw_z", at, [S])
    k.rw_sg = k.at("rw_sg", at + 4 * kb, [S])
    k.rw_b = k.at("rw_b", at + 8 * kb, [S])
    k.rw_kk = k.at("rw_kk", at + 12 * kb, [S])
    k.rw_rp = k.at("rw_rp", at + 16 * kb, [HALF])
    at += 18 * kb
    k.rw_s = k.at("rw_s", at, [HD])
    k.rw_pc = k.at("rw_pc", at + 256, [S // CH])
    assert at + 320 <= C
    k.rw_up = k.at("rw_up", K + 4 * N_CONST + 32, [P])
    k.rw_l = k.at("rw_l", C, [S])
    k.rw_wdad = k.at("rw_wdad", C + 4 * kb, [S])
    k.rw_kkp = k.at("rw_kkp", C + 8 * kb, [HALF])
    k.rw_bq = k.at("rw_bq", C + 10 * kb, [HALF])
    k.rw_y = k.at("rw_y", C + 12 * kb, [HALF])
    k.rw_out = k.at("rw_out", C + 14 * kb, [2, HALF])
    k.rw_bds = k.at("rw_bds", C + 18 * kb, [9, NC, P])
    k.rw_bd = [k.rw_bds[:, n] for n in range(3)]
    (k.rw_lt_bd, k.rw_akt_bd, k.rw_xt_bd, k.rw_t1_bd, k.rw_ke_tm, k.rw_kkp_tm) = (k.rw_bds[:, n] for n in range(3, 9))
    k.rw_arbt = k.at("rw_arbt", C + 54 * kb, [NC, HD])
    k.rw_arkt = k.at("rw_arkt", C + 56 * kb, [NC, HD])
    k.rw_xm = k.at("rw_xm", C + 58 * kb, [NC, HD])
    k.rw_xt = k.at("rw_xt", C + 60 * kb, [NC, HD])
    k.rw_t1 = k.at("rw_t1", C + 62 * kb, [NC, HD])
    k.rw_v_tm = k.at("rw_v_tm", V + 4 * kb, [NC, HD])
    k.rw_t = [k.at(f"rw_t{n}", V + (6 + 2 * n) * kb, [HALF]) for n in range(3)]
    k.rw_s_all = k.at("rw_s_all", V + 6 * kb, [NC, HD])
    k.rw_d = k.at("rw_d", V + 4 * kb, [S])
    k.rw_e = k.at("rw_e", V + 8 * kb, [S])
    k.branches = k.at("branches_again", X, [8, S])
    k.x1_again = k.at("x1_again", C, [KT, S])
    k.dps = nc.alloc_psum_tensor("dps", [P, 2, S], F32)
    k.aps = nc.alloc_psum_tensor("aps", [P, 4, HALF], F32)
    return k


def const(k, name, lo=0, hi=P):
    a, b = CONST[name]
    return k.const[lo:hi, a:b]


def vec(k, name, n):
    return k.vec[:, bass.ds(n + VEC[name], 1)] if not isinstance(n, int) else k.vec[:, VEC[name] + n:VEC[name] + n + 1]


def one(t, n):
    return t[:, n, :] if isinstance(n, int) else t[:, bass.ds(n, 1), :].rearrange("p a t -> p (a t)")


def dense(k, pe, blk, slot, sub, rhs_hi, rhs_lo, n_k, pair, use, done, rows=P, ready=None,
          first=True, last=True):
    pe.wait_ge(k.sem("w_split"), blk + 1)
    if first:
        pe.wait_ge(k.sem(f"pair{pair}_out"), use + 1)
    for t in range(n_k):
        if ready is not None:
            pe.wait_ge(k.sem(ready[0]), ready[1] + t + 1)
        for n, (w, x) in enumerate(((k.w_hi, rhs_hi), (k.w_hi, rhs_lo), (k.w_lo, rhs_hi))):
            for h in range(2):
                mm = k.nc.tensor.matmul(k.dps[0:rows, pair, h * HALF:(h + 1) * HALF], w[:, slot, sub + t, 0:rows],
                                        x(t)[:, h * HALF:(h + 1) * HALF],
                                        start=first and t == 0 and n == 0, stop=last and t == n_k - 1 and n == 2)
    mm.then_inc(k.sem(done), 1)


def stat(k, pe, norm):
    pe.wait_ge(k.sem("sumsq_done"), KT * (norm + 1) + 2)
    for h in range(2):
        mm = k.nc.tensor.matmul(k.aps[:, h, :], const(k, "mean"), k.sumsq[:, h * HALF:(h + 1) * HALF],
                                start=True, stop=True)
    mm.then_inc(k.sem("stat_done"), 1)


def fixed_wait(k, act):
    act.wait_ge(k.sem("vec_loaded"), 16)


def split_act(k, act, n, gain=None, src=None):
    src = k.x if src is None else src
    scale = 1.0 if gain is None else vec(k, gain, n)
    if not isinstance(n, int):
        fixed_wait(k, act)
    k.nc.scalar.activation(one(k.h_hi, n), one(src, n), ACT.Copy, scale=scale).then_inc(k.sem("h_hi_done"), 1)


def split_dve(k, dve, fill, n, gain=None, src=None):
    src = k.x if src is None else src
    dve.wait_ge(k.sem("h_hi_done"), n + (KT * fill + 1))
    if gain is None:
        ins = k.nc.vector.tensor_tensor(one(k.h_lo, n), one(src, n), one(k.h_hi, n).bitcast(F32), ALU.subtract)
    else:
        ins = k.nc.vector.scalar_tensor_tensor(one(k.h_lo, n), one(src, n), vec(k, gain, n),
                                               one(k.h_hi, n).bitcast(F32), ALU.mult, ALU.subtract)
    ins.then_inc(k.sem("h_lo_done"), 1)


def square_wait(k, act, norm, n):
    act.wait_ge(k.sem("sumsq_done"), n + (KT * norm + 1))


def square_act(k, act, norm, n, sq, waited=False):
    if not waited:
        square_wait(k, act, norm, n)
    if not isinstance(n, int) and not waited:
        fixed_wait(k, act)
    k.nc.scalar.activation(sq, one(k.x, n), ACT.Square).then_inc(k.sem("sq_done"), 1)


def sumsq_begin(k, dve, norm):
    if norm:
        dve.wait_ge(k.sem("stat_done"), norm)
    k.nc.vector.memset(k.sumsq[:, :], 0.0).then_inc(k.sem("sumsq_zero"), 1)
    dve.wait_ge(k.sem("sumsq_zero"), norm + 1)


def sumsq_dve(k, dve, norm, n, sq):
    dve.wait_ge(k.sem("sumsq_done"), n + (KT * norm + 2))
    dve.wait_ge(k.sem("sq_done"), n + (KT * norm + 1))
    k.nc.vector.tensor_tensor(k.sumsq[:, :], k.sumsq[:, :], sq, ALU.add).then_inc(k.sem("sumsq_done"), 1)


def inv_act(k, act, norm):
    act.wait_ge(k.sem("stat_done"), norm + 1)
    k.nc.scalar.activation(k.std[:, :], k.aps[:, 0:2, :].rearrange("p a b -> p (a b)"), ACT.Sqrt,
                           bias=EPS).then_inc(k.sem("std_done"), 1)


def inv_dve(k, dve, norm):
    dve.wait_ge(k.sem("std_done"), norm + 1)
    k.nc.vector.reciprocal(k.inv[:, :], k.std[:, :]).then_inc(k.sem("inv_done"), 1)
    dve.wait_ge(k.sem("inv_done"), norm + 1)


def rows(x):
    return lambda t: x[:, t, :]


def entry_act(k, act, x_t):
    for q in range(4):
        act.dma_start(k.x[:, 2 * q:2 * q + 2, :], x_t[:, 2 * q:2 * q + 2, :]).then_inc(k.sem(f"x_loaded{q}"), 16)
    act.wait_ge(k.sem("vec_loaded"), 16)
    for n in range(KT):
        if n % 2 == 0:
            act.wait_ge(k.sem(f"x_loaded{n // 2}"), 16)
        split_act(k, act, n, "norm_mix")
        square_act(k, act, 0, n, k.sq[n % 2][:, :])
    inv_act(k, act, 0)


def entry_dve(k, dve):
    dve.wait_ge(k.sem("vec_loaded"), 16)
    dve.wait_ge(k.sem("const_loaded"), 16)
    sumsq_begin(k, dve, 0)
    for n in range(KT):
        split_dve(k, dve, 0, n, "norm_mix")
        sumsq_dve(k, dve, 0, n, k.sq[n % 2][:, :])
    inv_dve(k, dve, 0)


def pool_pe(k, pe):
    for g in range(POOL_GROUPS):
        dense(k, pe, BLK["pool"] + g, g % 2, 0, rows(k.h_hi), rows(k.h_lo), KT, g % 2, g // 2, "blk_done",
              ready=("h_lo_done", 0) if g == 0 else None)
        if g == 0:
            stat(k, pe, 0)


def pool_dve(k, dve):
    v = k.nc.vector
    v.memset(k.u_pad[:, 0:16], 0.0).then_inc(k.sem("u_zero"), 1)
    sums = 0
    for g, w in enumerate(WINDOWS):
        dve.wait_ge(k.sem("blk_done"), BLK["pool"] + g + 1)
        if g == 0:
            dve.wait_ge(k.sem("inv_done"), 1)
            dve.wait_ge(k.sem("u_zero"), 1)
        v.tensor_tensor(k.u_pad[:, 16:], k.dps[:, g % 2, :], k.inv[:, :], ALU.mult).then_inc(k.sem(f"pair{g % 2}_out"), 1)
        dve.wait_ge(k.sem(f"pair{g % 2}_out"), g // 2 + 2)
        src, reach, step = k.u_pad, 1, 1
        while step < w:
            dst = k.win[0] if src is not k.win[0] else k.win[1]
            v.tensor_tensor(dst[:, reach:], src[:, reach:], src[:, reach - step:16 + S - step],
                            ALU.add).then_inc(k.sem("win_done"), 1)
            sums += 1
            dve.wait_ge(k.sem("win_done"), sums)
            src, step = dst, 2 * step
            reach += step
        if g:
            dve.wait_ge(k.sem("pool_hi_done"), g)
        a = CONST["pool_count"][0] + 16 * g
        v.tensor_tensor(k.pooled[:, 0:16], src[:, 16:32], k.const[:, a:a + 16], ALU.mult).then_inc(k.sem("head_done"), 1)
        v.scalar_tensor_tensor(k.pooled[:, 16:], src[:, 32:], 1.0 / w, k.u_pad[:, 32:], ALU.mult,
                               ALU.subtract).then_inc(k.sem("body_done"), 1)
        dve.wait_ge(k.sem("head_done"), g + 1)
        v.tensor_tensor(k.pooled[:, 0:16], k.pooled[:, 0:16], k.u_pad[:, 16:32], ALU.subtract).then_inc(k.sem("pooled_done"), 1)
        dve.wait_ge(k.sem("pool_hi_done"), g + 1)
        v.tensor_tensor(k.ya_lo[:, g, :], k.pooled[:, :], k.ya_hi[:, g, :].bitcast(F32),
                        ALU.subtract).then_inc(k.sem("pool_lo_done"), 1)


def pool_act(k, act):
    for g in range(POOL_GROUPS):
        act.wait_ge(k.sem("body_done"), g + 1)
        act.wait_ge(k.sem("pooled_done"), g + 1)
        k.nc.scalar.activation(k.ya_hi[:, g, :], k.pooled[:, :], ACT.Copy).then_inc(k.sem("pool_hi_done"), 1)


UNITS = [(c, b, h) for c in range(2) for b in range(4 * c + 3, -1, -1) for h in range(2)]
N_UNITS = len(UNITS)
ACC_COUNT = [sum(1 for _, b, _ in UNITS[:u + 1] if b) for u in range(N_UNITS)]
ACCS = ACC_COUNT[-1]
CHUNK_END = [u for u, (c, b, h) in enumerate(UNITS) if b == 0 and h == 1]


def unit(u):
    c, b, h = UNITS[u]
    return c, b, h, max(0, P * b - HALF * c), 4 * c + 3 - b


def sb_pe(k, pe):
    mul, ident = k.nc.tensor.matmul, const(k, "ident")
    with pe.Fori(0, PAIRS) as i:
        blk, use = i * 4 + BLK["sb"], i * 2 + TILE["sb"] // 2
        dense(k, pe, blk, 0, 0, rows(k.h_hi), rows(k.h_lo), KT, 0, use, "blk_done")
        dense(k, pe, blk + 1, 1, 0, rows(k.h_hi), rows(k.h_lo), KT, 1, use, "blk_done")
        dense(k, pe, blk + 2, 0, 0, rows(k.h_hi), rows(k.h_lo), KT, 0, use + 1, "blk_done")
        pe.wait_ge(k.sem("pool_lo_done"), POOL_GROUPS)
        dense(k, pe, blk + 3, 1, 0, lambda t: one(k.ya_hi, i), lambda t: one(k.ya_lo, i), 1, 1, use + 1, "blk_done")
        pe.wait_ge(k.sem("pair0_out"), use + 3)
        for b in range(KT):
            mm = k.nc.tensor.transpose(k.aps[:, b // 4, (b % 4) * P:(b % 4 + 1) * P], k.sb_vt[:, b * P:(b + 1) * P], ident)
        mm.then_inc(k.sem("sb_vtr_done"), 1)
        pe.wait_ge(k.sem("pair1_out"), use + 2)
        pe.wait_ge(k.sem("sb_v_done"), i + 1)
        for s in range(N_UNITS + 3):
            if s < N_UNITS:
                c, b, h, lo, n = unit(s)
                head = slice(h * HD, (h + 1) * HD)
                if s >= 3:
                    pe.wait_ge(k.sem("sb_a_done"), i * N_UNITS + (s - 2))
                mm = mul(k.aps[:, s % 3, lo:HALF], k.sb_k[head, b * P:(b + 1) * P], k.sb_q[head, c * HALF + lo:(c + 1) * HALF],
                         start=True, stop=False, skip_group_check=True)
                if b >= 4 * c:
                    mm = mul(k.aps[:, s % 3, lo:lo + P], ident, const(k, "sb_mask"), start=False, stop=False, skip_group_check=True)
                mm.then_inc(k.sem("sb_z_done"), 1)
            if 2 <= s < N_UNITS + 2:
                c, b, h, lo, n = unit(s - 2)
                bank = (s - 2) % 3
                pe.wait_ge(k.sem("sb_sp_done"), i * N_UNITS + (s - 1))
                mm = mul(k.aps[:, bank, lo:HALF], const(k, "neg_tri"), k.sb_sp[:, bank, lo:HALF], start=False, stop=n == 0, skip_group_check=True)
                if n:
                    seen = lo + P if b >= 4 * c else lo
                    pe.wait_ge(k.sem("sb_acc_done"), i * ACCS + ACC_COUNT[s - 4])
                    mm = mul(k.aps[:, bank, seen:HALF], const(k, "neg_ones"), k.sb_acc[:, h, n % 2, seen:HALF], start=False, stop=True, skip_group_check=True)
                mm.then_inc(k.sem("sb_r_done"), 1)
            if s >= 3:
                c, b, h, lo, n = unit(s - 3)
                pe.wait_ge(k.sem("sb_a_done"), i * N_UNITS + (s - 2))
                if n == 0 and h == 0 and c == 1:
                    pe.wait_ge(k.sem("sb_y_done"), i * 2 + 1)
                for t in range(lo // P, 4):
                    mm = mul(k.aps[:, 3, t * P + h * HD:t * P + (h + 1) * HD], k.sb_a[:, (s - 3) % 2, t * P:(t + 1) * P],
                             k.sb_v[:, b, h * HD:(h + 1) * HD], start=n == 0 and h == 0 and t == lo // P, stop=b == 0,
                             skip_group_check=True)
                mm.then_inc(k.sem("sb_pv_done"), 1)
                if s - 3 in CHUNK_END:
                    pe.wait_ge(k.sem("sb_o_done"), i * 2 + (c + 1))
                    for t in range(4):
                        mm = k.nc.tensor.transpose(k.aps[:, 3, t * P:(t + 1) * P], k.sb_o[:, t, :], ident)
                    mm.then_inc(k.sem("sb_ot_done"), 1)


def sb_dve(k, dve):
    v = k.nc.vector

    def result(i, c):
        dve.wait_ge(k.sem("sb_yb_hi_done"), i * 2 + (c + 1))
        v.tensor_tensor(one(k.yb_lo, i)[:, c * HALF:(c + 1) * HALF], k.aps[:, 3, :],
                        one(k.yb_hi, i)[:, c * HALF:(c + 1) * HALF].bitcast(F32), ALU.subtract).then_inc(k.sem("sb_y_done"), 1)

    with dve.Fori(0, PAIRS) as i:
        blk, use = i * 4 + BLK["sb"], i * 2 + TILE["sb"] // 2
        dve.wait_ge(k.sem("blk_done"), blk + 1)
        v.scalar_tensor_tensor(k.sb_q[:, :], k.dps[:, 0, :], HD ** -0.5, k.inv[:, :], ALU.mult, ALU.mult).then_inc(k.sem("pair0_out"), 1)
        dve.wait_ge(k.sem("blk_done"), blk + 2)
        v.tensor_tensor(k.sb_k[:, :], k.dps[:, 1, :], k.inv[:, :], ALU.mult).then_inc(k.sem("pair1_out"), 1)
        dve.wait_ge(k.sem("blk_done"), blk + 3)
        v.tensor_tensor(k.sb_vt[:, :], k.dps[:, 0, :], k.inv[:, :], ALU.mult).then_inc(k.sem("pair0_out"), 1)
        dve.wait_ge(k.sem("sb_ya_hi_done"), i + 1)
        v.scalar_tensor_tensor(one(k.ya_lo, i), k.dps[:, 1, :], vec(k, "pool_scale", i), one(k.ya_hi, i).bitcast(F32),
                               ALU.mult, ALU.subtract).then_inc(k.sem("pair1_out"), 1)
        for u in range(N_UNITS):
            c, b, h, lo, n = unit(u)
            dve.wait_ge(k.sem("sb_ln_done"), i * N_UNITS + (u + 1))
            if u >= 3:
                dve.wait_ge(k.sem("sb_r_done"), i * N_UNITS + (u - 2))
            v.scalar_tensor_tensor(k.sb_sp[:, u % 3, lo:], k.aps[:, u % 3, lo:HALF], 0.0, k.sb_e[:, u % 2, lo:],
                                   ALU.max, ALU.add).then_inc(k.sem("sb_sp_done"), 1)
            if b:
                dve.wait_ge(k.sem("sb_sp_done"), i * N_UNITS + (u + 1))
                if u >= 2:
                    dve.wait_ge(k.sem("sb_r_done"), i * N_UNITS + (u - 1))
                seen = lo + P if b >= 4 * c else lo
                if seen > lo:
                    last = v.tensor_copy(k.sb_acc[:, h, (n + 1) % 2, lo:seen], k.sb_sp[:, u % 3, lo:seen])
                if n:
                    dve.wait_ge(k.sem("sb_acc_done"), i * ACCS + ACC_COUNT[u - 2])
                    last = v.tensor_tensor(k.sb_acc[:, h, (n + 1) % 2, seen:], k.sb_acc[:, h, n % 2, seen:],
                                           k.sb_sp[:, u % 3, seen:], ALU.add)
                last.then_inc(k.sem("sb_acc_done"), 1)
            if u == CHUNK_END[0] + 4:
                result(i, 0)
        result(i, 1)


def sb_act(k, act):
    a = k.nc.scalar

    def take(i, c):
        act.wait_ge(k.sem("sb_pv_done"), i * N_UNITS + (CHUNK_END[c] + 1))
        a.activation(k.sb_o[:, :, :].rearrange("p a b -> p (a b)"), k.aps[:, 3, :], ACT.Copy).then_inc(k.sem("sb_o_done"), 1)

    def upper(i, c):
        act.wait_ge(k.sem("sb_ot_done"), i * 2 + (c + 1))
        fixed_wait(k, act)
        a.activation(one(k.yb_hi, i)[:, c * HALF:(c + 1) * HALF], k.aps[:, 3, :], ACT.Copy).then_inc(k.sem("sb_yb_hi_done"), 1)

    a.preload_act_table_set("natural_log_exp_and_others")
    with act.Fori(0, PAIRS) as i:
        act.wait_ge(k.sem("blk_done"), i * 4 + (BLK["sb"] + 4))
        fixed_wait(k, act)
        a.activation(one(k.ya_hi, i), k.dps[:, 1, :], ACT.Copy, scale=vec(k, "pool_scale", i)).then_inc(k.sem("sb_ya_hi_done"), 1)
        act.wait_ge(k.sem("sb_vtr_done"), i + 1)
        a.activation(k.sb_v[:, :, :].rearrange("p a b -> p (a b)"), k.aps[:, 0:2, :].rearrange("p a b -> p (a b)"),
                     ACT.Copy).then_inc(k.sem("sb_v_done"), 1)
        for s in range(N_UNITS + 2):
            if s < N_UNITS:
                c, b, h, lo, n = unit(s)
                e = k.sb_e[:, s % 2, lo:]
                act.wait_ge(k.sem("sb_z_done"), i * N_UNITS + (s + 1))
                if s >= 2:
                    act.wait_ge(k.sem("sb_sp_done"), i * N_UNITS + (s - 1))
                a.activation(e, k.aps[:, s % 3, lo:HALF], ACT.Abs).then_inc(k.sem("sb_abs_done"), 1)
                act.wait_ge(k.sem("sb_abs_done"), i * N_UNITS + (s + 1))
                a.activation(e, e, ACT.Exp, scale=-1.0).then_inc(k.sem("sb_exp_done"), 1)
                act.wait_ge(k.sem("sb_exp_done"), i * N_UNITS + (s + 1))
                a.activation(e, e, ACT.Ln, bias=1.0).then_inc(k.sem("sb_ln_done"), 1)
            if s >= 2:
                u = s - 2
                c, b, h, lo, n = unit(u)
                act.wait_ge(k.sem("sb_r_done"), i * N_UNITS + (u + 1))
                if u >= 2:
                    act.wait_ge(k.sem("sb_pv_done"), i * N_UNITS + (u - 1))
                a.activation(k.sb_a[:, u % 2, lo:], k.aps[:, u % 3, lo:HALF], ACT.Exp).then_inc(k.sem("sb_a_done"), 1)
            if s == CHUNK_END[0] + 3:
                take(i, 0)
            if s == CHUNK_END[0] + 4:
                upper(i, 0)
        take(i, 1)
        upper(i, 1)


def merge_pe(k, pe, blk0, use0, loaded=None):
    with pe.Fori(0, KT // 2) as i:
        for j in range(2):
            blk, use = i * 6 + (blk0 + 3 * j), [i * 4 + (use0[g] + 2 * j) for g in range(2)]
            dense(k, pe, blk, j, 0, rows(k.h_hi), rows(k.h_lo), KT, 0, use[0], "blk_done")
            dense(k, pe, blk + 1, 1 - j, 0, rows(k.h_hi), rows(k.h_lo), KT, 1, use[1], "blk_done")
            if loaded is not None:
                pe.wait_ge(k.sem(loaded[0]), loaded[1])
            dense(k, pe, blk + 2, j, 0, rows(k.ya_hi), rows(k.ya_lo), 4, 0, use[0] + 1, "branch_a_done")
            dense(k, pe, blk + 2, j, 4, rows(k.yb_hi), rows(k.yb_lo), 4, 1, use[1] + 1, "blk_done")


def merge_dve(k, dve, blk0, use0, call):
    v = k.nc.vector
    with dve.Fori(0, KT // 2) as i:
        for j in range(2):
            n, blk, use = i * 2 + j, i * 6 + (blk0 + 3 * j), [i * 4 + (use0[g] + 2 * j) for g in range(2)]
            for g in range(2):
                dve.wait_ge(k.sem("blk_done"), blk + (g + 1))
                v.tensor_tensor(k.tmp[g][:, :], k.dps[:, g, :], k.inv[:, :], ALU.mult).then_inc(k.sem(f"pair{g}_out"), 1)
            dve.wait_ge(k.sem("branch_a_done"), i * 2 + (KT * call + j + 1))
            dve.wait_ge(k.sem("gate_done"), i * 4 + (2 * KT * call + 2 * j + 1))
            v.tensor_tensor(one(k.merged, n), k.dps[:, 0, :], k.tmp0[:, :], ALU.mult).then_inc(k.sem("pair0_out"), 1)
            dve.wait_ge(k.sem("blk_done"), blk + 3)
            dve.wait_ge(k.sem("gate_done"), i * 4 + (2 * KT * call + 2 * j + 2))
            v.tensor_tensor(k.tmp1[:, :], k.dps[:, 1, :], k.tmp1[:, :], ALU.mult).then_inc(k.sem("pair1_out"), 1)
            dve.wait_ge(k.sem("pair0_out"), use[0] + 3)
            dve.wait_ge(k.sem("pair1_out"), use[1] + 3)
            v.tensor_tensor(one(k.merged, n), one(k.merged, n), k.tmp1[:, :], ALU.add).then_inc(k.sem("merged_done"), 1)
            dve.wait_ge(k.sem("merged_done"), i * 2 + (KT * call + j + 1))


def merge_act(k, act, use0, bias):
    with act.Fori(0, KT // 2) as i:
        for j in range(2):
            for g in range(2):
                act.wait_ge(k.sem(f"pair{g}_out"), i * 4 + (use0[g] + 2 * j + 2))
                if bias is not None:
                    fixed_wait(k, act)
                b = 0.0 if bias is None else vec(k, bias, i * 2 + (j + KT * g))
                k.nc.scalar.activation(k.tmp[g][:, :], k.tmp[g][:, :], ACT.Sigmoid, bias=b).then_inc(k.sem("gate_done"), 1)


def merged_split_act(k, act, blk_end, call):
    act.wait_ge(k.sem("blk_done"), blk_end)
    act.wait_ge(k.sem("merged_done"), KT * (call + 1))
    for n in range(KT):
        split_act(k, act, n, src=k.merged)


def merged_split_dve(k, dve, fill, call):
    dve.wait_ge(k.sem("merged_done"), KT * (call + 1))
    for n in range(KT):
        split_dve(k, dve, fill, n, src=k.merged)


def out_pe(k, pe):
    with pe.Fori(0, KT // 2) as i:
        for j in range(2):
            dense(k, pe, i * 2 + (BLK["out"] + j), j, 0, rows(k.h_hi), rows(k.h_lo), KT, j, i + TILE["out"] // 2, "blk_done",
                  ready=("h_lo_done", KT) if j == 0 else None)
    stat(k, pe, 1)


def out_dve(k, dve):
    sumsq_begin(k, dve, 1)
    dve.wait_ge(k.sem("x_again_loaded"), 16)
    with dve.Fori(0, KT // 2) as i:
        for j in range(2):
            n = i * 2 + j
            dve.wait_ge(k.sem("blk_done"), i * 2 + (BLK["out"] + j + 1))
            k.nc.vector.tensor_tensor(one(k.x, n), k.dps[:, j, :], one(k.x_again, n), ALU.add).then_inc(k.sem(f"pair{j}_out"), 1)
            sumsq_dve(k, dve, 1, n, k.sq[j][:, :])
    for n in range(KT):
        split_dve(k, dve, 2, n, "norm_ffn")
    inv_dve(k, dve, 1)


def out_act(k, act, x_t):
    act.wait_ge(k.sem("blk_done"), BLK["out"])
    act.dma_start(k.x_again[:, :, :], x_t).then_inc(k.sem("x_again_loaded"), 16)
    merged_split_act(k, act, BLK["out"], 0)
    with act.Fori(0, KT // 2) as i:
        for j in range(2):
            act.wait_ge(k.sem(f"pair{j}_out"), i + (TILE["out"] // 2 + 2))
            square_act(k, act, 1, i * 2 + j, k.sq[j][:, :])
    act.wait_ge(k.sem("blk_done"), BLK["ffn"])
    for n in range(KT):
        split_act(k, act, n, "norm_ffn")
    inv_act(k, act, 1)


def ffn_places():
    before, blk, tile = 0, BLK["ffn"], TILE["ffn"]
    for c, n in enumerate(FF_CHUNKS):
        yield c, n, before, blk, tile, blk + 2 * n, tile + 2 * n
        before, blk, tile = before + n, blk + 2 * n + KT, tile + 2 * n + KT


def ffn_pe(k, pe):
    for c, n_f, before, blk, tile, blk_d, tile_d in ffn_places():
        with pe.Fori(0, n_f) as i:
            dense(k, pe, i * 2 + blk, 0, 0, rows(k.h_hi), rows(k.h_lo), KT, 0, i + tile // 2, "blk_done",
                  ready=("h_lo_done", 2 * KT) if c == 0 else None)
            dense(k, pe, i * 2 + (blk + 1), 1, 0, rows(k.h_hi), rows(k.h_lo), KT, 1, i + tile // 2, "blk_done")
        with pe.Fori(0, KT // 2) as i:
            for j in range(2):
                dense(k, pe, i * 2 + (blk_d + j), j, 0, rows(k.hid_hi), rows(k.hid_lo), n_f, j, i + tile_d // 2, "blk_done",
                      ready=("hid_lo_done", before) if j == 0 else None)
    stat(k, pe, 2)


def ffn_dve(k, dve):
    v = k.nc.vector
    for c, n_f, before, blk, tile, blk_d, tile_d in ffn_places():
        with dve.Fori(0, n_f) as i:
            dve.wait_ge(k.sem("blk_done"), i * 2 + (blk + 1))
            v.tensor_tensor(k.tmp0[:, :], k.dps[:, 0, :], k.inv[:, :], ALU.mult).then_inc(k.sem("pair0_out"), 1)
            dve.wait_ge(k.sem("blk_done"), i * 2 + (blk + 2))
            v.tensor_tensor(k.tmp1[:, :], k.dps[:, 1, :], k.inv[:, :], ALU.mult).then_inc(k.sem("pair1_out"), 1)
            dve.wait_ge(k.sem("silu_done"), i + (before + 1))
            dve.wait_ge(k.sem("pair1_out"), i + (tile // 2 + 2))
            v.tensor_tensor(k.tmp1[:, :], k.tmp1[:, :], k.tmp0[:, :], ALU.mult).then_inc(k.sem("hid_done"), 1)
            dve.wait_ge(k.sem("hid_hi_done"), i + (before + 1))
            v.tensor_tensor(one(k.hid_lo, i), k.tmp1[:, :], one(k.hid_hi, i).bitcast(F32), ALU.subtract).then_inc(k.sem("hid_lo_done"), 1)
            dve.wait_ge(k.sem("hid_lo_done"), i + (before + 1))
        last = c == len(FF_CHUNKS) - 1
        if last:
            sumsq_begin(k, dve, 2)
        with dve.Fori(0, KT // 2) as i:
            for j in range(2):
                n = i * 2 + j
                dve.wait_ge(k.sem("blk_done"), i * 2 + (blk_d + j + 1))
                v.tensor_tensor(one(k.x, n), k.dps[:, j, :], one(k.x, n), ALU.add).then_inc(k.sem(f"pair{j}_out"), 1)
                if last:
                    split_dve(k, dve, 3, n, "norm_ple")
                    sumsq_dve(k, dve, 2, n, k.sq[j][:, :])
    inv_dve(k, dve, 2)


def ffn_act(k, act):
    a = k.nc.scalar
    for c, n_f, before, blk, tile, blk_d, tile_d in ffn_places():
        with act.Fori(0, n_f) as i:
            act.wait_ge(k.sem("pair0_out"), i + (tile // 2 + 2))
            a.activation(k.tmp0[:, :], k.tmp0[:, :], ACT.Silu).then_inc(k.sem("silu_done"), 1)
            act.wait_ge(k.sem("hid_done"), i + (before + 1))
            fixed_wait(k, act)
            a.activation(one(k.hid_hi, i), k.tmp1[:, :], ACT.Copy).then_inc(k.sem("hid_hi_done"), 1)
        if c == len(FF_CHUNKS) - 1:
            with act.Fori(0, KT // 2) as i:
                for j in range(2):
                    act.wait_ge(k.sem(f"pair{j}_out"), i + (tile_d // 2 + 2))
                    square_wait(k, act, 2, i * 2 + j)
                    split_act(k, act, i * 2 + j, "norm_ple")
                    square_act(k, act, 2, i * 2 + j, k.sq[j][:, :], waited=True)
    inv_act(k, act, 2)


def ple_pe(k, pe):
    with pe.Fori(0, KT // 2) as i:
        for j in range(2):
            blk, use = i * 4 + (BLK["ple"] + 2 * j), i * 2 + (TILE["ple"] // 2 + j)
            dense(k, pe, blk, 0, 0, rows(k.h_hi), rows(k.h_lo), KT, 0, use, "blk_done",
                  ready=("h_lo_done", 3 * KT) if j == 0 else None)
            dense(k, pe, blk + 1, 1, 0, rows(k.p_hi), rows(k.p_lo), 2, 1, use, "blk_done",
                  ready=("p_lo_done", 0) if j == 0 else None)
    stat(k, pe, 3)


def ple_dve(k, dve):
    v = k.nc.vector
    for t in range(2):
        dve.wait_ge(k.sem("p_hi_done"), t + 1)
        v.tensor_tensor(k.p_lo[:, t, :], k.p_raw[:, t, :], k.p_hi[:, t, :].bitcast(F32), ALU.subtract).then_inc(k.sem("p_lo_done"), 1)
    sumsq_begin(k, dve, 3)
    with dve.Fori(0, KT // 2) as i:
        for j in range(2):
            n, blk, use = i * 2 + j, i * 4 + (BLK["ple"] + 2 * j), i * 2 + (TILE["ple"] // 2 + j)
            dve.wait_ge(k.sem("blk_done"), blk + 1)
            v.tensor_tensor(k.tmp[j][:, :], k.dps[:, 0, :], k.inv[:, :], ALU.mult).then_inc(k.sem("pair0_out"), 1)
            dve.wait_ge(k.sem("blk_done"), blk + 2)
            dve.wait_ge(k.sem("ple_gate_done"), n + 1)
            v.tensor_tensor(k.tmp[j][:, :], k.dps[:, 1, :], k.tmp[j][:, :], ALU.mult).then_inc(k.sem("pair1_out"), 1)
            dve.wait_ge(k.sem("pair1_out"), use + 2)
            v.tensor_tensor(one(k.x, n), one(k.x, n), k.tmp[j][:, :], ALU.add).then_inc(k.sem("ple_x_done"), 1)
            sumsq_dve(k, dve, 3, n, k.sq_ple[j][:, :])
    inv_dve(k, dve, 3)


def ple_act(k, act, p_t):
    a = k.nc.scalar
    act.wait_ge(k.sem("blk_done"), BLK["ple"])
    act.dma_start(k.p_raw[:, :, :], p_t).then_inc(k.sem("p_loaded"), 16)
    act.wait_ge(k.sem("p_loaded"), 16)
    for t in range(2):
        a.activation(k.p_hi[:, t, :], k.p_raw[:, t, :], ACT.Copy).then_inc(k.sem("p_hi_done"), 1)
    with act.Fori(0, KT // 2) as i:
        for j in range(2):
            n, use = i * 2 + j, i * 2 + (TILE["ple"] // 2 + j)
            act.wait_ge(k.sem("pair0_out"), use + 2)
            a.activation(k.tmp[j][:, :], k.tmp[j][:, :], ACT.Sigmoid).then_inc(k.sem("ple_gate_done"), 1)
            act.wait_ge(k.sem("ple_x_done"), n + 1)
            square_act(k, act, 3, n, k.sq_ple[j][:, :])
    inv_act(k, act, 3)



def bridge_dve(k, dve):
    sumsq_begin(k, dve, 4)
    for n in range(KT + 1):
        if n < KT:
            k.nc.vector.scalar_tensor_tensor(k.x[:, n, :], k.x[:, n, :], vec(k, "norm_final", n), k.inv[:, :],
                                             ALU.mult, ALU.mult).then_inc(k.sem("x1_done"), 1)
        if n:
            split_dve(k, dve, 4, n - 1, "g_pre")
            sumsq_dve(k, dve, 4, n - 1, k.sq[(n - 1) % 2][:, :])
    inv_dve(k, dve, 4)


def bridge_act(k, act, x1_t, pos_t):
    for n in range(KT):
        act.wait_ge(k.sem("x1_done"), n + 1)
        split_act(k, act, n, "g_pre")
        square_act(k, act, 4, n, k.sq[n % 2][:, :])
        if n % 2:
            act.dma_start(x1_t[:, n - 1:n + 1, :], k.x[:, n - 1:n + 1, :]).then_inc(k.sem("x1_spilled"), 16)
    inv_act(k, act, 4)
    act.wait_ge(k.sem("sumsq_done"), KT * 5 + 2)
    act.dma_start(k.pos[:, :], pos_t).then_inc(k.sem("pos_loaded"), 16)


LATENT_USE = TILE["mla"] // 2


def latent_pe(k, pe):
    b = BLK["mla"]
    mul = k.nc.tensor.matmul
    dense(k, pe, b, 0, 0, rows(k.h_hi), rows(k.h_lo), KT, 0, LATENT_USE, "blk_done", ready=("h_lo_done", 4 * KT))
    stat(k, pe, 4)
    dense(k, pe, b + 1, 1, 0, rows(k.h_hi), rows(k.h_lo), KT, 1, LATENT_USE, "blk_done")
    dense(k, pe, b + 2, 0, 0, rows(k.h_hi), rows(k.h_lo), KT, 0, LATENT_USE + 1, "blk_done")
    dense(k, pe, b + 3, 1, 0, rows(k.h_hi), rows(k.h_lo), KT, 1, LATENT_USE + 1, "blk_done")
    pe.wait_ge(k.sem("pe_rot_done"), 1)
    for h in range(2):
        mm = mul(k.aps[:, h, :], const(k, "rope_sum", HD, P), k.pe_raw[HD:P, h * HALF:(h + 1) * HALF], start=True, stop=True)
    mm.then_inc(k.sem("pe_sum_done"), 1)
    pe.wait_ge(k.sem("latent_sq_done"), 1)
    for h in range(2):
        mm = mul(k.aps[:, 2 + h, :], const(k, "mean"), k.latent_sq[:, 2, h * HALF:(h + 1) * HALF], start=True, stop=True)
    mm.then_inc(k.sem("latent_stat_done"), 1)
    pe.wait_ge(k.sem("latent_sq_done"), 3)
    pe.wait_ge(k.sem("pe_key_done"), 1)
    for h in range(2):
        for n in range(2):
            mm = mul(k.aps[:, h, :], const(k, "mean"), k.latent_sq[:, n, h * HALF:(h + 1) * HALF], start=n == 0, stop=n == 1)
    mm.then_inc(k.sem("latent_stat_done"), 1)


def latent_dve(k, dve):
    v = k.nc.vector
    r = CONST["rope"][0]
    col = lambda n: k.const[:, r + n:r + n + 1]
    dve.wait_ge(k.sem("pos_loaded"), 16)
    dve.wait_ge(k.sem("x1_spilled"), 64)
    steps = (lambda: v.tensor_scalar(k.angle[:, :], k.pos[:, :], col(0), None, ALU.mult),
             lambda: v.tensor_scalar(k.turns[:, :], k.angle[:, :], 0.5 / np.pi, col(1), ALU.mult, ALU.add),
             lambda: v.tensor_scalar(k.turns[:, :], k.turns[:, :], ROUND, -ROUND, ALU.add, ALU.add),
             lambda: v.scalar_tensor_tensor(k.angle[:, :], k.turns[:, :], -TWO_PI[0], k.angle[:, :], ALU.mult, ALU.add),
             lambda: v.scalar_tensor_tensor(k.angle[:, :], k.turns[:, :], -TWO_PI[1], k.angle[:, :], ALU.mult, ALU.add),
             lambda: v.scalar_tensor_tensor(k.angle[:, :], k.turns[:, :], -TWO_PI[2], k.angle[:, :], ALU.mult, ALU.add),
             lambda: v.tensor_scalar(k.angle[:, :], k.angle[:, :], col(2), PI_BELOW, ALU.add, ALU.min),
             lambda: v.tensor_scalar(k.angle[:, :], k.angle[:, :], -PI_BELOW, None, ALU.max))
    for n, step in enumerate(steps):
        step().then_inc(k.sem("angle_done"), 1)
        dve.wait_ge(k.sem("angle_done"), n + 1)
    dve.wait_ge(k.sem("blk_done"), BLK["mla"] + 1)
    v.tensor_tensor(k.pe_raw[HD:P, :], k.dps[HD:P, 0, :], k.inv[HD:P, :], ALU.mult).then_inc(k.sem("pair0_out"), 1)
    for n, (pair, use) in enumerate(((1, LATENT_USE), (0, LATENT_USE + 1), (1, LATENT_USE + 1))):
        dve.wait_ge(k.sem("blk_done"), BLK["mla"] + n + 2)
        v.tensor_tensor(k.latent[:, (n + 2) % 3, :], k.dps[:, pair, :], k.inv[:, :], ALU.mult).then_inc(k.sem(f"pair{pair}_out"), 1)
        if n == 0:
            dve.wait_ge(k.sem("sin_done"), 1)
            v.tensor_scalar(k.trig[:, :], k.trig[:, :], col(3), None, ALU.mult).then_inc(k.sem("trig_done"), 1)
            dve.wait_ge(k.sem("trig_done"), 1)
            dve.wait_ge(k.sem("pair0_out"), LATENT_USE + 2)
            v.tensor_tensor(k.pe_raw[HD:P, :], k.pe_raw[HD:P, :], k.trig[HD:P, :], ALU.mult).then_inc(k.sem("pe_rot_done"), 1)
    dve.wait_ge(k.sem("latent_std_done"), 1)
    v.reciprocal(k.inv_kv[:, :], k.latent_std[:, 0, :]).then_inc(k.sem("latent_inv_done"), 1)
    dve.wait_ge(k.sem("latent_hi_done"), 1)
    v.scalar_tensor_tensor(k.ckv_lo[:, 0, :], k.latent[:, 2, :], vec(k, "g_kv", 0), k.ckv_hi[:, 0, :].bitcast(F32),
                           ALU.mult, ALU.subtract).then_inc(k.sem("latent_lo_done"), 1)
    for n in range(2):
        dve.wait_ge(k.sem("latent_hi_done"), n + 2)
        v.scalar_tensor_tensor(k.cq_lo[:, n, :], k.latent[:, n, :], vec(k, "g_q", n), k.cq_hi[:, n, :].bitcast(F32),
                               ALU.mult, ALU.subtract).then_inc(k.sem("latent_lo_done"), 1)
    dve.wait_ge(k.sem("latent_std_done"), 2)
    v.reciprocal(k.inv_q[:, :], k.latent_std[:, 1, :]).then_inc(k.sem("latent_inv_done"), 1)
    dve.wait_ge(k.sem("latent_inv_done"), 2)


def latent_act(k, act):
    a = k.nc.scalar
    act.wait_ge(k.sem("angle_done"), 8)
    a.activation(k.trig[:, :], k.angle[:, :], ACT.Sin).then_inc(k.sem("sin_done"), 1)
    act.wait_ge(k.sem("pair1_out"), LATENT_USE + 2)
    a.activation(k.latent_sq[:, 2, :], k.latent[:, 2, :], ACT.Square).then_inc(k.sem("latent_sq_done"), 1)
    act.wait_ge(k.sem("pe_sum_done"), 1)
    a.activation(k.mla_k[HD:P, :], k.aps[HD:P, 0:2, :].rearrange("p a b -> p (a b)"), ACT.Copy).then_inc(k.sem("pe_key_done"), 1)
    a.activation(k.ckv_hi[:, 0, :], k.latent[:, 2, :], ACT.Copy, scale=vec(k, "g_kv", 0)).then_inc(k.sem("latent_hi_done"), 1)
    for n in range(2):
        act.wait_ge(k.sem(f"pair{n}_out"), LATENT_USE + 3)
        a.activation(k.latent_sq[:, n, :], k.latent[:, n, :], ACT.Square).then_inc(k.sem("latent_sq_done"), 1)
        a.activation(k.cq_hi[:, n, :], k.latent[:, n, :], ACT.Copy, scale=vec(k, "g_q", n)).then_inc(k.sem("latent_hi_done"), 1)
    for n, (bank, width) in enumerate(((2, 128), (0, 256))):
        act.wait_ge(k.sem("latent_stat_done"), n + 1)
        a.activation(k.latent_std[:, n, :], k.aps[:, bank:bank + 2, :].rearrange("p a b -> p (a b)"), ACT.Sqrt, bias=EPS,
                     scale=D / width).then_inc(k.sem("latent_std_done"), 1)


MLA_USE0 = LATENT_USE + 2
MLA_USE1 = LATENT_USE + 2
GROUPS = [(b, g, min(4, b + 1 - g)) for b in range(KT) for g in range(0, b + 1, 4)]
N_GROUPS = len(GROUPS)


def mla_pe(k, pe):
    mul, ident = k.nc.tensor.matmul, const(k, "ident")
    for_pair = 6
    with pe.Fori(0, PAIRS) as i:
        blk, use = i * 2 + (BLK["mla"] + 4), i * for_pair + MLA_USE0
        dense(k, pe, blk, 0, 0, rows(k.h_hi), rows(k.h_lo), KT, 0, use, "blk_done")
        pe.wait_ge(k.sem("latent_lo_done"), 3)
        for h in range(2):
            def scores(b):
                n = i * 16 + (8 * h + b + 1)
                r = b % 2
                if b >= 2:
                    pe.wait_ge(k.sem("mla_exp_done"), n - 2)
                for lo in range(0, (b + 1) * P, HALF):
                    hi = min(lo + HALF, (b + 1) * P)
                    mm = mul(k.aps[:, 2 * r + lo // HALF, 0:hi - lo], k.mla_q[:, b * P:(b + 1) * P], k.mla_k[:, lo:hi],
                             start=True, stop=False, skip_group_check=True)
                at = b * P % HALF
                mm = mul(k.aps[:, 2 * r + b * P // HALF, at:at + P], ident, const(k, "mla_mask"), start=False, stop=True, skip_group_check=True)
                mm.then_inc(k.sem("mla_s_done"), 1)

            def turn(g):
                b, first, n = GROUPS[g]
                c = i * 2 * N_GROUPS + (N_GROUPS * h + g)
                pe.wait_ge(k.sem("mla_p_done"), i * 16 + (8 * h + b + 1))
                if g:
                    pe.wait_ge(k.sem("mla_pt_done"), c)
                for t in range(n):
                    mm = k.nc.tensor.transpose(k.dps[:, 1, t * P:(t + 1) * P], k.mla_p[:, b % 2, (first + t) * P:(first + t + 1) * P], ident)
                mm.then_inc(k.sem("mla_t_done"), 1)

            def values(g):
                b, first, n = GROUPS[g]
                pe.wait_ge(k.sem("mla_pt_done"), i * 2 * N_GROUPS + (N_GROUPS * h + g + 1))
                for t in range(n):
                    mm = mul(k.dps[:, 1, HALF + b * HD:HALF + (b + 1) * HD], k.mla_pt[:, g % 2, t * P:(t + 1) * P],
                             k.mla_v[:, h, first + t, :], start=g == 0 and t == 0, stop=first + t == b, skip_group_check=True)
                mm.then_inc(k.sem("mla_pv_done"), 1)

            dense(k, pe, blk + 1, 1, 3 * h, rows(k.cq_hi), rows(k.cq_lo), 2, 0, use + (1 + 2 * h), "mla_proj_done")
            dense(k, pe, blk + 1, 1, 3 * h + 2, rows(k.ckv_hi), rows(k.ckv_lo), 1, 0, use + (2 + 2 * h), "blk_done" if h else "mla_proj_done")
            pe.wait_ge(k.sem("pair0_out"), use + (4 + 2 * h))
            if h:
                pe.wait_ge(k.sem("mla_o_done"), i * 2 + 1)
            for b in range(KT):
                mm = mul(k.dps[:, 1, b * HD:(b + 1) * HD], k.mla_vt[HD:P, b * P:(b + 1) * P], const(k, "ident", HD, P)[:, HD:P],
                         start=True, stop=True)
            mm.then_inc(k.sem("mla_vtr_done"), 1)
            pe.wait_ge(k.sem("mla_q_done"), i * 2 + (h + 1))
            scores(0)
            scores(1)
            pe.wait_ge(k.sem("mla_v_done"), i * 2 + (h + 1))
            g = 0
            for s in range(2, KT + 2):
                if s < KT:
                    scores(s)
                while g < N_GROUPS and GROUPS[g][0] == s - 2:
                    turn(g)
                    if g:
                        values(g - 1)
                    g += 1
            values(N_GROUPS - 1)
        pe.wait_ge(k.sem("mla_o_done"), i * 2 + 2)
        pe.wait_ge(k.sem("pair0_out"), use + 6)
        for b in range(KT):
            mm = k.nc.tensor.transpose(k.dps[:, 0, b * P:(b + 1) * P], k.mla_o[:, b, :], ident)
        mm.then_inc(k.sem("mla_yt_done"), 1)


def mla_dve(k, dve):
    v = k.nc.vector
    with dve.Fori(0, PAIRS) as i:
        blk, use = i * 2 + (BLK["mla"] + 4), i * 6 + MLA_USE0
        dve.wait_ge(k.sem("blk_done"), blk + 1)
        v.tensor_tensor(k.mla_gate[:, :], k.dps[:, 0, :], k.inv[:, :], ALU.mult).then_inc(k.sem("pair0_out"), 1)
        for h in range(2):
            dve.wait_ge(k.sem("mla_proj_done"), i * 3 + (2 * h + 1))
            v.tensor_tensor(k.mla_q[:, :], k.dps[:, 0, :], k.inv_q[:, :], ALU.mult).then_inc(k.sem("pair0_out"), 1)
            dve.wait_ge(k.sem("pair0_out"), use + (3 + 2 * h))
            v.tensor_tensor(k.mla_q[HD:P, :], k.mla_q[HD:P, :], k.trig[HD:P, :], ALU.mult).then_inc(k.sem("mla_q_done"), 1)
            if h:
                dve.wait_ge(k.sem("blk_done"), blk + 2)
            else:
                dve.wait_ge(k.sem("mla_proj_done"), i * 3 + 2)
            v.tensor_tensor(k.mla_k[0:HD, :], k.dps[0:HD, 0, :], k.inv_kv[0:HD, :], ALU.mult).then_inc(k.sem("mla_k_done"), 1)
            v.tensor_tensor(k.mla_vt[HD:P, :], k.dps[HD:P, 0, :], k.inv_kv[HD:P, :], ALU.mult).then_inc(k.sem("pair0_out"), 1)

            def normalise(b):
                n = i * 16 + (8 * h + b + 1)
                r = b % 2
                dve.wait_ge(k.sem("mla_exp_done"), n)
                v.reciprocal(k.mla_sum[:, r, 1:2], k.mla_sum[:, r, 0:1]).then_inc(k.sem("mla_rsum_done"), 1)
                dve.wait_ge(k.sem("mla_rsum_done"), n)
                v.tensor_scalar(k.mla_p[:, r, 0:(b + 1) * P], k.mla_p[:, r, 0:(b + 1) * P], k.mla_sum[:, r, 1:2], None,
                                ALU.mult).then_inc(k.sem("mla_p_done"), 1)

            for b in range(KT):
                n = i * 16 + (8 * h + b + 1)
                r = b % 2
                dve.wait_ge(k.sem("mla_s_done"), n)
                v.tensor_reduce(k.mla_max[:, r, 0:1], k.aps[:, 2 * r:2 * r + 2, :].rearrange("p a b -> p (a b)")[:, 0:(b + 1) * P],
                                AX.X, ALU.max).then_inc(k.sem("mla_max_done"), 1)
                dve.wait_ge(k.sem("mla_max_done"), n)
                v.tensor_scalar(k.mla_max[:, r, 1:2], k.mla_max[:, r, 0:1], -MLA_SCALE, None, ALU.mult).then_inc(k.sem("mla_neg_done"), 1)
                if b:
                    normalise(b - 1)
            normalise(KT - 1)
        dve.wait_ge(k.sem("mla_yt_done"), i + 1)
        dve.wait_ge(k.sem("mla_gate_done"), i + 1)
        v.tensor_tensor(one(k.mla_out, i), k.dps[:, 0, :], k.mla_gate[:, :], ALU.mult).then_inc(k.sem("pair0_out"), 1)
        dve.wait_ge(k.sem("pair0_out"), use + 7)


def mla_act(k, act):
    a = k.nc.scalar
    with act.Fori(0, PAIRS) as i:
        use = i * 6 + MLA_USE0
        act.wait_ge(k.sem("pair0_out"), use + 2)
        a.activation(k.mla_gate[:, :], k.mla_gate[:, :], ACT.Silu).then_inc(k.sem("mla_gate_done"), 1)
        for h in range(2):
            act.wait_ge(k.sem("mla_vtr_done"), i * 2 + (h + 1))
            a.activation(k.mla_v[:, h, :, :].rearrange("p a b -> p (a b)"), k.dps[:, 1, 0:HALF], ACT.Copy).then_inc(k.sem("mla_v_done"), 1)
            g = 0
            for s in range(KT + 2):
                while g < N_GROUPS and GROUPS[g][0] == s - 2:
                    c = i * 2 * N_GROUPS + (N_GROUPS * h + g)
                    act.wait_ge(k.sem("mla_t_done"), c + 1)
                    if g >= 2:
                        act.wait_ge(k.sem("mla_pv_done"), c - 1)
                    w = GROUPS[g][2] * P
                    a.activation(k.mla_pt[:, g % 2, 0:w], k.dps[:, 1, 0:w], ACT.Copy).then_inc(k.sem("mla_pt_done"), 1)
                    g += 1
                if s < KT:
                    n = i * 16 + (8 * h + s + 1)
                    r = s % 2
                    act.wait_ge(k.sem("mla_neg_done"), n)
                    a.activation(k.mla_p[:, r, 0:(s + 1) * P], k.aps[:, 2 * r:2 * r + 2, :].rearrange("p a b -> p (a b)")[:, 0:(s + 1) * P],
                                 ACT.Exp, bias=k.mla_max[:, r, 1:2], scale=MLA_SCALE, accum_out=k.mla_sum[:, r, 0:1]).then_inc(k.sem("mla_exp_done"), 1)
            act.wait_ge(k.sem("mla_pv_done"), i * 2 * N_GROUPS + N_GROUPS * (h + 1))
            a.activation(k.mla_o[:, :, h * HD:(h + 1) * HD], k.dps[:, 1, HALF:2 * HALF].rearrange("p (a b) -> p a b", a=KT),
                         ACT.Copy).then_inc(k.sem("mla_o_done"), 1)


LEVEL_STEPS = range(1, LEVELS + 1)
PRODUCTS = (["lt", "l", "ak_t", "rb_t", "rk_t", "kkp_tm", "v_tm", "akv", "be_tm", "ke_tm"]
            + [f"{n}{l}" for l in LEVEL_STEPS for n in ("t", "x", "xt") if (n, l) != ("x", LEVELS)]
            + ["u0", "w1_t"] + [f"{n}{c}" for c in range(NC) for n in ("w1s", "ds")] + ["y", "rk", "mean", "var"])
VALUES = (["rp", "kkp", "bq", "kq", "l_rel", "lt", "xt_part", "xt0", "x_part", "x0", "ak_t", "rb_t", "rk_t", "be", "ke"]
          + [f"{n}{l}" for l in LEVEL_STEPS for n in ("t", "x", "xt") if (n, l) != ("x", LEVELS)]
          + ["s_in"] + [f"{n}{c}" for c in range(NC) for n in ("u", "s")]
          + ["rk", "centred", "rkv", "rstd", "normed", "gained", "summed"])
COPIES = (["p", "pp", "q", "kkp_bd", "bq_bd", "v_bd", "e", "xt_bd0", "kkp_tm", "v_tm", "akv", "be_tm", "ke_tm", "v_tm_bd"]
          + [f"{n}{l}" for l in LEVEL_STEPS for n in ("t_bd", "xt_bd")]
          + ["u0", "w1_t", "s_bd", "u_bd", "y", "sq", "std"])
TAKEN_BY = {"lt": (VALUES, "xt_part"), "l": (VALUES, "x_part"), "ak_t": (VALUES, "ak_t"), "rb_t": (VALUES, "rb_t"),
            "rk_t": (VALUES, "rk_t"), **{n: (COPIES, n) for n in ("kkp_tm", "v_tm", "akv", "be_tm", "ke_tm")},
            **{f"{n}{l}": (VALUES, f"{n}{l}") for l in LEVEL_STEPS for n in ("t", "x", "xt")}}
RW_USE0 = MLA_USE0 + 6 * PAIRS
RW_USE1 = MLA_USE1


class Half:

    def __init__(self, i, g):
        self.i, self.g = i, g
        self.tokens = slice(g * HALF, (g + 1) * HALF)

    def at(self, steps, name):
        n = len(steps)
        return self.i * (2 * n) + (self.g * n + steps.index(name) + 1)

    def product(self, name):
        return self.at(PRODUCTS, name)

    def value(self, name):
        return self.at(VALUES, name)

    def copy(self, name):
        return self.at(COPIES, name)


def bank(k, name):
    return k.aps[:, PRODUCTS.index(name) % 4, :]


def chunks(ap):
    return ap.rearrange("p (c t) -> p c t", c=NC)


def head_halves():
    for h in range(2):
        yield slice(h * HD, (h + 1) * HD)


def masked(k, name, head=slice(0, P)):
    return const(k, name, head.start, head.stop).rearrange("p (a b) -> p a b", a=1).to_broadcast([head.stop - head.start, NC, HD])


def rw_pe(k, pe):
    mul = k.nc.tensor.matmul
    second = lambda x: lambda t: x[:, t + 4, :]
    dense(k, pe, BLK["rwkv"], 0, 0, rows(k.h_hi), rows(k.h_lo), 4, 0, RW_USE0, "blk_done", last=False)
    dense(k, pe, BLK["rwkv"] + 1, 1, 0, second(k.h_hi), second(k.h_lo), 4, 0, RW_USE0, "blk_done", first=False)
    with pe.Fori(0, PAIRS) as i:
        blk, use0, use1 = i * 4 + (BLK["rwkv"] + 2), i * 3 + (RW_USE0 + 1), i * 3 + RW_USE1
        dense(k, pe, blk, 0, 0, rows(k.h_hi), rows(k.h_lo), KT, 0, use0, "blk_done")
        dense(k, pe, blk + 1, 1, 0, rows(k.h_hi), rows(k.h_lo), KT, 1, use1, "blk_done")
        dense(k, pe, blk + 2, 0, 0, rows(k.h_hi), rows(k.h_lo), KT, 0, use0 + 1, "blk_done")
        dense(k, pe, blk + 3, 1, 0, rows(k.h_hi), rows(k.h_lo), KT, 1, use1 + 1, "blk_done")
        pe.wait_ge(k.sem("rw_tanh_done"), 1)
        pe.wait_ge(k.sem("rw_up_loaded"), i * 16 + 16)
        for n, (use, done) in enumerate(((use0, "rw_w_done"), (use1, "rw_a_done"))):
            pe.wait_ge(k.sem(f"pair{n}_out"), use + 3)
            head = slice(n * HD, (n + 1) * HD)
            for h in range(2):
                mm = mul(k.dps[:, n, h * HALF:(h + 1) * HALF], k.rw_up[head, :], k.rw_wdad[head, h * HALF:(h + 1) * HALF],
                         start=True, stop=True)
            mm.then_inc(k.sem(done), 1)
        pe.wait_ge(k.sem("rw_kk_sq_done"), i + 1)
        for h in range(2):
            mm = mul(k.aps[:, h, :], const(k, "headsum"), k.rw_e[:, h * HALF:(h + 1) * HALF], start=True, stop=True)
        mm.then_inc(k.sem("rw_kk_norm_done"), 1)
        for g in range(2):
            rw_half_pe(k, pe, Half(i, g))


def rw_half_pe(k, pe, u):
    mul = k.nc.tensor.matmul
    product = k.sem("rw_product")

    def value(name):
        pe.wait_ge(k.sem("rw_value"), u.value(name))

    def copy(name):
        pe.wait_ge(k.sem("rw_copy"), u.copy(name))

    def free(name):
        steps, taken = TAKEN_BY[PRODUCTS[PRODUCTS.index(name) - 4]]
        value(taken) if steps is VALUES else copy(taken)

    def each_chunk(name, lhs, rhs):
        for c in range(NC):
            mm = mul(bank(k, name)[:, c * CH:(c + 1) * CH], lhs[:, c, :], rhs(c), start=True, stop=True)
        mm.then_inc(product, 1)

    along = lambda x: lambda c: x[:, c * CH:(c + 1) * CH]
    chunk = lambda x: lambda c: x[:, c, :]
    kkp_bd, bq_bd, kq_bd = k.rw_bd
    value("kq")
    copy("bq_bd")
    each_chunk("lt", bq_bd, along(k.rw_kkp))
    each_chunk("l", kkp_bd, along(k.rw_bq))
    each_chunk("ak_t", kq_bd, along(k.rw_kkp))
    each_chunk("rb_t", bq_bd, along(k.rw_rp))
    free("rk_t")
    each_chunk("rk_t", kq_bd, along(k.rw_rp))
    ident = lambda c: const(k, "pair_ident")
    free("kkp_tm")
    each_chunk("kkp_tm", kkp_bd, ident)
    copy("v_bd")
    free("v_tm")
    each_chunk("v_tm", k.rw_t1_bd, ident)
    free("akv")
    copy("v_tm")
    each_chunk("akv", k.rw_akt_bd, chunk(k.rw_v_tm))
    free("be_tm")
    value("be")
    each_chunk("be_tm", bq_bd, ident)
    free("ke_tm")
    value("ke")
    each_chunk("ke_tm", kq_bd, ident)
    for l in LEVEL_STEPS:
        free(f"t{l}")
        value("x0" if l == 1 else f"x{l - 1}")
        each_chunk(f"t{l}", k.rw_lt_bd, chunk(k.rw_xm))
        if l < LEVELS:
            free(f"x{l}")
            value(f"t{l}")
            copy(f"xt_bd{l - 1}")
            each_chunk(f"x{l}", k.rw_xt_bd, chunk(k.rw_t1))
        free(f"xt{l}")
        copy(f"t_bd{l}")
        each_chunk(f"xt{l}", k.rw_t1_bd, chunk(k.rw_xt))
    copy(f"xt_bd{LEVELS}")
    each_chunk("u0", k.rw_xt_bd, along(k.rw_y))
    each_chunk("w1_t", k.rw_kkp_tm, chunk(k.rw_xt))
    copy("w1_t")
    for c in range(NC):
        at = slice(c % 2 * HD, (c % 2 + 1) * HD)
        value(f"s{c - 1}" if c else "s_in")
        mul(k.aps[:, 0, at], k.rw_lt_bd[:, c, :], k.rw_s_all[:, c, :], start=True, stop=True).then_inc(product, 1)
        mul(k.aps[:, 1, at], k.rw_ke_tm[:, c, :], k.rw_v_tm[:, c, :], start=True, stop=False)
        value(f"u{c}")
        mul(k.aps[:, 1, at], k.rw_akt_bd[:, c, :], k.rw_t1[:, c, :], start=False, stop=True).then_inc(product, 1)
    copy("u_bd")
    for c in range(NC):
        t = slice(c * CH, (c + 1) * CH)
        mul(k.aps[:, 2, t], k.rw_bd[1][:, c, :], k.rw_rp[:, t], start=True, stop=False)
        mul(k.aps[:, 2, t], k.rw_bd[2][:, c, :], k.rw_arkt[:, c, :], start=False, stop=False)
        mm = mul(k.aps[:, 2, t], k.rw_bd[0][:, c, :], k.rw_arbt[:, c, :], start=False, stop=True)
    mm.then_inc(product, 1)
    value("rk")
    mul(k.aps[:, 0, :], const(k, "headsum"), k.rw_bq[:, :], start=True, stop=True).then_inc(product, 1)
    copy("y")
    mul(k.aps[:, 3, :], const(k, "headsum"), k.rw_y[:, :], start=True, stop=True).then_inc(product, 1)
    copy("sq")
    mul(k.aps[:, 3, :], const(k, "headsum"), k.rw_t[1][:, :], start=True, stop=True).then_inc(product, 1)


def rw_dve(k, dve):
    v = k.nc.vector
    raw, mixed = k.sem("rw_diff_done"), k.sem("rw_mix_done")

    def shift(n, seq, pad, out, mu):
        v.tensor_tensor(k.rw_d[:, :], pad[:, 0:S], seq, ALU.subtract).then_inc(raw, 1)
        dve.wait_ge(raw, n)
        v.scalar_tensor_tensor(out, k.rw_d[:, :], mu, seq, ALU.mult, ALU.add).then_inc(mixed, 1)
        dve.wait_ge(mixed, n)

    dve.wait_ge(k.sem("yb_spilled"), 16)
    v.memset(k.rw_bds[:, :, :, :], 0.0)
    for n in range(3):
        zeroed = v.memset(k.rw_pad[n][:, 0:1], 0.0)
    zeroed.then_inc(k.sem("rw_zeroed"), 1)
    dve.wait_ge(k.sem("rw_zeroed"), 1)
    dve.wait_ge(k.sem("blk_done"), BLK["rwkv"] + 2)
    v.tensor_tensor(k.rw_r, k.dps[:, 0, :], k.inv[:, :], ALU.mult).then_inc(k.sem("pair0_out"), 1)
    dve.wait_ge(k.sem("pair0_out"), RW_USE0 + 2)
    shift(1, k.rw_r, k.rw_pad[0], k.rw_wdad[:, :], vec(k, "mu", 12))
    with dve.Fori(0, PAIRS) as i:
        blk, use = i * 4 + (BLK["rwkv"] + 2), (i * 3 + (RW_USE0 + 1), i * 3 + RW_USE1)
        v.memset(k.rw_s[:, :], 0.0).then_inc(k.sem("rw_s_zero"), 1)
        for n, seq in enumerate((k.rw_r, k.rw_k, k.rw_v)):
            dve.wait_ge(k.sem("blk_done"), blk + (n + 1))
            v.tensor_tensor(seq, k.dps[:, n % 2, :], k.inv[:, :], ALU.mult).then_inc(k.sem(f"pair{n % 2}_out"), 1)
            dve.wait_ge(k.sem(f"pair{n % 2}_out"), use[n % 2] + (n // 2 + 2))
            shift(i * 3 + (n + 2), seq, k.rw_pad[n], seq, vec(k, "mu", i + 4 * n))
        v.tensor_scalar(k.rw_kk[:, :], k.rw_k, vec(k, "k_k", i), None, ALU.mult).then_inc(k.sem("rw_kk_done"), 1)
        dve.wait_ge(k.sem("blk_done"), blk + 4)
        v.tensor_tensor(k.rw_z[:, :], k.dps[:, 1, :], k.inv[:, :], ALU.mult).then_inc(k.sem("pair1_out"), 1)
        dve.wait_ge(k.sem("pair0_out"), use[0] + 4)
        for h in range(2):
            t = slice(h * HALF, (h + 1) * HALF)
            v.tensor_tensor_scan(k.rw_l[:, t], const(k, "reset"), k.rw_sg[:, t], 0.0, ALU.mult, ALU.add).then_inc(k.sem("rw_l_done"), 1)
        dve.wait_ge(k.sem("rw_l_done"), i * 2 + 2)
        v.tensor_tensor(k.rw_sg[:, :], k.rw_l[:, :], k.rw_sg[:, :], ALU.subtract).then_inc(k.sem("rw_lp_done"), 1)
        dve.wait_ge(k.sem("rw_kk_norm_done"), i + 1)
        dve.wait_ge(k.sem("pair1_out"), use[1] + 4)
        v.tensor_scalar(k.rw_e[:, :], k.rw_b[:, :], -1.0, vec(k, "k_a", i), ALU.add, ALU.mult).then_inc(k.sem("rw_rate_done"), 1)
        dve.wait_ge(k.sem("rw_kk_root_done"), i + 1)
        steps = (lambda: v.tensor_scalar(k.rw_d[:, :], k.rw_d[:, :], 1e-12, None, ALU.max),
                 lambda: v.reciprocal(k.rw_d[:, :], k.rw_d[:, :]),
                 lambda: v.tensor_tensor(k.rw_kk[:, :], k.rw_kk[:, :], k.rw_d[:, :], ALU.mult),
                 lambda: v.tensor_tensor(k.rw_b[:, :], k.rw_b[:, :], k.rw_kk[:, :], ALU.mult))
        for n, step in enumerate(steps):
            step().then_inc(k.sem("rw_unit_done"), 1)
            dve.wait_ge(k.sem("rw_unit_done"), i * 4 + (n + 1))
        dve.wait_ge(k.sem("rw_rate_done"), i + 1)
        v.scalar_tensor_tensor(k.rw_k, k.rw_e[:, :], 1.0, k.rw_k, ALU.add, ALU.mult).then_inc(k.sem("rw_in_done"), 1)
        dve.wait_ge(k.sem("rw_in_done"), i + 1)
        dve.wait_ge(k.sem("rw_s_zero"), i + 1)
        for g in range(2):
            rw_half_dve(k, dve, Half(i, g))


def rw_half_dve(k, dve, u):
    v = k.nc.vector
    made = k.sem("rw_value")
    ts = u.tokens

    def product(name):
        dve.wait_ge(k.sem("rw_product"), u.product(name))

    def copy(name):
        dve.wait_ge(k.sem("rw_copy"), u.copy(name))

    def value(name):
        dve.wait_ge(made, u.value(name))

    def into_bd(bd, seq, scale):
        for head in head_halves():
            ins = v.tensor_tensor(bd[head, :, head], chunks(seq[head]), chunks(scale[head, :]), ALU.mult)
        ins.then_inc(made, 1)

    def mask_bd(bd, name):
        product(name)
        for head in head_halves():
            ins = v.tensor_tensor(bd[head, :, head], chunks(bank(k, name)[head]), masked(k, "strict_t", head), ALU.mult)
        ins.then_inc(made, 1)

    p, pp, q = k.rw_t
    l_half = k.rw_l[:, ts]
    copy("p")
    v.tensor_tensor(k.rw_rp[:, :], k.rw_r[:, ts], p[:, :], ALU.mult).then_inc(made, 1)
    copy("pp")
    v.tensor_tensor(k.rw_kkp[:, :], k.rw_kk[:, ts], pp[:, :], ALU.mult).then_inc(made, 1)
    copy("q")
    v.tensor_tensor(k.rw_bq[:, :], k.rw_b[:, ts], q[:, :], ALU.mult).then_inc(made, 1)
    into_bd(k.rw_bd[2], k.rw_k[:, ts], q)
    value("rp")
    v.tensor_tensor(chunks(p[:, :]), chunks(l_half), chunks(l_half)[:, :, CH - 1:CH].to_broadcast([P, NC, CH]),
                    ALU.subtract).then_inc(made, 1)
    mask_bd(k.rw_lt_bd, "lt")
    for first, mask, out, part in (("lt", "lev0_t", k.rw_xt, "xt_part"), ("l", "lev0", k.rw_xm, "x_part")):
        product(first)
        v.tensor_tensor(out[:, :, :], chunks(bank(k, first)), masked(k, mask), ALU.mult).then_inc(made, 1)
        value(part)
        v.tensor_tensor(out[:, :, :], masked(k, "pair_ident"), out[:, :, :], ALU.subtract).then_inc(made, 1)
    mask_bd(k.rw_akt_bd, "ak_t")
    for name, out in (("rb_t", k.rw_arbt), ("rk_t", k.rw_arkt)):
        product(name)
        v.tensor_tensor(out[:, :, :], chunks(bank(k, name)), masked(k, "incl_t"), ALU.mult).then_inc(made, 1)
    copy("e")
    into_bd(k.rw_bd[1], k.rw_b[:, ts], p)
    into_bd(k.rw_bd[2], k.rw_k[:, ts], p)
    for l in LEVEL_STEPS:
        product(f"t{l}")
        v.tensor_tensor(k.rw_t1[:, :, :], chunks(bank(k, f"t{l}")), masked(k, f"lev{l}"), ALU.mult).then_inc(made, 1)
        if l < LEVELS:
            product(f"x{l}")
            v.tensor_tensor(k.rw_xm[:, :, :], k.rw_xm[:, :, :], chunks(bank(k, f"x{l}")), ALU.subtract).then_inc(made, 1)
        product(f"xt{l}")
        v.tensor_tensor(k.rw_xt[:, :, :], k.rw_xt[:, :, :], chunks(bank(k, f"xt{l}")), ALU.subtract).then_inc(made, 1)
    v.tensor_copy(k.rw_s_all[:, 0, :], k.rw_s[:, :]).then_inc(made, 1)
    value("s_in")
    copy("u0")
    for c in range(NC):
        at = slice(c % 2 * HD, (c % 2 + 1) * HD)
        product(f"w1s{c}")
        v.scalar_tensor_tensor(k.rw_t1[:, c, :], k.aps[:, 0, at], -1.0, k.rw_xm[:, c, :], ALU.mult, ALU.subtract).then_inc(made, 1)
        product(f"ds{c}")
        if c:
            value(f"s{c - 1}")
        pc = k.rw_pc[:, u.g * NC + c:u.g * NC + c + 1]
        out = k.rw_s_all[:, c + 1, :] if c < NC - 1 else k.rw_s[:, :]
        v.scalar_tensor_tensor(out, k.rw_s_all[:, c, :], pc, k.aps[:, 1, at], ALU.mult, ALU.add).then_inc(made, 1)
    v.scalar_tensor_tensor(k.rw_bq[:, :], k.rw_r[:, ts], vec(k, "r_k", u.i), k.rw_k[:, ts], ALU.mult, ALU.mult).then_inc(made, 1)
    product("mean")
    y = k.rw_t[0]
    v.scalar_tensor_tensor(y[:, :], k.aps[:, 3, :], -1.0 / HD, k.rw_y[:, :], ALU.mult, ALU.add).then_inc(made, 1)
    v.tensor_tensor(k.rw_kkp[:, :], k.aps[:, 0, :], k.rw_v[:, ts], ALU.mult).then_inc(made, 1)
    copy("std")
    v.reciprocal(k.rw_t[2][:, :], k.rw_t[2][:, :]).then_inc(made, 1)
    value("rstd")
    v.tensor_tensor(y[:, :], y[:, :], k.rw_t[2][:, :], ALU.mult).then_inc(made, 1)
    value("normed")
    v.tensor_scalar(y[:, :], y[:, :], vec(k, "gn_gain", u.i), vec(k, "gn_bias", u.i), ALU.mult, ALU.add).then_inc(made, 1)
    value("gained")
    v.tensor_tensor(y[:, :], y[:, :], k.rw_kkp[:, :], ALU.add).then_inc(made, 1)
    value("summed")
    dve.wait_ge(k.sem("rw_spilled"), u.i * 32 + (u.g * 16 + 16))
    v.tensor_tensor(k.rw_out[:, u.g, :], y[:, :], k.rw_z[:, ts], ALU.mult).then_inc(k.sem("rw_gated"), 1)
    dve.wait_ge(k.sem("rw_gated"), u.i * 2 + (u.g + 2))


def rw_act(k, act, w_up, branches):
    a = k.nc.scalar
    act.wait_ge(k.sem("pair0_out"), RW_USE0 + 1)
    act.dma_start(branches[:, 4:8, :], k.mla_out[:, :, :]).then_inc(k.sem("yb_spilled"), 16)
    act.wait_ge(k.sem("rw_mix_done"), 1)
    a.activation(k.rw_wdad[0:HD, :], k.rw_wdad[0:HD, :], ACT.Tanh).then_inc(k.sem("rw_tanh_done"), 1)
    with act.Fori(0, PAIRS) as i:
        use0, use1 = i * 3 + (RW_USE0 + 1), i * 3 + RW_USE1
        act.dma_start(k.rw_up[:, :], w_up[bass.ds(i, 1)].rearrange("a p n -> p (a n)")).then_inc(k.sem("rw_up_loaded"), 16)
        act.wait_ge(k.sem("rw_kk_done"), i + 1)
        a.activation(k.rw_e[:, :], k.rw_kk[:, :], ACT.Square).then_inc(k.sem("rw_kk_sq_done"), 1)
        act.wait_ge(k.sem("pair1_out"), use1 + 3)
        a.activation(k.rw_z[:, :], k.rw_z[:, :], ACT.Silu).then_inc(k.sem("rw_silu_done"), 1)
        act.wait_ge(k.sem("rw_w_done"), i + 1)
        fixed_wait(k, act)
        a.activation(k.rw_sg[:, :], k.dps[:, 0, :], ACT.Sigmoid, bias=vec(k, "w0", i)).then_inc(k.sem("pair0_out"), 1)
        act.wait_ge(k.sem("rw_a_done"), i + 1)
        fixed_wait(k, act)
        a.activation(k.rw_b[:, :], k.dps[:, 1, :], ACT.Sigmoid, bias=vec(k, "a0", i)).then_inc(k.sem("pair1_out"), 1)
        act.wait_ge(k.sem("rw_kk_norm_done"), i + 1)
        a.activation(k.rw_d[:, :], k.aps[:, 0:2, :].rearrange("p a b -> p (a b)"), ACT.Sqrt).then_inc(k.sem("rw_kk_root_done"), 1)
        act.wait_ge(k.sem("rw_l_done"), i * 2 + 2)
        a.activation(k.rw_pc[:, :], k.rw_l[:, :].rearrange("p (c t) -> p c t", t=CH)[:, :, CH - 1:CH].rearrange("p c t -> p (c t)"),
                     ACT.Exp, scale=-DECAY).then_inc(k.sem("rw_pc_done"), 1)
        act.wait_ge(k.sem("rw_in_done"), i + 1)
        for g in range(2):
            rw_half_act(k, act, Half(i, g), branches)


def rw_half_act(k, act, u, branches):
    a = k.nc.scalar
    copied = k.sem("rw_copy")
    ts = u.tokens

    def product(name):
        act.wait_ge(k.sem("rw_product"), u.product(name))

    def value(name):
        act.wait_ge(k.sem("rw_value"), u.value(name))

    def flat(t):
        return t[:, :, :].rearrange("p a b -> p (a b)")

    def into_bd(bd, src):
        for head in head_halves():
            ins = a.activation(bd[head, :, head], src[head], ACT.Copy)
        ins.then_inc(copied, 1)

    act.wait_ge(k.sem("rw_gated"), u.i * 2 + (u.g + 1))
    a.activation(k.rw_t[0][:, :], k.rw_l[:, ts], ACT.Exp, scale=-DECAY).then_inc(copied, 1)
    a.activation(k.rw_t[1][:, :], k.rw_sg[:, ts], ACT.Exp, scale=-DECAY).then_inc(copied, 1)
    a.activation(k.rw_t[2][:, :], k.rw_l[:, ts], ACT.Exp, scale=DECAY).then_inc(copied, 1)
    value("kkp")
    into_bd(k.rw_bd[0], chunks(k.rw_kkp[:, :]))
    value("bq")
    into_bd(k.rw_bd[1], chunks(k.rw_bq[:, :]))
    into_bd(k.rw_t1_bd, chunks(k.rw_v[:, ts]))
    value("l_rel")
    a.activation(k.rw_t[0][:, :], k.rw_t[0][:, :], ACT.Exp, scale=DECAY).then_inc(copied, 1)
    value("xt0")
    into_bd(k.rw_xt_bd, k.rw_xt[:, :, :])
    product("kkp_tm")
    into_bd(k.rw_kkp_tm, chunks(bank(k, "kkp_tm")))
    product("v_tm")
    a.activation(flat(k.rw_v_tm), bank(k, "v_tm"), ACT.Copy).then_inc(copied, 1)
    product("akv")
    a.activation(k.rw_y[:, :], bank(k, "akv"), ACT.Copy).then_inc(copied, 1)
    product("be_tm")
    into_bd(k.rw_akt_bd, chunks(bank(k, "be_tm")))
    product("ke_tm")
    into_bd(k.rw_ke_tm, chunks(bank(k, "ke_tm")))
    act.wait_ge(copied, u.copy("v_tm"))
    into_bd(k.rw_bd[2], k.rw_v_tm[:, :, :])
    for l in LEVEL_STEPS:
        value(f"t{l}")
        into_bd(k.rw_t1_bd, k.rw_t1[:, :, :])
        value(f"xt{l}")
        into_bd(k.rw_xt_bd, k.rw_xt[:, :, :])
    product("u0")
    a.activation(flat(k.rw_xm), bank(k, "u0"), ACT.Copy).then_inc(copied, 1)
    product("w1_t")
    into_bd(k.rw_lt_bd, chunks(bank(k, "w1_t")))
    value(f"s{NC - 2}")
    into_bd(k.rw_bd[1], k.rw_s_all[:, :, :])
    value(f"u{NC - 1}")
    into_bd(k.rw_bd[0], k.rw_t1[:, :, :])
    product("y")
    a.activation(k.rw_y[:, :], k.aps[:, 2, :], ACT.Copy).then_inc(copied, 1)
    value("centred")
    a.activation(k.rw_t[1][:, :], k.rw_t[0][:, :], ACT.Square).then_inc(copied, 1)
    product("var")
    a.activation(k.rw_t[2][:, :], k.aps[:, 3, :], ACT.Sqrt, bias=GN_EPS, scale=1.0 / HD).then_inc(copied, 1)
    act.wait_ge(k.sem("rw_gated"), u.i * 2 + (u.g + 2))
    act.dma_start(branches[:, bass.ds(u.i, 1), ts].rearrange("p a t -> p (a t)"), k.rw_out[:, u.g, :]).then_inc(k.sem("rw_spilled"), 16)


MERGE2_USE = (RW_USE0 + 1 + 3 * PAIRS, RW_USE1 + 3 * PAIRS)
OUT2_USE = tuple(n + 2 * KT for n in MERGE2_USE)


def reload_act(k, act, branches):
    act.wait_ge(k.sem("rw_spilled"), 2 * PAIRS * 16 + 32)
    for q in range(4):
        act.dma_start(k.branches[:, 2 * q:2 * q + 2, :], branches[:, 2 * q:2 * q + 2, :]).then_inc(k.sem(f"branch_loaded{q}"), 16)
    for n in range(8):
        act.wait_ge(k.sem(f"branch_loaded{n // 2}"), 16)
        hi = (k.ya_hi, k.yb_hi)[n // 4]
        k.nc.scalar.activation(hi[:, n % 4, :], k.branches[:, n, :], ACT.Copy).then_inc(k.sem("branch_hi_done"), 1)


def reload_dve(k, dve):
    for n in range(8):
        dve.wait_ge(k.sem("branch_hi_done"), n + 1)
        hi, lo = ((k.ya_hi, k.ya_lo), (k.yb_hi, k.yb_lo))[n // 4]
        k.nc.vector.tensor_tensor(lo[:, n % 4, :], k.branches[:, n, :], hi[:, n % 4, :].bitcast(F32),
                                  ALU.subtract).then_inc(k.sem("branch_lo_done"), 1)


def out2_pe(k, pe):
    with pe.Fori(0, KT // 2) as i:
        for j in range(2):
            dense(k, pe, i * 2 + (BLK["out2"] + j), j, 0, rows(k.h_hi), rows(k.h_lo), KT, j, i + OUT2_USE[j], "blk_done",
                  ready=("h_lo_done", 5 * KT) if j == 0 else None)
    stat(k, pe, 5)


def out2_act(k, act, x1_t):
    act.wait_ge(k.sem("blk_done"), BLK["out2"])
    act.dma_start(k.x1_again[:, :, :], x1_t).then_inc(k.sem("x1_again_loaded"), 16)
    merged_split_act(k, act, BLK["out2"], 1)
    with act.Fori(0, KT // 2) as i:
        for j in range(2):
            act.wait_ge(k.sem(f"pair{j}_out"), i + (OUT2_USE[j] + 2))
            square_act(k, act, 5, i * 2 + j, k.sq[j][:, :])
    inv_act(k, act, 5)


def out2_dve(k, dve):
    v = k.nc.vector
    sumsq_begin(k, dve, 5)
    with dve.Fori(0, KT // 2) as i:
        for j in range(2):
            n = i * 2 + j
            dve.wait_ge(k.sem("blk_done"), i * 2 + (BLK["out2"] + j + 1))
            v.tensor_copy(one(k.x, n), k.dps[:, j, :]).then_inc(k.sem(f"pair{j}_out"), 1)
            sumsq_dve(k, dve, 5, n, k.sq[j][:, :])
    inv_dve(k, dve, 5)
    dve.wait_ge(k.sem("x1_again_loaded"), 16)
    for n in range(KT):
        v.scalar_tensor_tensor(k.x[:, n, :], k.x[:, n, :], vec(k, "g_post", n), k.inv[:, :], ALU.mult,
                               ALU.mult).then_inc(k.sem("post_done"), 1)
        dve.wait_ge(k.sem("post_done"), n + 1)
        v.tensor_tensor(k.x1_again[:, n, :], k.x1_again[:, n, :], k.x[:, n, :], ALU.add).then_inc(k.sem("result_done"), 1)


def store_sync(k, sp, out):
    for n in range(KT):
        sp.wait_ge(k.sem("result_done"), n + 1)
        sp.dma_start(out[:, n, :], k.x1_again[:, n, :]).then_inc(k.sem("stored"), 16)
    sp.wait_ge(k.sem("stored"), KT * 16)


def stream_sync(k, sp, w_stream, n_blk):
    for s in range(2):
        sp.dma_start(k.w_raw[:, s], w_stream[s]).then_inc(k.sem(f"w_loaded{s}"), 16)
    with sp.Fori(1, n_blk // 2) as i:
        for s in range(2):
            sp.wait_ge(k.sem("w_split"), i * 2 + (s - 1))
            sp.dma_start(k.w_raw[:, s], w_stream[bass.ds(i * 2 + s, 1)].rearrange("a p k n -> p (a k) n")).then_inc(k.sem(f"w_loaded{s}"), 16)


def stream_pool(k, pool, n_blk):
    g = k.nc.gpsimd
    g.memset(k.one[:, :], 1.0).then_inc(k.sem("one_done"), 1)
    pool.wait_ge(k.sem("one_done"), 1)
    ones = k.one[:, 0:1].to_broadcast([P, SUB * P]).rearrange("p (a b) -> p a b", a=SUB)

    def split(i, s, first):
        pool.wait_ge(k.sem(f"w_loaded{s}"), i * 16 + 16)
        if not first:
            pool.wait_ge(k.sem("blk_done"), i * 2 + (s - 1))
        g.tensor_tensor(k.w_hi[:, s], k.w_raw[:, s], ones, ALU.mult).then_inc(k.sem("w_hi_done"), 1)
        pool.wait_ge(k.sem("w_hi_done"), i * 2 + (s + 1))
        g.tensor_tensor(k.w_lo[:, s], k.w_raw[:, s], k.w_hi[:, s].bitcast(F32), ALU.subtract).then_inc(k.sem("w_split"), 1)

    for s in range(2):
        split(0, s, True)
    with pool.Fori(1, n_blk // 2) as i:
        for s in range(2):
            split(i, s, False)


def program(nc, ctx, t, n_blk, out):
    k = layout(nc, ctx)
    block = ctx.enter_context(nc.Block())

    @block.sync
    def _(sp):
        sp.dma_start(k.vec[:, :], t["vec"]).then_inc(k.sem("vec_loaded"), 16)
        sp.dma_start(k.const[:, :], t["const"]).then_inc(k.sem("const_loaded"), 16)
        stream_sync(k, sp, t["w_stream"], n_blk)
        store_sync(k, sp, out)

    @block.gpsimd
    def _(pool):
        stream_pool(k, pool, n_blk)

    @block.tensor
    def _(pe):
        pe.wait_ge(k.sem("const_loaded"), 16)
        pool_pe(k, pe)
        sb_pe(k, pe)
        merge_pe(k, pe, BLK["merge"], (TILE["merge"] // 2,) * 2)
        out_pe(k, pe)
        ffn_pe(k, pe)
        ple_pe(k, pe)
        latent_pe(k, pe)
        mla_pe(k, pe)
        rw_pe(k, pe)
        merge_pe(k, pe, BLK["merge2"], MERGE2_USE, ("branch_lo_done", 8))
        out2_pe(k, pe)

    @block.scalar
    def _(act):
        entry_act(k, act, t["x_t"])
        pool_act(k, act)
        sb_act(k, act)
        merge_act(k, act, (TILE["merge"] // 2,) * 2, None)
        out_act(k, act, t["x_t"])
        ffn_act(k, act)
        ple_act(k, act, t["p_t"])
        bridge_act(k, act, t["x1_t"], t["pos_t"])
        latent_act(k, act)
        mla_act(k, act)
        rw_act(k, act, t["w_up"], t["branches"])
        reload_act(k, act, t["branches"])
        merge_act(k, act, MERGE2_USE, "b_gate")
        out2_act(k, act, t["x1_t"])

    @block.vector
    def _(dve):
        dve.sem_inc(k.sem("pair0_out"), 1)
        dve.sem_inc(k.sem("pair1_out"), 1)
        dve.sem_inc(k.sem("sumsq_done"), 2)
        dve.sem_inc(k.sem("rw_gated"), 1)
        dve.sem_inc(k.sem("rw_spilled"), 32)
        entry_dve(k, dve)
        pool_dve(k, dve)
        sb_dve(k, dve)
        merge_dve(k, dve, BLK["merge"], (TILE["merge"] // 2,) * 2, 0)
        merged_split_dve(k, dve, 1, 0)
        out_dve(k, dve)
        ffn_dve(k, dve)
        ple_dve(k, dve)
        bridge_dve(k, dve)
        latent_dve(k, dve)
        mla_dve(k, dve)
        rw_dve(k, dve)
        reload_dve(k, dve)
        merge_dve(k, dve, BLK["merge2"], MERGE2_USE, 1)
        merged_split_dve(k, dve, 5, 1)
        out2_dve(k, dve)


def constants():
    c = np.zeros((P, N_CONST), np.float32)
    p = np.arange(P)[:, None]
    q = np.arange(P)[None, :]
    put = lambda name, a: c.__setitem__((slice(None), slice(*CONST[name])), a)
    put("ident", p == q)
    put("mean", 1.0 / D)
    put("headsum", p // HD == q // HD)
    put("neg_tri", -1.0 * (p >= q))
    put("neg_ones", -1.0)
    put("sb_mask", np.where(p >= q, NEG, 0.0))
    put("mla_mask", np.where(q > p, NEG, 0.0))
    r, f = p % HD, np.arange(HD)[None, :]
    put("pair_ident", r == f)
    put("strict_t", r < f)
    put("strict", r > f)
    put("incl_t", r <= f)
    for n in range(6):
        b = 1 << n
        put(f"lev{n}", (r // (2 * b) == f // (2 * b)) & (r // b > f // b))
    put("lev0_t", (r // 2 == f // 2) & (r < f))
    for g, w in enumerate(WINDOWS):
        a = CONST["pool_count"][0] + 16 * g
        c[:, a:a + 16] = 1.0 / np.minimum(np.arange(16) + 1, w)
    put("reset", (np.arange(HALF) % CH != 0)[None, :])
    put("rope_sum", (p >= HD) & (q >= HD) & (p % ROPE == q % ROPE))
    half = ROPE // 2
    freq = ROPE_THETA ** (-np.arange(0, ROPE, 2, dtype=np.float32) / np.float32(ROPE))
    a = CONST["rope"][0]
    c[HD:, a] = freq[np.arange(HD) % half]
    c[HD:HD + ROPE, a + 1] = 0.25
    c[HD:HD + ROPE, a + 2] = np.pi / 2
    c[HD:, a + 3] = 1.0
    c[HD + ROPE:HD + ROPE + half, a + 3] = -1.0
    return c


def tiles(w):
    return w.reshape(w.shape[0] // P, P, w.shape[1]).transpose(1, 0, 2)


def stream(i):
    blocks = []

    def put(*parts):
        b, at = np.zeros((P, SUB, P), np.float32), 0
        for a in parts:
            b[:, at:at + a.shape[1], :a.shape[2]] = a
            at += a.shape[1]
        blocks.append(b)

    col = lambda w, n: tiles(w)[:, :, n * P:(n + 1) * P]
    w_in = i["w_in"][0]
    q0, k0, v0, a0, b0 = 4, 8, 12, 16, 24
    for g in range(POOL_GROUPS):
        put(col(w_in, g))
    for g in range(PAIRS):
        put(col(w_in, q0 + g))
        put(col(w_in, k0 + g))
        put(col(w_in, v0 + g))
        put(i["w_pool"][0, g][:, None, :])
    for n in range(KT):
        put(col(w_in, a0 + n))
        put(col(w_in, b0 + n))
        put(col(i["w_branch_a"][0], n), col(i["w_branch_b"][0], n))
    for n in range(KT):
        put(col(i["w_out"][0], n))
    f = 0
    for n_f in FF_CHUNKS:
        for t in range(f, f + n_f):
            put(col(i["w_ffn_gate"][0], t))
            put(col(i["w_ffn_up"][0], t))
        for n in range(KT):
            put(col(i["w_ffn_down"][0][f * P:(f + n_f) * P], n))
        f += n_f
    for n in range(KT):
        put(col(i["w_ple_gate"][0], n))
        put(col(i["w_ple_proj"][0], n))
    w_in = i["w_in_2"]
    names = ("r", "k", "v", "wd_ad", "z_a", "c_q", "c_kv", "k_pe", "z_b", "g_a", "g_b")
    widths = (512, 512, 512, 128, 512, 256, 128, ROPE, 512, D, D)
    start = dict(zip(names, np.cumsum((0,) + widths)))
    entry = lambda name, n: tiles(w_in[:, start[name] + n * P:start[name] + (n + 1) * P])
    half = ROPE // 2
    turned = np.r_[half:ROPE, 0:half]
    k_pe = w_in[:, start["k_pe"]:start["k_pe"] + ROPE]
    put(tiles(np.concatenate([np.zeros((D, HD), np.float32), k_pe, k_pe[:, turned]], axis=1)))
    put(entry("c_kv", 0))
    put(entry("c_q", 0))
    put(entry("c_q", 1))
    w_uq = i["w_uq_2"].reshape(2 * P, 2 * PAIRS, HD + ROPE)
    w_ukv = i["w_ukv_2"].reshape(P, 2 * PAIRS, P)
    for g in range(PAIRS):
        put(entry("z_b", g))
        put(*(part for h in (2 * g, 2 * g + 1) for part in
              (tiles(np.concatenate([w_uq[:, h], w_uq[:, h, HD + turned]], axis=1)), tiles(w_ukv[:, h]))))
    put(entry("wd_ad", 0)[:, 0:4])
    put(entry("wd_ad", 0)[:, 4:8])
    for g in range(PAIRS):
        for name in ("r", "k", "v", "z_a"):
            put(entry(name, g))
    for n in range(KT):
        put(entry("g_a", n))
        put(entry("g_b", n))
        put(col(i["w_out_a_2"], n), col(i["w_out_b_2"], n))
    for n in range(KT):
        put(col(i["w_o_2"], n))
    return np.stack(blocks)


def vectors(i):
    v = np.zeros((P, N_VEC), np.float32)

    def put(name, a):
        a = a.reshape(-1, P).T
        v[:, VEC[name]:VEC[name] + a.shape[1]] = a

    for name in ("norm_mix", "norm_ffn", "norm_ple", "norm_final", "pool_scale"):
        put(name, i[name])
    for name in ("g_pre", "g_post", "b_gate", "w0", "a0", "k_k", "k_a", "r_k", "gn_gain", "gn_bias", "g_q", "g_kv"):
        put(name, i[name + "_2"])
    put("mu", i["mu_shift_2"])
    return v


def kernel(**inputs):
    import concourse.bacc as bacc
    from concourse.bass_utils import run_bass_kernel_spmd

    i = {name: np.asarray(a) for name, a in inputs.items()}
    arrays = {"x_t": np.ascontiguousarray(tiles(i["x"][0].T)), "p_t": np.ascontiguousarray(tiles(i["p"][0, 0].T)),
              "w_stream": stream(i), "vec": vectors(i), "const": constants(),
              "pos_t": np.ascontiguousarray(np.broadcast_to(i["positions_2"].astype(np.int32, copy=False), (P, S))),
              "w_up": np.ascontiguousarray(np.concatenate([i["w_decay_up_2"], i["w_iclr_up_2"]]).reshape(P, PAIRS, P).transpose(1, 0, 2))}
    nc = bacc.Bacc("TRN2", target_bir_lowering=False, num_devices=1)
    t = {name: nc.dram_tensor(name, a.shape, mybir.dt.from_np(a.dtype), kind="ExternalInput").ap() for name, a in arrays.items()}
    out = nc.dram_tensor("out_t", (P, KT, S), F32, kind="ExternalOutput").ap()
    with ExitStack() as ctx:
        t["x1_t"] = nc.dram_tensor("x1_t", (P, KT, S), F32, kind="Internal").ap()
        t["branches"] = nc.dram_tensor("branches", (P, 8, S), F32, kind="Internal").ap()
        program(nc, ctx, t, len(arrays["w_stream"]), out)
    got = run_bass_kernel_spmd(nc, [arrays], core_ids=[0]).results[0]["out_t"]
    return np.ascontiguousarray(got.transpose(1, 0, 2).reshape(D, S).T)[None]
```

```python
from contextlib import ExitStack

import numpy as np

import concourse.bass as bass
from concourse import mybir

F32 = mybir.dt.float32
F32R = mybir.dt.float32r
I32 = mybir.dt.int32
ACT = mybir.ActivationFunctionType
ALU = mybir.AluOpType
AX = mybir.AxisListType

P = 128
D = 1024
S = 1024
HALF = 512
KT = D // P
SUB = 8
NEG = -1.0e30
EPS = 1e-6

POOL_GROUPS = 4
WINDOWS = (2, 4, 8, 16)
PAIRS = 4
HD = 64
FF = 2816
FF_TILES = FF // P
FF_CHUNKS = (8, 8, 6)
assert sum(FF_CHUNKS) == FF_TILES

GN_EPS = 64e-5
DECAY = 0.6065306597
CH = 64
NC = HALF // CH
LEVELS = 5
ROPE = 32
ROPE_THETA = 10000.0
MLA_SCALE = (HD + ROPE) ** -0.5
ROUND = 1.5 * 2.0 ** 23
TWO_PI = (6.28125, 1.93500518798828125e-3, 3.0199159819e-07)
PI_BELOW = 3.1415925

CONST = {}
_at = 0
for _name, _width in (("ident", P), ("mean", P), ("headsum", P), ("neg_tri", P), ("neg_ones", P),
                      ("sb_mask", P), ("mla_mask", P), ("pair_ident", HD), ("strict_t", HD), ("strict", HD),
                      ("incl_t", HD), ("lev0", HD), ("lev0_t", HD), ("lev1", HD), ("lev2", HD), ("lev3", HD),
                      ("lev4", HD), ("lev5", HD), ("rope_sum", P), ("pool_count", 64), ("reset", HALF),
                      ("rope", 8)):
    CONST[_name] = (_at, _at + _width)
    _at += _width
N_CONST = _at

VEC = {}
_at = 0
for _name, _width in (("norm_mix", 8), ("norm_ffn", 8), ("norm_ple", 8), ("norm_final", 8), ("pool_scale", 4),
                      ("g_pre", 8), ("g_post", 8), ("b_gate", 16), ("mu", 13), ("w0", 4), ("a0", 4), ("k_k", 4),
                      ("k_a", 4), ("r_k", 4), ("gn_gain", 4), ("gn_bias", 4), ("g_q", 2), ("g_kv", 1)):
    VEC[_name] = _at
    _at += _width
N_VEC = _at

BLK = {"pool": 0}
TILE = {"pool": 0}


def _stage(name, after, blocks, tiles):
    BLK[name] = BLK[after] + blocks
    TILE[name] = TILE[after] + tiles


_stage("sb", "pool", 4, 4)
_stage("merge", "sb", 16, 16)
_stage("out", "merge", 24, 32)
_stage("ffn", "out", 8, 8)
_stage("ple", "ffn", 2 * FF_TILES + KT * len(FF_CHUNKS), 2 * FF_TILES + KT * len(FF_CHUNKS))
_stage("mla", "ple", 16, 16)
_stage("rwkv", "mla", 4 + 2 * 4, 4 + 6 * 4)
_stage("merge2", "rwkv", 2 + 4 * 4, 2 + 6 * 4)
_stage("out2", "merge2", 24, 32)
_stage("end", "out2", 8, 8)


class Core:

    def __init__(self, nc, ctx):
        self.nc, self.ctx, self.sems = nc, ctx, {}
        self.ahead, self.half = {}, {}

    def sem(self, name):
        if name not in self.sems:
            self.sems[name] = self.ctx.enter_context(self.nc.semaphore(name))
        return self.sems[name]

    def at(self, name, offset, shape, dt=F32):
        return self.nc.alloc_sbuf_tensor_at(name, [P, *shape], dt, offset=offset)


def layout(nc, ctx):
    k = Core(nc, ctx)
    kb = 1024
    W = 16512
    K = W + 24 * kb
    H = K + 10 * kb
    X = H + 64 * kb
    C = X + 32 * kb
    V = C + 64 * kb
    k.w_raw = k.at("w_raw", W, [2, SUB, P])
    k.w_hi = k.at("w_hi", W + 8 * kb, [2, SUB, P], F32R)
    k.w_lo = k.at("w_lo", W + 16 * kb, [2, SUB, P], F32R)
    k.const = k.at("const", K, [N_CONST])
    k.vec = k.at("vec", V + 12 * kb, [N_VEC])
    k.one = k.at("one", V + 12 * kb + 4 * N_VEC, [1])
    k.h_hi = k.at("h_hi", H, [KT, S], F32R)
    k.h_lo = k.at("h_lo", H + 32 * kb, [KT, S], F32R)
    k.x = k.at("x_res", X, [KT, S])
    k.inv = k.at("inv", V, [S])
    k.tmp0 = k.at("tmp0", V + 4 * kb, [S])
    k.tmp1 = k.at("tmp1", V + 8 * kb, [S])
    k.tmp = [k.tmp0, k.tmp1]
    k.sq = [k.tmp0, k.tmp1]
    k.sq_ple = [k.at(f"sq_ple{n}", C + (24 + 4 * n) * kb, [S]) for n in range(2)]
    k.sumsq = k.at("sumsq", C + 56 * kb, [S])
    k.std = k.at("std", C + 60 * kb, [S])
    k.u_pad = k.at("u_pad", X, [16 + S])
    k.win = [k.at(f"win{n}", X + (n + 1) * 4160, [16 + S]) for n in range(2)]
    k.pooled = k.at("pooled", X + 3 * 4160, [S])
    k.ya_hi = k.at("ya_hi", C, [4, S], F32R)
    k.ya_lo = k.at("ya_lo", C + 16 * kb, [4, S], F32R)
    k.yb_hi = k.at("yb_hi", C + 32 * kb, [4, S], F32R)
    k.yb_lo = k.at("yb_lo", C + 48 * kb, [4, S], F32R)
    k.sb_q = k.at("sb_q", X, [S])
    k.sb_k = k.at("sb_k", X + 4 * kb, [S])
    k.sb_v = k.at("sb_v", X + 8 * kb, [KT, P])
    k.sb_e = k.at("sb_e", X + 12 * kb, [2, HALF])
    k.sb_sp = k.at("sb_sp", X + 16 * kb, [3, HALF])
    k.sb_acc = k.at("sb_acc", X + 22 * kb, [2, 2, HALF])
    k.sb_o = k.at("sb_o", X + 30 * kb, [4, P])
    k.sb_vt = k.at("sb_vt", V + 4 * kb, [S])
    k.sb_a = k.at("sb_a", V + 8 * kb, [2, HALF])
    k.merged = k.at("merged", X, [KT, S])
    k.x_again = k.at("x_again", C, [KT, S])
    k.hid_hi = k.at("hid_hi", C, [SUB, S], F32R)
    k.hid_lo = k.at("hid_lo", C + 32 * kb, [SUB, S], F32R)
    k.p_raw = k.at("p_raw", C + 16 * kb, [2, S])
    k.p_hi = k.at("p_hi", C, [2, S], F32R)
    k.p_lo = k.at("p_lo", C + 8 * kb, [2, S], F32R)
    k.cq_hi = k.at("cq_hi", X, [2, S], F32R)
    k.cq_lo = k.at("cq_lo", X + 8 * kb, [2, S], F32R)
    k.ckv_hi = k.at("ckv_hi", X + 16 * kb, [1, S], F32R)
    k.ckv_lo = k.at("ckv_lo", X + 20 * kb, [1, S], F32R)
    k.trig = k.at("trig", X + 24 * kb, [S])
    k.inv_q = k.at("inv_q", X + 28 * kb, [S])
    k.inv_kv = k.at("inv_kv", C, [S])
    k.mla_k = k.at("mla_k", C + 4 * kb, [S])
    k.mla_q = k.at("mla_q", C + 8 * kb, [S])
    k.mla_v = k.at("mla_v", C + 12 * kb, [2, KT, HD])
    k.mla_p = k.at("mla_p", C + 16 * kb, [2, S])
    k.mla_o = k.at("mla_o", C + 24 * kb, [KT, P])
    k.mla_gate = k.at("mla_gate", C + 28 * kb, [S])
    k.mla_vt = k.at("mla_vt", V + 4 * kb, [S])
    k.mla_out = k.at("mla_out", C + 32 * kb, [4, S])
    k.mla_pt = k.at("mla_pt", V + 8 * kb, [2, HALF])
    k.latent = k.at("latent", C + 32 * kb, [3, S])
    k.latent_sq = k.at("latent_sq", C + 44 * kb, [3, S])
    k.latent_std = k.at("latent_std", C + 56 * kb, [2, S])
    k.pos = k.at("pos", V + 4 * kb, [S], I32)
    k.angle = k.at("angle", V + 8 * kb, [S])
    k.turns = k.at("turns", X + 16 * kb, [S])
    k.pe_raw = k.at("pe_raw", X + 20 * kb, [S])
    free = V + 12 * kb + 4 * N_VEC + 32
    k.mla_max = k.at("mla_max", free, [2, 2])
    k.mla_sum = k.at("mla_sum", free + 32, [2, 2])
    k.rw_pad = [k.at(f"rw_{name}", X + 4128 * n, [S + 1]) for n, name in enumerate("rkv")]
    k.rw_r, k.rw_k, k.rw_v = (t[:, 1:S + 1] for t in k.rw_pad)
    at = X + 3 * 4128
    k.rw_z = k.at("rw_z", at, [S])
    k.rw_sg = k.at("rw_sg", at + 4 * kb, [S])
    k.rw_b = k.at("rw_b", at + 8 * kb, [S])
    k.rw_kk = k.at("rw_kk", at + 12 * kb, [S])
    k.rw_centred = k.at("rw_centred", at + 16 * kb, [HALF])
    k.rw_s = k.at("rw_s", at + 18 * kb, [HD])
    k.rw_pc = k.at("rw_pc", at + 18 * kb + 256, [S // CH])
    assert at + 18 * kb + 320 <= C
    k.rw_up = k.at("rw_up", K + 4 * N_CONST + 32, [P])
    k.rw_d = k.at("rw_d", V + 4 * kb, [S])
    k.rw_e = k.at("rw_e", V + 8 * kb, [S])
    k.rw_t = [k.at(f"rw_t{n}", V + (4 + 2 * n) * kb, [HALF]) for n in range(3)]
    k.rw_rstd = k.at("rw_rstd", V + 10 * kb, [HALF])
    k.rw_l = k.at("rw_l", C, [S])
    k.rw_wdad = k.at("rw_wdad", C + 4 * kb, [S])
    k.rw_out = k.at("rw_out", C + 8 * kb, [2, HALF])
    at = C + 12 * kb
    for name in ("rp", "kkp", "bq", "kq", "be", "ke", "rkv"):
        k.ahead[name] = [k.at(f"rw_{name}{g}", at + 2 * g * kb, [NC, HD]) for g in range(2)]
        at += 4 * kb
    for name in ("lt", "akt", "xm", "xt", "t1", "arbt", "arkt", "kkp_tm", "v_tm", "be_tm", "ke_tm", "akv"):
        k.half[name] = k.at(f"rw_{name}", at, [NC, HD])
        at += 2 * kb
    assert at <= V
    for name, room in (("w1_t", "lt"), ("u0", "xm"), ("u", "t1"), ("s", "akt"), ("y", "akv")):
        k.half[name] = k.half[room]
    k.branches = k.at("branches_again", X, [8, S])
    k.x1_again = k.at("x1_again", C, [KT, S])
    k.dps = nc.alloc_psum_tensor("dps", [P, 2, S], F32)
    k.aps = nc.alloc_psum_tensor("aps", [P, 4, HALF], F32)
    return k


def const(k, name, lo=0, hi=P):
    a, b = CONST[name]
    return k.const[lo:hi, a:b]


def vec(k, name, n):
    return k.vec[:, bass.ds(n + VEC[name], 1)] if not isinstance(n, int) else k.vec[:, VEC[name] + n:VEC[name] + n + 1]


def one(t, n):
    return t[:, n, :] if isinstance(n, int) else t[:, bass.ds(n, 1), :].rearrange("p a t -> p (a t)")


def dense(k, pe, blk, slot, sub, rhs_hi, rhs_lo, n_k, pair, use, done, rows=P, ready=None,
          first=True, last=True):
    pe.wait_ge(k.sem("w_split"), blk + 1)
    if first:
        pe.wait_ge(k.sem(f"pair{pair}_out"), use + 1)
    for t in range(n_k):
        if ready is not None:
            pe.wait_ge(k.sem(ready[0]), ready[1] + t + 1)
        for n, (w, x) in enumerate(((k.w_hi, rhs_hi), (k.w_hi, rhs_lo), (k.w_lo, rhs_hi))):
            for h in range(2):
                mm = k.nc.tensor.matmul(k.dps[0:rows, pair, h * HALF:(h + 1) * HALF], w[:, slot, sub + t, 0:rows],
                                        x(t)[:, h * HALF:(h + 1) * HALF],
                                        start=first and t == 0 and n == 0, stop=last and t == n_k - 1 and n == 2)
    if done is not None:
        mm.then_inc(k.sem(done), 1)


def dense_part(k, pe, blk, slot, pair, use, done, lo, hi):
    if lo == 0:
        pe.wait_ge(k.sem("w_split"), blk + 1)
        pe.wait_ge(k.sem(f"pair{pair}_out"), use + 1)
    for n in range(lo, hi):
        t, h = n // 6, n % 2
        w, x = ((k.w_hi, k.h_hi), (k.w_hi, k.h_lo), (k.w_lo, k.h_hi))[n % 6 // 2]
        mm = k.nc.tensor.matmul(k.dps[:, pair, h * HALF:(h + 1) * HALF], w[:, slot, t, :], x[:, t, h * HALF:(h + 1) * HALF],
                                start=n < 2, stop=n >= 6 * KT - 2, skip_group_check=True)
    if hi == 6 * KT:
        mm.then_inc(k.sem(done), 1)


def stat(k, pe, norm):
    pe.wait_ge(k.sem("sumsq_done"), KT * (norm + 1) + 2)
    for h in range(2):
        mm = k.nc.tensor.matmul(k.aps[:, h, :], const(k, "mean"), k.sumsq[:, h * HALF:(h + 1) * HALF],
                                start=True, stop=True)
    mm.then_inc(k.sem("stat_done"), 1)


def fixed_wait(k, act):
    act.wait_ge(k.sem("vec_loaded"), 16)


def split_act(k, act, n, gain=None, src=None):
    src = k.x if src is None else src
    scale = 1.0 if gain is None else vec(k, gain, n)
    if not isinstance(n, int):
        fixed_wait(k, act)
    k.nc.scalar.activation(one(k.h_hi, n), one(src, n), ACT.Copy, scale=scale).then_inc(k.sem("h_hi_done"), 1)


def split_dve(k, dve, fill, n, gain=None, src=None):
    src = k.x if src is None else src
    dve.wait_ge(k.sem("h_hi_done"), n + (KT * fill + 1))
    if gain is None:
        ins = k.nc.vector.tensor_tensor(one(k.h_lo, n), one(src, n), one(k.h_hi, n).bitcast(F32), ALU.subtract)
    else:
        ins = k.nc.vector.scalar_tensor_tensor(one(k.h_lo, n), one(src, n), vec(k, gain, n),
                                               one(k.h_hi, n).bitcast(F32), ALU.mult, ALU.subtract)
    ins.then_inc(k.sem("h_lo_done"), 1)


def square_wait(k, act, norm, n):
    act.wait_ge(k.sem("sumsq_done"), n + (KT * norm + 1))


def square_act(k, act, norm, n, sq, waited=False):
    if not waited:
        square_wait(k, act, norm, n)
    if not isinstance(n, int) and not waited:
        fixed_wait(k, act)
    k.nc.scalar.activation(sq, one(k.x, n), ACT.Square).then_inc(k.sem("sq_done"), 1)


def sumsq_begin(k, dve, norm):
    if norm:
        dve.wait_ge(k.sem("stat_done"), norm)
    k.nc.vector.memset(k.sumsq[:, :], 0.0).then_inc(k.sem("sumsq_zero"), 1)
    dve.wait_ge(k.sem("sumsq_zero"), norm + 1)


def sumsq_dve(k, dve, norm, n, sq):
    dve.wait_ge(k.sem("sumsq_done"), n + (KT * norm + 2))
    dve.wait_ge(k.sem("sq_done"), n + (KT * norm + 1))
    k.nc.vector.tensor_tensor(k.sumsq[:, :], k.sumsq[:, :], sq, ALU.add).then_inc(k.sem("sumsq_done"), 1)


def inv_act(k, act, norm):
    act.wait_ge(k.sem("stat_done"), norm + 1)
    k.nc.scalar.activation(k.std[:, :], k.aps[:, 0:2, :].rearrange("p a b -> p (a b)"), ACT.Sqrt,
                           bias=EPS).then_inc(k.sem("std_done"), 1)


def inv_dve(k, dve, norm):
    dve.wait_ge(k.sem("std_done"), norm + 1)
    k.nc.vector.reciprocal(k.inv[:, :], k.std[:, :]).then_inc(k.sem("inv_done"), 1)
    dve.wait_ge(k.sem("inv_done"), norm + 1)


def rows(x):
    return lambda t: x[:, t, :]


def entry_act(k, act, x_t):
    for q in range(4):
        act.dma_start(k.x[:, 2 * q:2 * q + 2, :], x_t[:, 2 * q:2 * q + 2, :]).then_inc(k.sem(f"x_loaded{q}"), 16)
    act.wait_ge(k.sem("vec_loaded"), 16)
    for n in range(KT):
        if n % 2 == 0:
            act.wait_ge(k.sem(f"x_loaded{n // 2}"), 16)
        split_act(k, act, n, "norm_mix")
        square_act(k, act, 0, n, k.sq[n % 2][:, :])
    inv_act(k, act, 0)


def entry_dve(k, dve):
    dve.wait_ge(k.sem("vec_loaded"), 16)
    dve.wait_ge(k.sem("const_loaded"), 16)
    sumsq_begin(k, dve, 0)
    for n in range(KT):
        split_dve(k, dve, 0, n, "norm_mix")
        sumsq_dve(k, dve, 0, n, k.sq[n % 2][:, :])
    inv_dve(k, dve, 0)


def pool_pe(k, pe):
    for g in range(POOL_GROUPS):
        dense(k, pe, BLK["pool"] + g, g % 2, 0, rows(k.h_hi), rows(k.h_lo), KT, g % 2, g // 2, "blk_done",
              ready=("h_lo_done", 0) if g == 0 else None)
        if g == 0:
            stat(k, pe, 0)


def pool_dve(k, dve):
    v = k.nc.vector
    v.memset(k.u_pad[:, 0:16], 0.0).then_inc(k.sem("u_zero"), 1)
    sums = 0
    for g, w in enumerate(WINDOWS):
        dve.wait_ge(k.sem("blk_done"), BLK["pool"] + g + 1)
        if g == 0:
            dve.wait_ge(k.sem("inv_done"), 1)
            dve.wait_ge(k.sem("u_zero"), 1)
        v.tensor_tensor(k.u_pad[:, 16:], k.dps[:, g % 2, :], k.inv[:, :], ALU.mult).then_inc(k.sem(f"pair{g % 2}_out"), 1)
        dve.wait_ge(k.sem(f"pair{g % 2}_out"), g // 2 + 2)
        src, reach, step = k.u_pad, 1, 1
        while step < w:
            dst = k.win[0] if src is not k.win[0] else k.win[1]
            v.tensor_tensor(dst[:, reach:], src[:, reach:], src[:, reach - step:16 + S - step],
                            ALU.add).then_inc(k.sem("win_done"), 1)
            sums += 1
            dve.wait_ge(k.sem("win_done"), sums)
            src, step = dst, 2 * step
            reach += step
        if g:
            dve.wait_ge(k.sem("pool_hi_done"), g)
        a = CONST["pool_count"][0] + 16 * g
        v.tensor_tensor(k.pooled[:, 0:16], src[:, 16:32], k.const[:, a:a + 16], ALU.mult).then_inc(k.sem("head_done"), 1)
        v.scalar_tensor_tensor(k.pooled[:, 16:], src[:, 32:], 1.0 / w, k.u_pad[:, 32:], ALU.mult,
                               ALU.subtract).then_inc(k.sem("body_done"), 1)
        dve.wait_ge(k.sem("head_done"), g + 1)
        v.tensor_tensor(k.pooled[:, 0:16], k.pooled[:, 0:16], k.u_pad[:, 16:32], ALU.subtract).then_inc(k.sem("pooled_done"), 1)
        dve.wait_ge(k.sem("pool_hi_done"), g + 1)
        v.tensor_tensor(k.ya_lo[:, g, :], k.pooled[:, :], k.ya_hi[:, g, :].bitcast(F32),
                        ALU.subtract).then_inc(k.sem("pool_lo_done"), 1)


def pool_act(k, act):
    for g in range(POOL_GROUPS):
        act.wait_ge(k.sem("body_done"), g + 1)
        act.wait_ge(k.sem("pooled_done"), g + 1)
        k.nc.scalar.activation(k.ya_hi[:, g, :], k.pooled[:, :], ACT.Copy).then_inc(k.sem("pool_hi_done"), 1)


UNITS = [(c, b, h) for c in range(2) for b in range(4 * c + 3, -1, -1) for h in range(2)]
N_UNITS = len(UNITS)
ACC_COUNT = [sum(1 for _, b, _ in UNITS[:u + 1] if b) for u in range(N_UNITS)]
ACCS = ACC_COUNT[-1]
CHUNK_END = [u for u, (c, b, h) in enumerate(UNITS) if b == 0 and h == 1]


def unit(u):
    c, b, h = UNITS[u]
    return c, b, h, max(0, P * b - HALF * c), 4 * c + 3 - b


def sb_pe(k, pe):
    mul, ident = k.nc.tensor.matmul, const(k, "ident")
    with pe.Fori(0, PAIRS) as i:
        blk, use = i * 4 + BLK["sb"], i * 2 + TILE["sb"] // 2
        dense(k, pe, blk, 0, 0, rows(k.h_hi), rows(k.h_lo), KT, 0, use, "blk_done")
        dense(k, pe, blk + 1, 1, 0, rows(k.h_hi), rows(k.h_lo), KT, 1, use, "blk_done")
        dense(k, pe, blk + 2, 0, 0, rows(k.h_hi), rows(k.h_lo), KT, 0, use + 1, "blk_done")
        pe.wait_ge(k.sem("pool_lo_done"), POOL_GROUPS)
        dense(k, pe, blk + 3, 1, 0, lambda t: one(k.ya_hi, i), lambda t: one(k.ya_lo, i), 1, 1, use + 1, "blk_done")
        pe.wait_ge(k.sem("pair0_out"), use + 3)
        for b in range(KT):
            mm = k.nc.tensor.transpose(k.aps[:, b // 4, (b % 4) * P:(b % 4 + 1) * P], k.sb_vt[:, b * P:(b + 1) * P], ident)
        mm.then_inc(k.sem("sb_vtr_done"), 1)
        pe.wait_ge(k.sem("pair1_out"), use + 2)
        pe.wait_ge(k.sem("sb_v_done"), i + 1)
        for s in range(N_UNITS + 3):
            if s < N_UNITS:
                c, b, h, lo, n = unit(s)
                head = slice(h * HD, (h + 1) * HD)
                if s >= 3:
                    pe.wait_ge(k.sem("sb_a_done"), i * N_UNITS + (s - 2))
                mm = mul(k.aps[:, s % 3, lo:HALF], k.sb_k[head, b * P:(b + 1) * P], k.sb_q[head, c * HALF + lo:(c + 1) * HALF],
                         start=True, stop=False, skip_group_check=True)
                if b >= 4 * c:
                    mm = mul(k.aps[:, s % 3, lo:lo + P], ident, const(k, "sb_mask"), start=False, stop=False, skip_group_check=True)
                mm.then_inc(k.sem("sb_z_done"), 1)
            if 2 <= s < N_UNITS + 2:
                c, b, h, lo, n = unit(s - 2)
                bank = (s - 2) % 3
                pe.wait_ge(k.sem("sb_sp_done"), i * N_UNITS + (s - 1))
                mm = mul(k.aps[:, bank, lo:HALF], const(k, "neg_tri"), k.sb_sp[:, bank, lo:HALF], start=False, stop=n == 0, skip_group_check=True)
                if n:
                    seen = lo + P if b >= 4 * c else lo
                    pe.wait_ge(k.sem("sb_acc_done"), i * ACCS + ACC_COUNT[s - 4])
                    mm = mul(k.aps[:, bank, seen:HALF], const(k, "neg_ones"), k.sb_acc[:, h, n % 2, seen:HALF], start=False, stop=True, skip_group_check=True)
                mm.then_inc(k.sem("sb_r_done"), 1)
            if s >= 3:
                c, b, h, lo, n = unit(s - 3)
                pe.wait_ge(k.sem("sb_a_done"), i * N_UNITS + (s - 2))
                if n == 0 and h == 0 and c == 1:
                    pe.wait_ge(k.sem("sb_y_done"), i * 2 + 1)
                for t in range(lo // P, 4):
                    mm = mul(k.aps[:, 3, t * P + h * HD:t * P + (h + 1) * HD], k.sb_a[:, (s - 3) % 2, t * P:(t + 1) * P],
                             k.sb_v[:, b, h * HD:(h + 1) * HD], start=n == 0 and h == 0 and t == lo // P, stop=b == 0,
                             skip_group_check=True)
                mm.then_inc(k.sem("sb_pv_done"), 1)
                if s - 3 in CHUNK_END:
                    pe.wait_ge(k.sem("sb_o_done"), i * 2 + (c + 1))
                    for t in range(4):
                        mm = k.nc.tensor.transpose(k.aps[:, 3, t * P:(t + 1) * P], k.sb_o[:, t, :], ident)
                    mm.then_inc(k.sem("sb_ot_done"), 1)


def sb_dve(k, dve):
    v = k.nc.vector

    def result(i, c):
        dve.wait_ge(k.sem("sb_yb_hi_done"), i * 2 + (c + 1))
        v.tensor_tensor(one(k.yb_lo, i)[:, c * HALF:(c + 1) * HALF], k.aps[:, 3, :],
                        one(k.yb_hi, i)[:, c * HALF:(c + 1) * HALF].bitcast(F32), ALU.subtract).then_inc(k.sem("sb_y_done"), 1)

    with dve.Fori(0, PAIRS) as i:
        blk, use = i * 4 + BLK["sb"], i * 2 + TILE["sb"] // 2
        dve.wait_ge(k.sem("blk_done"), blk + 1)
        v.scalar_tensor_tensor(k.sb_q[:, :], k.dps[:, 0, :], HD ** -0.5, k.inv[:, :], ALU.mult, ALU.mult).then_inc(k.sem("pair0_out"), 1)
        dve.wait_ge(k.sem("blk_done"), blk + 2)
        v.tensor_tensor(k.sb_k[:, :], k.dps[:, 1, :], k.inv[:, :], ALU.mult).then_inc(k.sem("pair1_out"), 1)
        dve.wait_ge(k.sem("blk_done"), blk + 3)
        v.tensor_tensor(k.sb_vt[:, :], k.dps[:, 0, :], k.inv[:, :], ALU.mult).then_inc(k.sem("pair0_out"), 1)
        dve.wait_ge(k.sem("sb_ya_hi_done"), i + 1)
        v.scalar_tensor_tensor(one(k.ya_lo, i), k.dps[:, 1, :], vec(k, "pool_scale", i), one(k.ya_hi, i).bitcast(F32),
                               ALU.mult, ALU.subtract).then_inc(k.sem("pair1_out"), 1)
        for u in range(N_UNITS):
            c, b, h, lo, n = unit(u)
            dve.wait_ge(k.sem("sb_ln_done"), i * N_UNITS + (u + 1))
            if u >= 3:
                dve.wait_ge(k.sem("sb_r_done"), i * N_UNITS + (u - 2))
            v.scalar_tensor_tensor(k.sb_sp[:, u % 3, lo:], k.aps[:, u % 3, lo:HALF], 0.0, k.sb_e[:, u % 2, lo:],
                                   ALU.max, ALU.add).then_inc(k.sem("sb_sp_done"), 1)
            if b:
                dve.wait_ge(k.sem("sb_sp_done"), i * N_UNITS + (u + 1))
                if u >= 2:
                    dve.wait_ge(k.sem("sb_r_done"), i * N_UNITS + (u - 1))
                seen = lo + P if b >= 4 * c else lo
                if seen > lo:
                    last = v.tensor_copy(k.sb_acc[:, h, (n + 1) % 2, lo:seen], k.sb_sp[:, u % 3, lo:seen])
                if n:
                    dve.wait_ge(k.sem("sb_acc_done"), i * ACCS + ACC_COUNT[u - 2])
                    last = v.tensor_tensor(k.sb_acc[:, h, (n + 1) % 2, seen:], k.sb_acc[:, h, n % 2, seen:],
                                           k.sb_sp[:, u % 3, seen:], ALU.add)
                last.then_inc(k.sem("sb_acc_done"), 1)
            if u == CHUNK_END[0] + 4:
                result(i, 0)
        result(i, 1)


def sb_act(k, act):
    a = k.nc.scalar

    def take(i, c):
        act.wait_ge(k.sem("sb_pv_done"), i * N_UNITS + (CHUNK_END[c] + 1))
        a.activation(k.sb_o[:, :, :].rearrange("p a b -> p (a b)"), k.aps[:, 3, :], ACT.Copy).then_inc(k.sem("sb_o_done"), 1)

    def upper(i, c):
        act.wait_ge(k.sem("sb_ot_done"), i * 2 + (c + 1))
        fixed_wait(k, act)
        a.activation(one(k.yb_hi, i)[:, c * HALF:(c + 1) * HALF], k.aps[:, 3, :], ACT.Copy).then_inc(k.sem("sb_yb_hi_done"), 1)

    a.preload_act_table_set("natural_log_exp_and_others")
    with act.Fori(0, PAIRS) as i:
        act.wait_ge(k.sem("blk_done"), i * 4 + (BLK["sb"] + 4))
        fixed_wait(k, act)
        a.activation(one(k.ya_hi, i), k.dps[:, 1, :], ACT.Copy, scale=vec(k, "pool_scale", i)).then_inc(k.sem("sb_ya_hi_done"), 1)
        act.wait_ge(k.sem("sb_vtr_done"), i + 1)
        a.activation(k.sb_v[:, :, :].rearrange("p a b -> p (a b)"), k.aps[:, 0:2, :].rearrange("p a b -> p (a b)"),
                     ACT.Copy).then_inc(k.sem("sb_v_done"), 1)
        for s in range(N_UNITS + 2):
            if s < N_UNITS:
                c, b, h, lo, n = unit(s)
                e = k.sb_e[:, s % 2, lo:]
                act.wait_ge(k.sem("sb_z_done"), i * N_UNITS + (s + 1))
                if s >= 2:
                    act.wait_ge(k.sem("sb_sp_done"), i * N_UNITS + (s - 1))
                a.activation(e, k.aps[:, s % 3, lo:HALF], ACT.Abs).then_inc(k.sem("sb_abs_done"), 1)
                act.wait_ge(k.sem("sb_abs_done"), i * N_UNITS + (s + 1))
                a.activation(e, e, ACT.Exp, scale=-1.0).then_inc(k.sem("sb_exp_done"), 1)
                act.wait_ge(k.sem("sb_exp_done"), i * N_UNITS + (s + 1))
                a.activation(e, e, ACT.Ln, bias=1.0).then_inc(k.sem("sb_ln_done"), 1)
            if s >= 2:
                u = s - 2
                c, b, h, lo, n = unit(u)
                act.wait_ge(k.sem("sb_r_done"), i * N_UNITS + (u + 1))
                if u >= 2:
                    act.wait_ge(k.sem("sb_pv_done"), i * N_UNITS + (u - 1))
                a.activation(k.sb_a[:, u % 2, lo:], k.aps[:, u % 3, lo:HALF], ACT.Exp).then_inc(k.sem("sb_a_done"), 1)
            if s == CHUNK_END[0] + 3:
                take(i, 0)
            if s == CHUNK_END[0] + 4:
                upper(i, 0)
        take(i, 1)
        upper(i, 1)


def merge_pe(k, pe, blk0, use0, ready=None):
    def gates(i, j):
        blk, use = i * 6 + (blk0 + 3 * j), [i * 4 + (use0[g] + 2 * j) for g in range(2)]
        for g in range(2):
            dense(k, pe, blk + g, (j + g) % 2, 0, rows(k.h_hi), rows(k.h_lo), KT, g, use[g], "blk_done")

    def branches(i, j):
        blk, use = i * 6 + (blk0 + 3 * j), [i * 4 + (use0[g] + 2 * j) for g in range(2)]
        dense(k, pe, blk + 2, j, 0, rows(k.ya_hi), rows(k.ya_lo), 4, 0, use[0] + 1, "branch_a_done")
        dense(k, pe, blk + 2, j, 4, rows(k.yb_hi), rows(k.yb_lo), 4, 1, use[1] + 1, "blk_done")

    if ready is None:
        gates(0, 0)
    else:
        pe.wait_ge(k.sem(ready[0]), ready[1])
    with pe.Fori(0, KT // 2 - 1) as i:
        for j in range(2):
            branches(i, j)
            gates(i + j, 1 - j)
    branches(KT // 2 - 1, 0)
    gates(KT // 2 - 1, 1)
    branches(KT // 2 - 1, 1)


def merge_dve(k, dve, blk0, use0, call):
    v = k.nc.vector
    with dve.Fori(0, KT // 2) as i:
        for j in range(2):
            n, blk, use = i * 2 + j, i * 6 + (blk0 + 3 * j), [i * 4 + (use0[g] + 2 * j) for g in range(2)]
            for g in range(2):
                dve.wait_ge(k.sem("blk_done"), blk + (g + 1))
                v.tensor_tensor(k.tmp[g][:, :], k.dps[:, g, :], k.inv[:, :], ALU.mult).then_inc(k.sem(f"pair{g}_out"), 1)
            dve.wait_ge(k.sem("branch_a_done"), i * 2 + (KT * call + j + 1))
            dve.wait_ge(k.sem("gate_done"), i * 4 + (2 * KT * call + 2 * j + 1))
            v.tensor_tensor(one(k.merged, n), k.dps[:, 0, :], k.tmp0[:, :], ALU.mult).then_inc(k.sem("pair0_out"), 1)
            dve.wait_ge(k.sem("blk_done"), blk + 3)
            dve.wait_ge(k.sem("gate_done"), i * 4 + (2 * KT * call + 2 * j + 2))
            v.tensor_tensor(k.tmp1[:, :], k.dps[:, 1, :], k.tmp1[:, :], ALU.mult).then_inc(k.sem("pair1_out"), 1)
            dve.wait_ge(k.sem("pair0_out"), use[0] + 3)
            dve.wait_ge(k.sem("pair1_out"), use[1] + 3)
            v.tensor_tensor(one(k.merged, n), one(k.merged, n), k.tmp1[:, :], ALU.add).then_inc(k.sem("merged_done"), 1)
            dve.wait_ge(k.sem("merged_done"), i * 2 + (KT * call + j + 1))


def merge_act(k, act, use0, bias):
    with act.Fori(0, KT // 2) as i:
        for j in range(2):
            for g in range(2):
                act.wait_ge(k.sem(f"pair{g}_out"), i * 4 + (use0[g] + 2 * j + 2))
                if bias is not None:
                    fixed_wait(k, act)
                b = 0.0 if bias is None else vec(k, bias, i * 2 + (j + KT * g))
                k.nc.scalar.activation(k.tmp[g][:, :], k.tmp[g][:, :], ACT.Sigmoid, bias=b).then_inc(k.sem("gate_done"), 1)


def merged_split_act(k, act, blk_end, call):
    act.wait_ge(k.sem("blk_done"), blk_end)
    act.wait_ge(k.sem("merged_done"), KT * (call + 1))
    for n in range(KT):
        split_act(k, act, n, src=k.merged)


def merged_split_dve(k, dve, fill, call):
    dve.wait_ge(k.sem("merged_done"), KT * (call + 1))
    for n in range(KT):
        split_dve(k, dve, fill, n, src=k.merged)


def out_pe(k, pe):
    with pe.Fori(0, KT // 2) as i:
        for j in range(2):
            dense(k, pe, i * 2 + (BLK["out"] + j), j, 0, rows(k.h_hi), rows(k.h_lo), KT, j, i + TILE["out"] // 2, "blk_done",
                  ready=("h_lo_done", KT) if j == 0 else None)
    stat(k, pe, 1)


def out_dve(k, dve):
    sumsq_begin(k, dve, 1)
    dve.wait_ge(k.sem("x_again_loaded"), 16)
    with dve.Fori(0, KT // 2) as i:
        for j in range(2):
            n = i * 2 + j
            dve.wait_ge(k.sem("blk_done"), i * 2 + (BLK["out"] + j + 1))
            k.nc.vector.tensor_tensor(one(k.x, n), k.dps[:, j, :], one(k.x_again, n), ALU.add).then_inc(k.sem(f"pair{j}_out"), 1)
            sumsq_dve(k, dve, 1, n, k.sq[j][:, :])
    for n in range(KT):
        split_dve(k, dve, 2, n, "norm_ffn")
    inv_dve(k, dve, 1)


def out_act(k, act, x_t):
    act.wait_ge(k.sem("blk_done"), BLK["out"])
    act.dma_start(k.x_again[:, :, :], x_t).then_inc(k.sem("x_again_loaded"), 16)
    merged_split_act(k, act, BLK["out"], 0)
    with act.Fori(0, KT // 2) as i:
        for j in range(2):
            act.wait_ge(k.sem(f"pair{j}_out"), i + (TILE["out"] // 2 + 2))
            square_act(k, act, 1, i * 2 + j, k.sq[j][:, :])
    act.wait_ge(k.sem("blk_done"), BLK["ffn"])
    for n in range(KT):
        split_act(k, act, n, "norm_ffn")
    inv_act(k, act, 1)


def ffn_places():
    before, blk, tile = 0, BLK["ffn"], TILE["ffn"]
    for c, n in enumerate(FF_CHUNKS):
        yield c, n, before, blk, tile, blk + 2 * n, tile + 2 * n
        before, blk, tile = before + n, blk + 2 * n + KT, tile + 2 * n + KT


def ffn_pe(k, pe):
    for c, n_f, before, blk, tile, blk_d, tile_d in ffn_places():
        with pe.Fori(0, n_f) as i:
            dense(k, pe, i * 2 + blk, 0, 0, rows(k.h_hi), rows(k.h_lo), KT, 0, i + tile // 2, "blk_done",
                  ready=("h_lo_done", 2 * KT) if c == 0 else None)
            dense(k, pe, i * 2 + (blk + 1), 1, 0, rows(k.h_hi), rows(k.h_lo), KT, 1, i + tile // 2, "blk_done")
        with pe.Fori(0, KT // 2) as i:
            for j in range(2):
                dense(k, pe, i * 2 + (blk_d + j), j, 0, rows(k.hid_hi), rows(k.hid_lo), n_f, j, i + tile_d // 2, "blk_done",
                      ready=("hid_lo_done", before) if j == 0 else None)
    stat(k, pe, 2)


def ffn_dve(k, dve):
    v = k.nc.vector
    for c, n_f, before, blk, tile, blk_d, tile_d in ffn_places():
        with dve.Fori(0, n_f) as i:
            dve.wait_ge(k.sem("blk_done"), i * 2 + (blk + 1))
            v.tensor_tensor(k.tmp0[:, :], k.dps[:, 0, :], k.inv[:, :], ALU.mult).then_inc(k.sem("pair0_out"), 1)
            dve.wait_ge(k.sem("blk_done"), i * 2 + (blk + 2))
            v.tensor_tensor(k.tmp1[:, :], k.dps[:, 1, :], k.inv[:, :], ALU.mult).then_inc(k.sem("pair1_out"), 1)
            dve.wait_ge(k.sem("silu_done"), i + (before + 1))
            dve.wait_ge(k.sem("pair1_out"), i + (tile // 2 + 2))
            v.tensor_tensor(k.tmp1[:, :], k.tmp1[:, :], k.tmp0[:, :], ALU.mult).then_inc(k.sem("hid_done"), 1)
            dve.wait_ge(k.sem("hid_hi_done"), i + (before + 1))
            v.tensor_tensor(one(k.hid_lo, i), k.tmp1[:, :], one(k.hid_hi, i).bitcast(F32), ALU.subtract).then_inc(k.sem("hid_lo_done"), 1)
            dve.wait_ge(k.sem("hid_lo_done"), i + (before + 1))
        last = c == len(FF_CHUNKS) - 1
        if last:
            sumsq_begin(k, dve, 2)
        with dve.Fori(0, KT // 2) as i:
            for j in range(2):
                n = i * 2 + j
                dve.wait_ge(k.sem("blk_done"), i * 2 + (blk_d + j + 1))
                v.tensor_tensor(one(k.x, n), k.dps[:, j, :], one(k.x, n), ALU.add).then_inc(k.sem(f"pair{j}_out"), 1)
                if last:
                    split_dve(k, dve, 3, n, "norm_ple")
                    sumsq_dve(k, dve, 2, n, k.sq[j][:, :])
    inv_dve(k, dve, 2)


def ffn_act(k, act):
    a = k.nc.scalar
    for c, n_f, before, blk, tile, blk_d, tile_d in ffn_places():
        with act.Fori(0, n_f) as i:
            act.wait_ge(k.sem("pair0_out"), i + (tile // 2 + 2))
            a.activation(k.tmp0[:, :], k.tmp0[:, :], ACT.Silu).then_inc(k.sem("silu_done"), 1)
            act.wait_ge(k.sem("hid_done"), i + (before + 1))
            fixed_wait(k, act)
            a.activation(one(k.hid_hi, i), k.tmp1[:, :], ACT.Copy).then_inc(k.sem("hid_hi_done"), 1)
        if c == len(FF_CHUNKS) - 1:
            with act.Fori(0, KT // 2) as i:
                for j in range(2):
                    act.wait_ge(k.sem(f"pair{j}_out"), i + (tile_d // 2 + 2))
                    square_wait(k, act, 2, i * 2 + j)
                    split_act(k, act, i * 2 + j, "norm_ple")
                    square_act(k, act, 2, i * 2 + j, k.sq[j][:, :], waited=True)
    inv_act(k, act, 2)


def ple_pe(k, pe):
    with pe.Fori(0, KT // 2) as i:
        for j in range(2):
            blk, use = i * 4 + (BLK["ple"] + 2 * j), i * 2 + (TILE["ple"] // 2 + j)
            dense(k, pe, blk, 0, 0, rows(k.h_hi), rows(k.h_lo), KT, 0, use, "blk_done",
                  ready=("h_lo_done", 3 * KT) if j == 0 else None)
            dense(k, pe, blk + 1, 1, 0, rows(k.p_hi), rows(k.p_lo), 2, 1, use, "blk_done",
                  ready=("p_lo_done", 0) if j == 0 else None)
    stat(k, pe, 3)


def ple_dve(k, dve):
    v = k.nc.vector
    for t in range(2):
        dve.wait_ge(k.sem("p_hi_done"), t + 1)
        v.tensor_tensor(k.p_lo[:, t, :], k.p_raw[:, t, :], k.p_hi[:, t, :].bitcast(F32), ALU.subtract).then_inc(k.sem("p_lo_done"), 1)
    sumsq_begin(k, dve, 3)
    with dve.Fori(0, KT // 2) as i:
        for j in range(2):
            n, blk, use = i * 2 + j, i * 4 + (BLK["ple"] + 2 * j), i * 2 + (TILE["ple"] // 2 + j)
            dve.wait_ge(k.sem("blk_done"), blk + 1)
            v.tensor_tensor(k.tmp[j][:, :], k.dps[:, 0, :], k.inv[:, :], ALU.mult).then_inc(k.sem("pair0_out"), 1)
            dve.wait_ge(k.sem("blk_done"), blk + 2)
            dve.wait_ge(k.sem("ple_gate_done"), n + 1)
            v.tensor_tensor(k.tmp[j][:, :], k.dps[:, 1, :], k.tmp[j][:, :], ALU.mult).then_inc(k.sem("pair1_out"), 1)
            dve.wait_ge(k.sem("pair1_out"), use + 2)
            v.tensor_tensor(one(k.x, n), one(k.x, n), k.tmp[j][:, :], ALU.add).then_inc(k.sem("ple_x_done"), 1)
            sumsq_dve(k, dve, 3, n, k.sq_ple[j][:, :])
    inv_dve(k, dve, 3)


def ple_act(k, act, p_t):
    a = k.nc.scalar
    act.wait_ge(k.sem("blk_done"), BLK["ple"])
    act.dma_start(k.p_raw[:, :, :], p_t).then_inc(k.sem("p_loaded"), 16)
    act.wait_ge(k.sem("p_loaded"), 16)
    for t in range(2):
        a.activation(k.p_hi[:, t, :], k.p_raw[:, t, :], ACT.Copy).then_inc(k.sem("p_hi_done"), 1)
    with act.Fori(0, KT // 2) as i:
        for j in range(2):
            n, use = i * 2 + j, i * 2 + (TILE["ple"] // 2 + j)
            act.wait_ge(k.sem("pair0_out"), use + 2)
            a.activation(k.tmp[j][:, :], k.tmp[j][:, :], ACT.Sigmoid).then_inc(k.sem("ple_gate_done"), 1)
            act.wait_ge(k.sem("ple_x_done"), n + 1)
            square_act(k, act, 3, n, k.sq_ple[j][:, :])
    inv_act(k, act, 3)



def bridge_dve(k, dve):
    sumsq_begin(k, dve, 4)
    for n in range(KT + 1):
        if n < KT:
            k.nc.vector.scalar_tensor_tensor(k.x[:, n, :], k.x[:, n, :], vec(k, "norm_final", n), k.inv[:, :],
                                             ALU.mult, ALU.mult).then_inc(k.sem("x1_done"), 1)
        if n:
            split_dve(k, dve, 4, n - 1, "g_pre")
            sumsq_dve(k, dve, 4, n - 1, k.sq[(n - 1) % 2][:, :])
    inv_dve(k, dve, 4)


def bridge_act(k, act, x1_t, pos_t):
    for n in range(KT):
        act.wait_ge(k.sem("x1_done"), n + 1)
        split_act(k, act, n, "g_pre")
        square_act(k, act, 4, n, k.sq[n % 2][:, :])
        if n % 2:
            act.dma_start(x1_t[:, n - 1:n + 1, :], k.x[:, n - 1:n + 1, :]).then_inc(k.sem("x1_spilled"), 16)
    inv_act(k, act, 4)
    act.wait_ge(k.sem("sumsq_done"), KT * 5 + 2)
    act.dma_start(k.pos[:, :], pos_t).then_inc(k.sem("pos_loaded"), 16)


LATENT_USE = TILE["mla"] // 2


def latent_pe(k, pe):
    b = BLK["mla"]
    mul = k.nc.tensor.matmul
    dense(k, pe, b, 0, 0, rows(k.h_hi), rows(k.h_lo), KT, 0, LATENT_USE, "blk_done", ready=("h_lo_done", 4 * KT))
    stat(k, pe, 4)
    dense(k, pe, b + 1, 1, 0, rows(k.h_hi), rows(k.h_lo), KT, 1, LATENT_USE, "blk_done")
    dense(k, pe, b + 2, 0, 0, rows(k.h_hi), rows(k.h_lo), KT, 0, LATENT_USE + 1, "blk_done")
    dense(k, pe, b + 3, 1, 0, rows(k.h_hi), rows(k.h_lo), KT, 1, LATENT_USE + 1, "blk_done")
    pe.wait_ge(k.sem("pe_rot_done"), 1)
    for h in range(2):
        mm = mul(k.aps[:, h, :], const(k, "rope_sum", HD, P), k.pe_raw[HD:P, h * HALF:(h + 1) * HALF], start=True, stop=True)
    mm.then_inc(k.sem("pe_sum_done"), 1)
    pe.wait_ge(k.sem("latent_sq_done"), 1)
    for h in range(2):
        mm = mul(k.aps[:, 2 + h, :], const(k, "mean"), k.latent_sq[:, 2, h * HALF:(h + 1) * HALF], start=True, stop=True)
    mm.then_inc(k.sem("latent_stat_done"), 1)
    pe.wait_ge(k.sem("latent_sq_done"), 3)
    pe.wait_ge(k.sem("pe_key_done"), 1)
    for h in range(2):
        for n in range(2):
            mm = mul(k.aps[:, h, :], const(k, "mean"), k.latent_sq[:, n, h * HALF:(h + 1) * HALF], start=n == 0, stop=n == 1)
    mm.then_inc(k.sem("latent_stat_done"), 1)


def latent_dve(k, dve):
    v = k.nc.vector
    r = CONST["rope"][0]
    col = lambda n: k.const[:, r + n:r + n + 1]
    dve.wait_ge(k.sem("pos_loaded"), 16)
    dve.wait_ge(k.sem("x1_spilled"), 64)
    steps = (lambda: v.tensor_scalar(k.angle[:, :], k.pos[:, :], col(0), None, ALU.mult),
             lambda: v.tensor_scalar(k.turns[:, :], k.angle[:, :], 0.5 / np.pi, col(1), ALU.mult, ALU.add),
             lambda: v.tensor_scalar(k.turns[:, :], k.turns[:, :], ROUND, -ROUND, ALU.add, ALU.add),
             lambda: v.scalar_tensor_tensor(k.angle[:, :], k.turns[:, :], -TWO_PI[0], k.angle[:, :], ALU.mult, ALU.add),
             lambda: v.scalar_tensor_tensor(k.angle[:, :], k.turns[:, :], -TWO_PI[1], k.angle[:, :], ALU.mult, ALU.add),
             lambda: v.scalar_tensor_tensor(k.angle[:, :], k.turns[:, :], -TWO_PI[2], k.angle[:, :], ALU.mult, ALU.add),
             lambda: v.tensor_scalar(k.angle[:, :], k.angle[:, :], col(2), PI_BELOW, ALU.add, ALU.min),
             lambda: v.tensor_scalar(k.angle[:, :], k.angle[:, :], -PI_BELOW, None, ALU.max))
    for n, step in enumerate(steps):
        step().then_inc(k.sem("angle_done"), 1)
        dve.wait_ge(k.sem("angle_done"), n + 1)
    dve.wait_ge(k.sem("blk_done"), BLK["mla"] + 1)
    v.tensor_tensor(k.pe_raw[HD:P, :], k.dps[HD:P, 0, :], k.inv[HD:P, :], ALU.mult).then_inc(k.sem("pair0_out"), 1)
    for n, (pair, use) in enumerate(((1, LATENT_USE), (0, LATENT_USE + 1), (1, LATENT_USE + 1))):
        dve.wait_ge(k.sem("blk_done"), BLK["mla"] + n + 2)
        v.tensor_tensor(k.latent[:, (n + 2) % 3, :], k.dps[:, pair, :], k.inv[:, :], ALU.mult).then_inc(k.sem(f"pair{pair}_out"), 1)
        if n == 0:
            dve.wait_ge(k.sem("sin_done"), 1)
            v.tensor_scalar(k.trig[:, :], k.trig[:, :], col(3), None, ALU.mult).then_inc(k.sem("trig_done"), 1)
            dve.wait_ge(k.sem("trig_done"), 1)
            dve.wait_ge(k.sem("pair0_out"), LATENT_USE + 2)
            v.tensor_tensor(k.pe_raw[HD:P, :], k.pe_raw[HD:P, :], k.trig[HD:P, :], ALU.mult).then_inc(k.sem("pe_rot_done"), 1)
    dve.wait_ge(k.sem("latent_std_done"), 1)
    v.reciprocal(k.inv_kv[:, :], k.latent_std[:, 0, :]).then_inc(k.sem("latent_inv_done"), 1)
    dve.wait_ge(k.sem("latent_hi_done"), 1)
    v.scalar_tensor_tensor(k.ckv_lo[:, 0, :], k.latent[:, 2, :], vec(k, "g_kv", 0), k.ckv_hi[:, 0, :].bitcast(F32),
                           ALU.mult, ALU.subtract).then_inc(k.sem("latent_lo_done"), 1)
    for n in range(2):
        dve.wait_ge(k.sem("latent_hi_done"), n + 2)
        v.scalar_tensor_tensor(k.cq_lo[:, n, :], k.latent[:, n, :], vec(k, "g_q", n), k.cq_hi[:, n, :].bitcast(F32),
                               ALU.mult, ALU.subtract).then_inc(k.sem("latent_lo_done"), 1)
    dve.wait_ge(k.sem("latent_std_done"), 2)
    v.reciprocal(k.inv_q[:, :], k.latent_std[:, 1, :]).then_inc(k.sem("latent_inv_done"), 1)
    dve.wait_ge(k.sem("latent_inv_done"), 2)


def latent_act(k, act):
    a = k.nc.scalar
    act.wait_ge(k.sem("angle_done"), 8)
    a.activation(k.trig[:, :], k.angle[:, :], ACT.Sin).then_inc(k.sem("sin_done"), 1)
    act.wait_ge(k.sem("pair1_out"), LATENT_USE + 2)
    a.activation(k.latent_sq[:, 2, :], k.latent[:, 2, :], ACT.Square).then_inc(k.sem("latent_sq_done"), 1)
    act.wait_ge(k.sem("pe_sum_done"), 1)
    a.activation(k.mla_k[HD:P, :], k.aps[HD:P, 0:2, :].rearrange("p a b -> p (a b)"), ACT.Copy).then_inc(k.sem("pe_key_done"), 1)
    a.activation(k.ckv_hi[:, 0, :], k.latent[:, 2, :], ACT.Copy, scale=vec(k, "g_kv", 0)).then_inc(k.sem("latent_hi_done"), 1)
    for n in range(2):
        act.wait_ge(k.sem(f"pair{n}_out"), LATENT_USE + 3)
        a.activation(k.latent_sq[:, n, :], k.latent[:, n, :], ACT.Square).then_inc(k.sem("latent_sq_done"), 1)
        a.activation(k.cq_hi[:, n, :], k.latent[:, n, :], ACT.Copy, scale=vec(k, "g_q", n)).then_inc(k.sem("latent_hi_done"), 1)
    for n, (bank, width) in enumerate(((2, 128), (0, 256))):
        act.wait_ge(k.sem("latent_stat_done"), n + 1)
        a.activation(k.latent_std[:, n, :], k.aps[:, bank:bank + 2, :].rearrange("p a b -> p (a b)"), ACT.Sqrt, bias=EPS,
                     scale=D / width).then_inc(k.sem("latent_std_done"), 1)


MLA_USE0 = LATENT_USE + 2
MLA_USE1 = LATENT_USE + 2
GROUPS = [(b, g, min(4, b + 1 - g)) for b in range(KT) for g in range(0, b + 1, 4)]
N_GROUPS = len(GROUPS)


def mla_pe(k, pe):
    mul, ident = k.nc.tensor.matmul, const(k, "ident")
    for_pair = 6
    with pe.Fori(0, PAIRS) as i:
        blk, use = i * 2 + (BLK["mla"] + 4), i * for_pair + MLA_USE0
        dense(k, pe, blk, 0, 0, rows(k.h_hi), rows(k.h_lo), KT, 0, use, "blk_done")
        pe.wait_ge(k.sem("latent_lo_done"), 3)
        for h in range(2):
            def scores(b):
                n = i * 16 + (8 * h + b + 1)
                r = b % 2
                if b >= 2:
                    pe.wait_ge(k.sem("mla_exp_done"), n - 2)
                for lo in range(0, (b + 1) * P, HALF):
                    hi = min(lo + HALF, (b + 1) * P)
                    mm = mul(k.aps[:, 2 * r + lo // HALF, 0:hi - lo], k.mla_q[:, b * P:(b + 1) * P], k.mla_k[:, lo:hi],
                             start=True, stop=False, skip_group_check=True)
                at = b * P % HALF
                mm = mul(k.aps[:, 2 * r + b * P // HALF, at:at + P], ident, const(k, "mla_mask"), start=False, stop=True, skip_group_check=True)
                mm.then_inc(k.sem("mla_s_done"), 1)

            def turn(g):
                b, first, n = GROUPS[g]
                c = i * 2 * N_GROUPS + (N_GROUPS * h + g)
                pe.wait_ge(k.sem("mla_p_done"), i * 16 + (8 * h + b + 1))
                if g:
                    pe.wait_ge(k.sem("mla_pt_done"), c)
                for t in range(n):
                    mm = k.nc.tensor.transpose(k.dps[:, 1, t * P:(t + 1) * P], k.mla_p[:, b % 2, (first + t) * P:(first + t + 1) * P], ident)
                mm.then_inc(k.sem("mla_t_done"), 1)

            def values(g):
                b, first, n = GROUPS[g]
                pe.wait_ge(k.sem("mla_pt_done"), i * 2 * N_GROUPS + (N_GROUPS * h + g + 1))
                for t in range(n):
                    mm = mul(k.dps[:, 1, HALF + b * HD:HALF + (b + 1) * HD], k.mla_pt[:, g % 2, t * P:(t + 1) * P],
                             k.mla_v[:, h, first + t, :], start=g == 0 and t == 0, stop=first + t == b, skip_group_check=True)
                mm.then_inc(k.sem("mla_pv_done"), 1)

            dense(k, pe, blk + 1, 1, 3 * h, rows(k.cq_hi), rows(k.cq_lo), 2, 0, use + (1 + 2 * h), "mla_proj_done")
            dense(k, pe, blk + 1, 1, 3 * h + 2, rows(k.ckv_hi), rows(k.ckv_lo), 1, 0, use + (2 + 2 * h), "blk_done" if h else "mla_proj_done")
            pe.wait_ge(k.sem("pair0_out"), use + (4 + 2 * h))
            if h:
                pe.wait_ge(k.sem("mla_o_done"), i * 2 + 1)
            for b in range(KT):
                mm = mul(k.dps[:, 1, b * HD:(b + 1) * HD], k.mla_vt[HD:P, b * P:(b + 1) * P], const(k, "ident", HD, P)[:, HD:P],
                         start=True, stop=True)
            mm.then_inc(k.sem("mla_vtr_done"), 1)
            pe.wait_ge(k.sem("mla_q_done"), i * 2 + (h + 1))
            scores(0)
            scores(1)
            pe.wait_ge(k.sem("mla_v_done"), i * 2 + (h + 1))
            g = 0
            for s in range(2, KT + 2):
                if s < KT:
                    scores(s)
                while g < N_GROUPS and GROUPS[g][0] == s - 2:
                    turn(g)
                    if g:
                        values(g - 1)
                    g += 1
            values(N_GROUPS - 1)
        pe.wait_ge(k.sem("mla_o_done"), i * 2 + 2)
        pe.wait_ge(k.sem("pair0_out"), use + 6)
        for b in range(KT):
            mm = k.nc.tensor.transpose(k.dps[:, 0, b * P:(b + 1) * P], k.mla_o[:, b, :], ident)
        mm.then_inc(k.sem("mla_yt_done"), 1)


def mla_dve(k, dve):
    v = k.nc.vector
    with dve.Fori(0, PAIRS) as i:
        blk, use = i * 2 + (BLK["mla"] + 4), i * 6 + MLA_USE0
        dve.wait_ge(k.sem("blk_done"), blk + 1)
        v.tensor_tensor(k.mla_gate[:, :], k.dps[:, 0, :], k.inv[:, :], ALU.mult).then_inc(k.sem("pair0_out"), 1)
        for h in range(2):
            dve.wait_ge(k.sem("mla_proj_done"), i * 3 + (2 * h + 1))
            v.tensor_tensor(k.mla_q[:, :], k.dps[:, 0, :], k.inv_q[:, :], ALU.mult).then_inc(k.sem("pair0_out"), 1)
            dve.wait_ge(k.sem("pair0_out"), use + (3 + 2 * h))
            v.tensor_tensor(k.mla_q[HD:P, :], k.mla_q[HD:P, :], k.trig[HD:P, :], ALU.mult).then_inc(k.sem("mla_q_done"), 1)
            if h:
                dve.wait_ge(k.sem("blk_done"), blk + 2)
            else:
                dve.wait_ge(k.sem("mla_proj_done"), i * 3 + 2)
            v.tensor_tensor(k.mla_k[0:HD, :], k.dps[0:HD, 0, :], k.inv_kv[0:HD, :], ALU.mult).then_inc(k.sem("mla_k_done"), 1)
            v.tensor_tensor(k.mla_vt[HD:P, :], k.dps[HD:P, 0, :], k.inv_kv[HD:P, :], ALU.mult).then_inc(k.sem("pair0_out"), 1)

            def normalise(b):
                n = i * 16 + (8 * h + b + 1)
                r = b % 2
                dve.wait_ge(k.sem("mla_exp_done"), n)
                v.reciprocal(k.mla_sum[:, r, 1:2], k.mla_sum[:, r, 0:1]).then_inc(k.sem("mla_rsum_done"), 1)
                dve.wait_ge(k.sem("mla_rsum_done"), n)
                v.tensor_scalar(k.mla_p[:, r, 0:(b + 1) * P], k.mla_p[:, r, 0:(b + 1) * P], k.mla_sum[:, r, 1:2], None,
                                ALU.mult).then_inc(k.sem("mla_p_done"), 1)

            for b in range(KT):
                n = i * 16 + (8 * h + b + 1)
                r = b % 2
                dve.wait_ge(k.sem("mla_s_done"), n)
                v.tensor_reduce(k.mla_max[:, r, 0:1], k.aps[:, 2 * r:2 * r + 2, :].rearrange("p a b -> p (a b)")[:, 0:(b + 1) * P],
                                AX.X, ALU.max).then_inc(k.sem("mla_max_done"), 1)
                dve.wait_ge(k.sem("mla_max_done"), n)
                v.tensor_scalar(k.mla_max[:, r, 1:2], k.mla_max[:, r, 0:1], -MLA_SCALE, None, ALU.mult).then_inc(k.sem("mla_neg_done"), 1)
                if b:
                    normalise(b - 1)
            normalise(KT - 1)
        dve.wait_ge(k.sem("mla_yt_done"), i + 1)
        dve.wait_ge(k.sem("mla_gate_done"), i + 1)
        v.tensor_tensor(one(k.mla_out, i), k.dps[:, 0, :], k.mla_gate[:, :], ALU.mult).then_inc(k.sem("pair0_out"), 1)
        dve.wait_ge(k.sem("pair0_out"), use + 7)


def mla_act(k, act):
    a = k.nc.scalar
    with act.Fori(0, PAIRS) as i:
        use = i * 6 + MLA_USE0
        act.wait_ge(k.sem("pair0_out"), use + 2)
        a.activation(k.mla_gate[:, :], k.mla_gate[:, :], ACT.Silu).then_inc(k.sem("mla_gate_done"), 1)
        for h in range(2):
            act.wait_ge(k.sem("mla_vtr_done"), i * 2 + (h + 1))
            a.activation(k.mla_v[:, h, :, :].rearrange("p a b -> p (a b)"), k.dps[:, 1, 0:HALF], ACT.Copy).then_inc(k.sem("mla_v_done"), 1)
            g = 0
            for s in range(KT + 2):
                while g < N_GROUPS and GROUPS[g][0] == s - 2:
                    c = i * 2 * N_GROUPS + (N_GROUPS * h + g)
                    act.wait_ge(k.sem("mla_t_done"), c + 1)
                    if g >= 2:
                        act.wait_ge(k.sem("mla_pv_done"), c - 1)
                    w = GROUPS[g][2] * P
                    a.activation(k.mla_pt[:, g % 2, 0:w], k.dps[:, 1, 0:w], ACT.Copy).then_inc(k.sem("mla_pt_done"), 1)
                    g += 1
                if s < KT:
                    n = i * 16 + (8 * h + s + 1)
                    r = s % 2
                    act.wait_ge(k.sem("mla_neg_done"), n)
                    a.activation(k.mla_p[:, r, 0:(s + 1) * P], k.aps[:, 2 * r:2 * r + 2, :].rearrange("p a b -> p (a b)")[:, 0:(s + 1) * P],
                                 ACT.Exp, bias=k.mla_max[:, r, 1:2], scale=MLA_SCALE, accum_out=k.mla_sum[:, r, 0:1]).then_inc(k.sem("mla_exp_done"), 1)
            act.wait_ge(k.sem("mla_pv_done"), i * 2 * N_GROUPS + N_GROUPS * (h + 1))
            a.activation(k.mla_o[:, :, h * HD:(h + 1) * HD], k.dps[:, 1, HALF:2 * HALF].rearrange("p (a b) -> p a b", a=KT),
                         ACT.Copy).then_inc(k.sem("mla_o_done"), 1)


LEVEL_STEPS = range(1, LEVELS + 1)


class Steps:

    def __init__(self, sem, names):
        self.sem, self.names = sem, names


LEVEL_NAMES = [f"{n}{l}" for l in LEVEL_STEPS for n in ("t", "x", "xt") if (n, l) != ("x", LEVELS)]
AHEAD = Steps("rw_ahead", ["rp", "kkp", "bq", "kq", "l_rel", "be", "ke", "rk"])
EXPS = Steps("rw_exps", ["p", "pp", "q", "e"])
PRODUCTS = Steps("rw_product", ["rk", "lt", "l", "ak_t", "rb_t", "rk_t", "kkp_tm", "v_tm", "akv", "be_tm", "ke_tm"] + LEVEL_NAMES
                 + ["u0", "w1_t"] + [f"{n}{c}" for c in range(NC) for n in ("w1s", "ds")])
VALUES = Steps("rw_value", ["rkv", "lt", "xt_part", "xt0", "x_part", "x0", "ak_t", "rb_t", "rk_t"] + LEVEL_NAMES
               + ["s_in"] + [f"{n}{c}" for c in range(NC) for n in ("u", "s")])
COPIES = Steps("rw_copy", ["kkp_tm", "v_tm", "akv", "be_tm", "ke_tm", "u0", "w1_t"])
Y_PRODUCTS = Steps("rw_y_product", ["y", "mean", "var"])
Y_VALUES = Steps("rw_y_value", ["centred", "rstd", "normed", "gained", "summed"])
Y_COPIES = Steps("rw_y_copy", ["y", "sq", "std"])
TAKEN_BY = {"rk": (VALUES, "rkv"), "lt": (VALUES, "xt_part"), "l": (VALUES, "x_part"), **{n: (VALUES, n) for n in ["ak_t", "rb_t", "rk_t"] + LEVEL_NAMES},
            **{n: (COPIES, n) for n in COPIES.names}}
BANKS = 3
RW_USE0 = MLA_USE0 + 6 * PAIRS
RW_USE1 = MLA_USE1


class Half:

    def __init__(self, k, i, g):
        self.k, self.i, self.g = k, i, g
        self.tokens = slice(g * HALF, (g + 1) * HALF)

    def at(self, steps, name):
        n = len(steps.names)
        return self.i * (2 * n) + (self.g * n + steps.names.index(name) + 1)

    def wait(self, engine, steps, name):
        engine.wait_ge(self.k.sem(steps.sem), self.at(steps, name))


def bank(k, name):
    return k.aps[:, PRODUCTS.names.index(name) % BANKS, :]


def chunks(ap):
    return ap.rearrange("p (c t) -> p c t", c=NC)


def flat(t):
    return t[:, :, :].rearrange("p a b -> p (a b)")


HEADS = tuple(slice(h * HD, (h + 1) * HD) for h in range(2))


def masked(k, name):
    return const(k, name).rearrange("p (a b) -> p a b", a=1).to_broadcast([P, NC, HD])


def both(k, out, lhs, rhs, start=True, stop=True):
    for head in HEADS:
        mm = k.nc.tensor.matmul(out[head], lhs[head], rhs[head], start=start, stop=stop, skip_group_check=True)
    return mm


def rw_pe(k, pe):
    mul = k.nc.tensor.matmul
    second = lambda x: lambda t: x[:, t + 4, :]
    dense(k, pe, BLK["rwkv"], 0, 0, rows(k.h_hi), rows(k.h_lo), 4, 0, RW_USE0, "blk_done", last=False)
    dense(k, pe, BLK["rwkv"] + 1, 1, 0, second(k.h_hi), second(k.h_lo), 4, 0, RW_USE0, "blk_done", first=False)
    for n, use in enumerate((RW_USE0 + 1, RW_USE1)):
        dense(k, pe, BLK["rwkv"] + (2 + n), n, 0, rows(k.h_hi), rows(k.h_lo), KT, n, use, "blk_done")
    pe.wait_ge(k.sem("rw_tanh_done"), 1)
    rw_pair_pe(k, pe, 0, None)
    with pe.Fori(1, PAIRS) as i:
        rw_pair_pe(k, pe, i, Half(k, i - 1, 1))
    for name in ("mean", "var"):
        rw_result_pe(k, pe, Half(k, PAIRS - 1, 1), name)


def rw_pair_pe(k, pe, i, before):
    mul = k.nc.tensor.matmul
    blk, use0, use1 = i * 4 + (BLK["rwkv"] + 2), i * 3 + (RW_USE0 + 1), i * 3 + RW_USE1
    pe.wait_ge(k.sem("rw_up_loaded"), i * 16 + 16)
    for n, (use, done) in enumerate(((use0, "rw_w_done"), (use1, "rw_a_done"))):
        pe.wait_ge(k.sem(f"pair{n}_out"), use + 2)
        for h in range(2):
            mm = mul(k.dps[:, n, h * HALF:(h + 1) * HALF], k.rw_up[HEADS[n], :], k.rw_wdad[HEADS[n], h * HALF:(h + 1) * HALF],
                     start=True, stop=True)
        mm.then_inc(k.sem(done), 1)
    pe.wait_ge(k.sem("rw_kk_sq_done"), i + 1)
    for h in range(2):
        mm = mul(k.aps[:, h, :], const(k, "headsum"), k.rw_e[:, h * HALF:(h + 1) * HALF], start=True, stop=True)
    mm.then_inc(k.sem("rw_kk_norm_done"), 1)
    dense(k, pe, blk + 2, 0, 0, rows(k.h_hi), rows(k.h_lo), KT, 0, use0 + 2, "blk_done")
    dense(k, pe, blk + 3, 1, 0, rows(k.h_hi), rows(k.h_lo), KT, 1, use1 + 2, "blk_done")
    first, last = Half(k, i, 0), Half(k, i, 1)
    rw_half_pe(k, pe, first, before, (blk + 4, 0, 0, use0 + 3))
    rw_half_pe(k, pe, last, first, (blk + 5, 1, 1, use1 + 3))


def rw_half_pe(k, pe, u, before, tile):
    product = k.sem("rw_product")
    made = {name: t[u.g] for name, t in k.ahead.items()}
    m = k.half
    filled = 0

    def fill(n):
        nonlocal filled
        n = min(n, 6 * KT - filled)
        if n:
            dense_part(k, pe, *tile, "blk_done", filled, filled + n)
        filled += n

    def free(name):
        u.wait(pe, *TAKEN_BY[PRODUCTS.names[PRODUCTS.names.index(name) - BANKS]])

    def each_chunk(name, lhs, rhs):
        fill(1)
        for c in range(NC):
            mm = both(k, bank(k, name)[:, c * CH:(c + 1) * CH], lhs[:, c, :], rhs[:, c, :])
        mm.then_inc(product, 1)

    def turned(name, lhs):
        ident = const(k, "pair_ident")
        fill(1)
        for c in range(NC):
            mm = both(k, bank(k, name)[:, c * CH:(c + 1) * CH], lhs[:, c, :], ident)
        mm.then_inc(product, 1)

    u.wait(pe, AHEAD, "rk")
    k.nc.tensor.matmul(bank(k, "rk"), const(k, "headsum"), flat(made["rkv"]), start=True, stop=True).then_inc(product, 1)
    if before is not None:
        before.wait(pe, VALUES, f"s{NC - 1}")
    each_chunk("lt", made["bq"], made["kkp"])
    each_chunk("l", made["kkp"], made["bq"])
    if before is not None:
        rw_result_pe(k, pe, before, "mean")
    free("ak_t")
    each_chunk("ak_t", made["kq"], made["kkp"])
    free("rb_t")
    each_chunk("rb_t", made["bq"], made["rp"])
    free("rk_t")
    each_chunk("rk_t", made["kq"], made["rp"])
    free("kkp_tm")
    turned("kkp_tm", made["kkp"])
    free("v_tm")
    fill(1)
    for c in range(NC):
        t = slice(u.g * HALF + c * CH, u.g * HALF + (c + 1) * CH)
        mm = both(k, bank(k, "v_tm")[:, c * CH:(c + 1) * CH], k.rw_v[:, t], const(k, "pair_ident"))
    mm.then_inc(product, 1)
    if before is not None:
        rw_result_pe(k, pe, before, "var")
    free("akv")
    u.wait(pe, COPIES, "v_tm")
    each_chunk("akv", m["akt"], m["v_tm"])
    free("be_tm")
    turned("be_tm", made["be"])
    free("ke_tm")
    turned("ke_tm", made["ke"])
    for l in LEVEL_STEPS:
        free(f"t{l}")
        u.wait(pe, VALUES, "x0" if l == 1 else f"x{l - 1}")
        each_chunk(f"t{l}", m["lt"], m["xm"])
        fill(1)
        u.wait(pe, VALUES, f"t{l}")
        if l < LEVELS:
            free(f"x{l}")
            each_chunk(f"x{l}", m["xt"], m["t1"])
        free(f"xt{l}")
        each_chunk(f"xt{l}", m["t1"], m["xt"])
    free("u0")
    u.wait(pe, VALUES, f"xt{LEVELS}")
    u.wait(pe, COPIES, "akv")
    each_chunk("u0", m["xt"], m["akv"])
    free("w1_t")
    each_chunk("w1_t", m["kkp_tm"], m["xt"])
    u.wait(pe, COPIES, "w1_t")
    for c in range(NC):
        at = slice(c % 2 * HD, (c % 2 + 1) * HD)
        u.wait(pe, VALUES, f"s{c - 1}" if c else "s_in")
        fill(1)
        both(k, k.aps[:, 0, at], m["w1_t"][:, c, :], m["s"][:, c, :]).then_inc(product, 1)
        both(k, k.aps[:, 1, at], m["ke_tm"][:, c, :], m["v_tm"][:, c, :], stop=False)
        u.wait(pe, VALUES, f"u{c}")
        fill(1)
        both(k, k.aps[:, 1, at], m["be_tm"][:, c, :], m["u"][:, c, :], start=False).then_inc(product, 1)
    if before is not None:
        before.wait(pe, Y_COPIES, "std")
    fill(1)
    for c in range(NC):
        t = slice(c * CH, (c + 1) * CH)
        both(k, k.aps[:, 3, t], m["s"][:, c, :], made["rp"][:, c, :], stop=False)
        both(k, k.aps[:, 3, t], m["v_tm"][:, c, :], m["arkt"][:, c, :], start=False, stop=False)
        mm = both(k, k.aps[:, 3, t], m["u"][:, c, :], m["arbt"][:, c, :], start=False)
    mm.then_inc(k.sem("rw_y_product"), 1)
    fill(6 * KT)


def rw_result_pe(k, pe, u, name):
    src, wait = {"mean": (flat(k.half["y"]), (Y_COPIES, "y")), "var": (k.rw_out[:, u.g, :], (Y_COPIES, "sq"))}[name]
    u.wait(pe, *wait)
    k.nc.tensor.matmul(k.aps[:, 3, :], const(k, "headsum"), src, start=True, stop=True).then_inc(k.sem("rw_y_product"), 1)


def rw_dve(k, dve):
    v = k.nc.vector
    dve.wait_ge(k.sem("yb_spilled"), 16)
    for n in range(3):
        zeroed = v.memset(k.rw_pad[n][:, 0:1], 0.0)
    zeroed.then_inc(k.sem("rw_zeroed"), 1)
    dve.wait_ge(k.sem("rw_zeroed"), 1)
    dve.wait_ge(k.sem("blk_done"), BLK["rwkv"] + 2)
    v.tensor_tensor(k.rw_r, k.dps[:, 0, :], k.inv[:, :], ALU.mult).then_inc(k.sem("pair0_out"), 1)
    dve.wait_ge(k.sem("pair0_out"), RW_USE0 + 2)
    rw_shift(k, dve, 1, k.rw_r, k.rw_pad[0], k.rw_wdad[:, :], vec(k, "mu", 12))
    rw_pair_dve(k, dve, 0, None)
    with dve.Fori(1, PAIRS) as i:
        rw_pair_dve(k, dve, i, Half(k, i - 1, 1))
    for step in Y_VALUES.names + ["gated"]:
        rw_result_dve(k, dve, Half(k, PAIRS - 1, 1), step)


def rw_shift(k, dve, n, seq, pad, out, mu):
    v = k.nc.vector
    v.tensor_tensor(k.rw_d[:, :], pad[:, 0:S], seq, ALU.subtract).then_inc(k.sem("rw_diff_done"), 1)
    dve.wait_ge(k.sem("rw_diff_done"), n)
    v.scalar_tensor_tensor(out, k.rw_d[:, :], mu, seq, ALU.mult, ALU.add).then_inc(k.sem("rw_mix_done"), 1)
    dve.wait_ge(k.sem("rw_mix_done"), n)


def rw_pair_dve(k, dve, i, before):
    v = k.nc.vector
    blk, use = i * 4 + (BLK["rwkv"] + 2), (i * 3 + (RW_USE0 + 1), i * 3 + RW_USE1)

    def take(n, seq, pair, nth):
        dve.wait_ge(k.sem("blk_done"), blk + (n + 1))
        v.tensor_tensor(seq, k.dps[:, pair, :], k.inv[:, :], ALU.mult).then_inc(k.sem(f"pair{pair}_out"), 1)
        dve.wait_ge(k.sem(f"pair{pair}_out"), use[pair] + (nth + 2))

    if before is not None:
        before.wait(dve, VALUES, f"s{NC - 1}")
    v.memset(k.rw_s[:, :], 0.0).then_inc(k.sem("rw_s_zero"), 1)
    take(0, k.rw_r, 0, 0)
    take(1, k.rw_k, 1, 0)
    rw_shift(k, dve, i * 3 + 2, k.rw_k, k.rw_pad[1], k.rw_k, vec(k, "mu", i + 4))
    v.tensor_scalar(k.rw_kk[:, :], k.rw_k, vec(k, "k_k", i), None, ALU.mult).then_inc(k.sem("rw_kk_done"), 1)
    rw_shift(k, dve, i * 3 + 3, k.rw_r, k.rw_pad[0], k.rw_r, vec(k, "mu", i))
    dve.wait_ge(k.sem("pair0_out"), use[0] + 3)
    for h in range(2):
        t = slice(h * HALF, (h + 1) * HALF)
        v.tensor_tensor_scan(k.rw_l[:, t], const(k, "reset"), k.rw_sg[:, t], 0.0, ALU.mult, ALU.add).then_inc(k.sem("rw_l_done"), 1)
    dve.wait_ge(k.sem("rw_l_done"), i * 2 + 2)
    v.tensor_tensor(k.rw_sg[:, :], k.rw_l[:, :], k.rw_sg[:, :], ALU.subtract).then_inc(k.sem("rw_lp_done"), 1)
    dve.wait_ge(k.sem("rw_kk_root_done"), i + 1)
    dve.wait_ge(k.sem("pair1_out"), use[1] + 3)
    v.tensor_scalar(k.rw_e[:, :], k.rw_b[:, :], -1.0, vec(k, "k_a", i), ALU.add, ALU.mult).then_inc(k.sem("rw_rate_done"), 1)
    steps = (lambda: v.tensor_scalar(k.rw_d[:, :], k.rw_d[:, :], 1e-12, None, ALU.max),
             lambda: v.reciprocal(k.rw_d[:, :], k.rw_d[:, :]),
             lambda: v.tensor_tensor(k.rw_kk[:, :], k.rw_kk[:, :], k.rw_d[:, :], ALU.mult),
             lambda: v.tensor_tensor(k.rw_b[:, :], k.rw_b[:, :], k.rw_kk[:, :], ALU.mult))
    for n, step in enumerate(steps):
        step().then_inc(k.sem("rw_unit_done"), 1)
        dve.wait_ge(k.sem("rw_unit_done"), i * 4 + (n + 1))
    dve.wait_ge(k.sem("rw_rate_done"), i + 1)
    v.scalar_tensor_tensor(k.rw_k, k.rw_e[:, :], 1.0, k.rw_k, ALU.add, ALU.mult).then_inc(k.sem("rw_in_done"), 1)
    dve.wait_ge(k.sem("rw_in_done"), i + 1)
    dve.wait_ge(k.sem("rw_s_zero"), i + 1)
    first, last = Half(k, i, 0), Half(k, i, 1)
    rw_ahead_dve(k, dve, first, range(0, 8))
    take(2, k.rw_v, 0, 2)
    rw_shift(k, dve, i * 3 + 4, k.rw_v, k.rw_pad[2], k.rw_v, vec(k, "mu", i + 8))
    rw_half_dve(k, dve, first, before)
    take(3, k.rw_z[:, :], 1, 2)
    rw_ahead_dve(k, dve, last, range(0, 5))
    rw_chunks_dve(k, dve, first)
    rw_ahead_dve(k, dve, last, range(5, 8))
    rw_half_dve(k, dve, last, first)
    rw_chunks_dve(k, dve, last)


def rw_ahead_dve(k, dve, u, steps):
    v = k.nc.vector
    ts = u.tokens
    p, pp, q = k.rw_t
    l_half = chunks(k.rw_l[:, ts])
    out = {name: flat(t[u.g]) for name, t in k.ahead.items()}
    mul = lambda name, x, y: v.tensor_tensor(out[name], x, y, ALU.mult)
    for n in steps:
        name = AHEAD.names[n]
        if name == "rp":
            u.wait(dve, EXPS, "p")
            ins = mul("rp", k.rw_r[:, ts], p[:, :])
        elif name == "kkp":
            u.wait(dve, EXPS, "pp")
            ins = mul("kkp", k.rw_kk[:, ts], pp[:, :])
        elif name == "bq":
            u.wait(dve, EXPS, "q")
            ins = mul("bq", k.rw_b[:, ts], q[:, :])
        elif name == "kq":
            ins = mul("kq", k.rw_k[:, ts], q[:, :])
        elif name == "l_rel":
            u.wait(dve, AHEAD, "rp")
            ins = v.tensor_tensor(chunks(p[:, :]), l_half, l_half[:, :, CH - 1:CH].to_broadcast([P, NC, CH]), ALU.subtract)
        elif name == "be":
            u.wait(dve, EXPS, "e")
            ins = mul("be", k.rw_b[:, ts], p[:, :])
        elif name == "ke":
            ins = mul("ke", k.rw_k[:, ts], p[:, :])
        else:
            ins = v.scalar_tensor_tensor(out["rkv"], k.rw_r[:, ts], vec(k, "r_k", u.i), k.rw_k[:, ts], ALU.mult, ALU.mult)
        ins.then_inc(k.sem("rw_ahead"), 1)


def rw_half_dve(k, dve, u, before):
    v = k.nc.vector
    made = k.sem("rw_value")
    m = k.half
    taken = lambda name: chunks(bank(k, name))
    rest = iter(Y_VALUES.names + ["gated"])

    def result_step():
        if before is not None:
            step = next(rest, None)
            if step:
                rw_result_dve(k, dve, before, step)

    def mask(out, name, which):
        return v.tensor_tensor(m[out][:, :, :], taken(name), masked(k, which), ALU.mult)

    u.wait(dve, PRODUCTS, "rk")
    rkv = flat(k.ahead["rkv"][u.g])
    v.tensor_tensor(rkv, bank(k, "rk"), k.rw_v[:, u.tokens], ALU.mult).then_inc(made, 1)
    u.wait(dve, PRODUCTS, "lt")
    mask("lt", "lt", "strict_t").then_inc(made, 1)
    for first, which, out, part in (("lt", "lev0_t", "xt", "xt_part"), ("l", "lev0", "xm", "x_part")):
        u.wait(dve, PRODUCTS, first)
        mask(out, first, which).then_inc(made, 1)
        u.wait(dve, VALUES, part)
        v.tensor_tensor(m[out][:, :, :], masked(k, "pair_ident"), m[out][:, :, :], ALU.subtract).then_inc(made, 1)
    result_step()
    for name, out, which in (("ak_t", "akt", "strict_t"), ("rb_t", "arbt", "incl_t"), ("rk_t", "arkt", "incl_t")):
        u.wait(dve, PRODUCTS, name)
        mask(out, name, which).then_inc(made, 1)
    for l in LEVEL_STEPS:
        u.wait(dve, PRODUCTS, f"t{l}")
        mask("t1", f"t{l}", f"lev{l}").then_inc(made, 1)
        for n, out in (("x", "xm"), ("xt", "xt")):
            if (n, l) != ("x", LEVELS):
                u.wait(dve, PRODUCTS, f"{n}{l}")
                v.tensor_tensor(m[out][:, :, :], m[out][:, :, :], taken(f"{n}{l}"), ALU.subtract).then_inc(made, 1)
        result_step()


def rw_chunks_dve(k, dve, u):
    v = k.nc.vector
    made = k.sem("rw_value")
    m = k.half
    v.tensor_copy(m["s"][:, 0, :], k.rw_s[:, :]).then_inc(made, 1)
    u.wait(dve, VALUES, "s_in")
    u.wait(dve, COPIES, "u0")
    for c in range(NC):
        at = slice(c % 2 * HD, (c % 2 + 1) * HD)
        u.wait(dve, PRODUCTS, f"w1s{c}")
        v.scalar_tensor_tensor(m["u"][:, c, :], k.aps[:, 0, at], -1.0, m["u0"][:, c, :], ALU.mult, ALU.subtract).then_inc(made, 1)
        u.wait(dve, PRODUCTS, f"ds{c}")
        if c:
            u.wait(dve, VALUES, f"s{c - 1}")
        pc = k.rw_pc[:, u.g * NC + c:u.g * NC + c + 1]
        out = m["s"][:, c + 1, :] if c < NC - 1 else k.rw_s[:, :]
        v.scalar_tensor_tensor(out, m["s"][:, c, :], pc, k.aps[:, 1, at], ALU.mult, ALU.add).then_inc(made, 1)


def rw_result_dve(k, dve, u, step):
    v = k.nc.vector
    made = k.sem("rw_y_value")
    y = k.rw_centred
    if step == "centred":
        u.wait(dve, Y_PRODUCTS, "mean")
        v.scalar_tensor_tensor(y[:, :], k.aps[:, 3, :], -1.0 / HD, flat(k.half["y"]), ALU.mult, ALU.add).then_inc(made, 1)
    elif step == "rstd":
        u.wait(dve, Y_COPIES, "std")
        v.reciprocal(k.rw_rstd[:, :], k.rw_rstd[:, :]).then_inc(made, 1)
    elif step == "normed":
        u.wait(dve, Y_VALUES, "rstd")
        v.tensor_tensor(y[:, :], y[:, :], k.rw_rstd[:, :], ALU.mult).then_inc(made, 1)
    elif step == "gained":
        u.wait(dve, Y_VALUES, "normed")
        v.tensor_scalar(y[:, :], y[:, :], vec(k, "gn_gain", u.i), vec(k, "gn_bias", u.i), ALU.mult, ALU.add).then_inc(made, 1)
    elif step == "summed":
        u.wait(dve, Y_VALUES, "gained")
        v.tensor_tensor(y[:, :], y[:, :], flat(k.ahead["rkv"][u.g]), ALU.add).then_inc(made, 1)
    else:
        u.wait(dve, Y_VALUES, "summed")
        dve.wait_ge(k.sem("rw_silu_done"), u.i + 1)
        v.tensor_tensor(k.rw_out[:, u.g, :], y[:, :], k.rw_z[:, u.tokens], ALU.mult).then_inc(k.sem("rw_gated"), 1)
        dve.wait_ge(k.sem("rw_gated"), u.i * 2 + (u.g + 1))


def rw_act(k, act, w_up, branches):
    a = k.nc.scalar
    act.wait_ge(k.sem("pair0_out"), RW_USE0 + 1)
    act.dma_start(branches[:, 4:8, :], k.mla_out[:, :, :]).then_inc(k.sem("yb_spilled"), 16)
    act.wait_ge(k.sem("rw_mix_done"), 1)
    a.activation(k.rw_wdad[0:HD, :], k.rw_wdad[0:HD, :], ACT.Tanh).then_inc(k.sem("rw_tanh_done"), 1)
    rw_pair_act(k, act, 0, None, w_up, branches)
    with act.Fori(1, PAIRS) as i:
        rw_pair_act(k, act, i, Half(k, i - 1, 1), w_up, branches)
    last = Half(k, PAIRS - 1, 1)
    for step in ("sq", "std"):
        rw_result_act(k, act, last, step)
    rw_spill(k, act, last, branches)


def rw_pair_act(k, act, i, before, w_up, branches):
    a = k.nc.scalar
    use0, use1 = i * 3 + (RW_USE0 + 1), i * 3 + RW_USE1
    act.dma_start(k.rw_up[:, :], w_up[bass.ds(i, 1)].rearrange("a p n -> p (a n)")).then_inc(k.sem("rw_up_loaded"), 16)
    act.wait_ge(k.sem("rw_kk_done"), i + 1)
    a.activation(k.rw_e[:, :], k.rw_kk[:, :], ACT.Square).then_inc(k.sem("rw_kk_sq_done"), 1)
    act.wait_ge(k.sem("rw_w_done"), i + 1)
    fixed_wait(k, act)
    a.activation(k.rw_sg[:, :], k.dps[:, 0, :], ACT.Sigmoid, bias=vec(k, "w0", i)).then_inc(k.sem("pair0_out"), 1)
    act.wait_ge(k.sem("rw_a_done"), i + 1)
    fixed_wait(k, act)
    a.activation(k.rw_b[:, :], k.dps[:, 1, :], ACT.Sigmoid, bias=vec(k, "a0", i)).then_inc(k.sem("pair1_out"), 1)
    act.wait_ge(k.sem("rw_kk_norm_done"), i + 1)
    act.wait_ge(k.sem("rw_mix_done"), i * 3 + 3)
    a.activation(k.rw_d[:, :], k.aps[:, 0:2, :].rearrange("p a b -> p (a b)"), ACT.Sqrt).then_inc(k.sem("rw_kk_root_done"), 1)
    act.wait_ge(k.sem("rw_l_done"), i * 2 + 2)
    a.activation(k.rw_pc[:, :], k.rw_l[:, :].rearrange("p (c t) -> p c t", t=CH)[:, :, CH - 1:CH].rearrange("p c t -> p (c t)"),
                 ACT.Exp, scale=-DECAY).then_inc(k.sem("rw_pc_done"), 1)
    act.wait_ge(k.sem("rw_in_done"), i + 1)
    first, last = Half(k, i, 0), Half(k, i, 1)
    rw_exps_act(k, act, first)
    rw_e_act(k, act, first)
    rw_half_act(k, act, first, before, last, branches)
    rw_half_act(k, act, last, first, None, branches)


def rw_spill(k, act, u, branches):
    act.wait_ge(k.sem("rw_gated"), u.i * 2 + (u.g + 1))
    act.dma_start(branches[:, bass.ds(u.i, 1), u.tokens].rearrange("p a t -> p (a t)"), k.rw_out[:, u.g, :]).then_inc(k.sem(f"rw_spilled{u.g}"), 16)


def rw_exps_act(k, act, u):
    a = k.nc.scalar
    for n, (src, sign) in enumerate(((k.rw_l, -1), (k.rw_sg, -1), (k.rw_l, 1))):
        a.activation(k.rw_t[n][:, :], src[:, u.tokens], ACT.Exp, scale=sign * DECAY).then_inc(k.sem("rw_exps"), 1)


def rw_e_act(k, act, u):
    u.wait(act, AHEAD, "l_rel")
    k.nc.scalar.activation(k.rw_t[0][:, :], k.rw_t[0][:, :], ACT.Exp, scale=DECAY).then_inc(k.sem("rw_exps"), 1)


def rw_half_act(k, act, u, before, after, branches):
    a = k.nc.scalar
    m = k.half

    def copy(name):
        u.wait(act, PRODUCTS, name)
        a.activation(flat(m[name]), bank(k, name), ACT.Copy).then_inc(k.sem("rw_copy"), 1)

    copy("kkp_tm")
    if before is not None:
        rw_result_act(k, act, before, "sq")
    copy("v_tm")
    if before is not None:
        rw_result_act(k, act, before, "std")
    copy("akv")
    copy("be_tm")
    copy("ke_tm")
    if after is not None:
        u.wait(act, AHEAD, "ke")
        rw_exps_act(k, act, after)
    copy("u0")
    copy("w1_t")
    if before is not None:
        rw_spill(k, act, before, branches)
    if after is not None:
        act.wait_ge(k.sem("pair1_out"), u.i * 3 + (RW_USE1 + 4))
        a.activation(k.rw_z[:, :], k.rw_z[:, :], ACT.Silu).then_inc(k.sem("rw_silu_done"), 1)
        rw_e_act(k, act, after)
    rw_result_act(k, act, u, "y")


def rw_result_act(k, act, u, step):
    a = k.nc.scalar
    done = k.sem("rw_y_copy")
    if step == "y":
        u.wait(act, Y_PRODUCTS, "y")
        a.activation(flat(k.half["y"]), k.aps[:, 3, :], ACT.Copy).then_inc(done, 1)
    elif step == "sq":
        u.wait(act, Y_VALUES, "centred")
        act.wait_ge(k.sem(f"rw_spilled{u.g}"), u.i * 16 + 16)
        a.activation(k.rw_out[:, u.g, :], k.rw_centred[:, :], ACT.Square).then_inc(done, 1)
    else:
        u.wait(act, Y_PRODUCTS, "var")
        a.activation(k.rw_rstd[:, :], k.aps[:, 3, :], ACT.Sqrt, bias=GN_EPS, scale=1.0 / HD).then_inc(done, 1)


MERGE2_USE = (RW_USE0 + 1 + 3 * PAIRS, RW_USE1 + 3 * PAIRS)
OUT2_USE = tuple(n + 2 * KT for n in MERGE2_USE)


def reload_act(k, act, branches):
    for g in range(2):
        act.wait_ge(k.sem(f"rw_spilled{g}"), PAIRS * 16 + 16)
    for q in range(4):
        act.dma_start(k.branches[:, 2 * q:2 * q + 2, :], branches[:, 2 * q:2 * q + 2, :]).then_inc(k.sem(f"branch_loaded{q}"), 16)
    for n in range(8):
        act.wait_ge(k.sem(f"branch_loaded{n // 2}"), 16)
        hi = (k.ya_hi, k.yb_hi)[n // 4]
        k.nc.scalar.activation(hi[:, n % 4, :], k.branches[:, n, :], ACT.Copy).then_inc(k.sem("branch_hi_done"), 1)


def reload_dve(k, dve):
    for n in range(8):
        dve.wait_ge(k.sem("branch_hi_done"), n + 1)
        hi, lo = ((k.ya_hi, k.ya_lo), (k.yb_hi, k.yb_lo))[n // 4]
        k.nc.vector.tensor_tensor(lo[:, n % 4, :], k.branches[:, n, :], hi[:, n % 4, :].bitcast(F32),
                                  ALU.subtract).then_inc(k.sem("branch_lo_done"), 1)


def out2_pe(k, pe):
    with pe.Fori(0, KT // 2) as i:
        for j in range(2):
            dense(k, pe, i * 2 + (BLK["out2"] + j), j, 0, rows(k.h_hi), rows(k.h_lo), KT, j, i + OUT2_USE[j], "blk_done",
                  ready=("h_lo_done", 5 * KT) if j == 0 else None)
    stat(k, pe, 5)


def out2_act(k, act, x1_t):
    act.wait_ge(k.sem("blk_done"), BLK["out2"])
    act.dma_start(k.x1_again[:, :, :], x1_t).then_inc(k.sem("x1_again_loaded"), 16)
    merged_split_act(k, act, BLK["out2"], 1)
    with act.Fori(0, KT // 2) as i:
        for j in range(2):
            act.wait_ge(k.sem(f"pair{j}_out"), i + (OUT2_USE[j] + 2))
            square_act(k, act, 5, i * 2 + j, k.sq[j][:, :])
    inv_act(k, act, 5)


def out2_dve(k, dve):
    v = k.nc.vector
    sumsq_begin(k, dve, 5)
    with dve.Fori(0, KT // 2) as i:
        for j in range(2):
            n = i * 2 + j
            dve.wait_ge(k.sem("blk_done"), i * 2 + (BLK["out2"] + j + 1))
            v.tensor_copy(one(k.x, n), k.dps[:, j, :]).then_inc(k.sem(f"pair{j}_out"), 1)
            sumsq_dve(k, dve, 5, n, k.sq[j][:, :])
    inv_dve(k, dve, 5)
    dve.wait_ge(k.sem("x1_again_loaded"), 16)
    for n in range(KT):
        v.scalar_tensor_tensor(k.x[:, n, :], k.x[:, n, :], vec(k, "g_post", n), k.inv[:, :], ALU.mult,
                               ALU.mult).then_inc(k.sem("post_done"), 1)
        dve.wait_ge(k.sem("post_done"), n + 1)
        v.tensor_tensor(k.x1_again[:, n, :], k.x1_again[:, n, :], k.x[:, n, :], ALU.add).then_inc(k.sem("result_done"), 1)


def store_sync(k, sp, out):
    for n in range(KT):
        sp.wait_ge(k.sem("result_done"), n + 1)
        sp.dma_start(out[:, n, :], k.x1_again[:, n, :]).then_inc(k.sem("stored"), 16)
    sp.wait_ge(k.sem("stored"), KT * 16)


def stream_sync(k, sp, w_stream, n_blk):
    for s in range(2):
        sp.dma_start(k.w_raw[:, s], w_stream[s]).then_inc(k.sem(f"w_loaded{s}"), 16)
    with sp.Fori(1, n_blk // 2) as i:
        for s in range(2):
            sp.wait_ge(k.sem("w_split"), i * 2 + (s - 1))
            sp.dma_start(k.w_raw[:, s], w_stream[bass.ds(i * 2 + s, 1)].rearrange("a p k n -> p (a k) n")).then_inc(k.sem(f"w_loaded{s}"), 16)


def stream_pool(k, pool, n_blk):
    g = k.nc.gpsimd
    g.memset(k.one[:, :], 1.0).then_inc(k.sem("one_done"), 1)
    pool.wait_ge(k.sem("one_done"), 1)
    ones = k.one[:, 0:1].to_broadcast([P, SUB * P]).rearrange("p (a b) -> p a b", a=SUB)

    def split(i, s, first):
        pool.wait_ge(k.sem(f"w_loaded{s}"), i * 16 + 16)
        if not first:
            pool.wait_ge(k.sem("blk_done"), i * 2 + (s - 1))
        g.tensor_tensor(k.w_hi[:, s], k.w_raw[:, s], ones, ALU.mult).then_inc(k.sem("w_hi_done"), 1)
        pool.wait_ge(k.sem("w_hi_done"), i * 2 + (s + 1))
        g.tensor_tensor(k.w_lo[:, s], k.w_raw[:, s], k.w_hi[:, s].bitcast(F32), ALU.subtract).then_inc(k.sem("w_split"), 1)

    for s in range(2):
        split(0, s, True)
    with pool.Fori(1, n_blk // 2) as i:
        for s in range(2):
            split(i, s, False)


def program(nc, ctx, t, n_blk, out):
    k = layout(nc, ctx)
    block = ctx.enter_context(nc.Block())

    @block.sync
    def _(sp):
        sp.dma_start(k.vec[:, :], t["vec"]).then_inc(k.sem("vec_loaded"), 16)
        sp.dma_start(k.const[:, :], t["const"]).then_inc(k.sem("const_loaded"), 16)
        stream_sync(k, sp, t["w_stream"], n_blk)
        store_sync(k, sp, out)

    @block.gpsimd
    def _(pool):
        stream_pool(k, pool, n_blk)

    @block.tensor
    def _(pe):
        pe.wait_ge(k.sem("const_loaded"), 16)
        pool_pe(k, pe)
        sb_pe(k, pe)
        merge_pe(k, pe, BLK["merge"], (TILE["merge"] // 2,) * 2)
        out_pe(k, pe)
        ffn_pe(k, pe)
        ple_pe(k, pe)
        latent_pe(k, pe)
        mla_pe(k, pe)
        rw_pe(k, pe)
        merge_pe(k, pe, BLK["merge2"], MERGE2_USE, ("branch_lo_done", 8))
        out2_pe(k, pe)

    @block.scalar
    def _(act):
        entry_act(k, act, t["x_t"])
        pool_act(k, act)
        sb_act(k, act)
        merge_act(k, act, (TILE["merge"] // 2,) * 2, None)
        out_act(k, act, t["x_t"])
        ffn_act(k, act)
        ple_act(k, act, t["p_t"])
        bridge_act(k, act, t["x1_t"], t["pos_t"])
        latent_act(k, act)
        mla_act(k, act)
        rw_act(k, act, t["w_up"], t["branches"])
        reload_act(k, act, t["branches"])
        merge_act(k, act, MERGE2_USE, "b_gate")
        out2_act(k, act, t["x1_t"])

    @block.vector
    def _(dve):
        dve.sem_inc(k.sem("pair0_out"), 1)
        dve.sem_inc(k.sem("pair1_out"), 1)
        dve.sem_inc(k.sem("sumsq_done"), 2)
        for g in range(2):
            dve.sem_inc(k.sem(f"rw_spilled{g}"), 16)
        entry_dve(k, dve)
        pool_dve(k, dve)
        sb_dve(k, dve)
        merge_dve(k, dve, BLK["merge"], (TILE["merge"] // 2,) * 2, 0)
        merged_split_dve(k, dve, 1, 0)
        out_dve(k, dve)
        ffn_dve(k, dve)
        ple_dve(k, dve)
        bridge_dve(k, dve)
        latent_dve(k, dve)
        mla_dve(k, dve)
        rw_dve(k, dve)
        reload_dve(k, dve)
        merge_dve(k, dve, BLK["merge2"], MERGE2_USE, 1)
        merged_split_dve(k, dve, 5, 1)
        out2_dve(k, dve)


def constants():
    c = np.zeros((P, N_CONST), np.float32)
    p = np.arange(P)[:, None]
    q = np.arange(P)[None, :]
    put = lambda name, a: c.__setitem__((slice(None), slice(*CONST[name])), a)
    put("ident", p == q)
    put("mean", 1.0 / D)
    put("headsum", p // HD == q // HD)
    put("neg_tri", -1.0 * (p >= q))
    put("neg_ones", -1.0)
    put("sb_mask", np.where(p >= q, NEG, 0.0))
    put("mla_mask", np.where(q > p, NEG, 0.0))
    r, f = p % HD, np.arange(HD)[None, :]
    put("pair_ident", r == f)
    put("strict_t", r < f)
    put("strict", r > f)
    put("incl_t", r <= f)
    for n in range(6):
        b = 1 << n
        put(f"lev{n}", (r // (2 * b) == f // (2 * b)) & (r // b > f // b))
    put("lev0_t", (r // 2 == f // 2) & (r < f))
    for g, w in enumerate(WINDOWS):
        a = CONST["pool_count"][0] + 16 * g
        c[:, a:a + 16] = 1.0 / np.minimum(np.arange(16) + 1, w)
    put("reset", (np.arange(HALF) % CH != 0)[None, :])
    put("rope_sum", (p >= HD) & (q >= HD) & (p % ROPE == q % ROPE))
    half = ROPE // 2
    freq = ROPE_THETA ** (-np.arange(0, ROPE, 2, dtype=np.float32) / np.float32(ROPE))
    a = CONST["rope"][0]
    c[HD:, a] = freq[np.arange(HD) % half]
    c[HD:HD + ROPE, a + 1] = 0.25
    c[HD:HD + ROPE, a + 2] = np.pi / 2
    c[HD:, a + 3] = 1.0
    c[HD + ROPE:HD + ROPE + half, a + 3] = -1.0
    return c


def tiles(w):
    return w.reshape(w.shape[0] // P, P, w.shape[1]).transpose(1, 0, 2)


def stream(i):
    blocks = []

    def put(*parts):
        b, at = np.zeros((P, SUB, P), np.float32), 0
        for a in parts:
            b[:, at:at + a.shape[1], :a.shape[2]] = a
            at += a.shape[1]
        blocks.append(b)

    col = lambda w, n: tiles(w)[:, :, n * P:(n + 1) * P]
    w_in = i["w_in"][0]
    q0, k0, v0, a0, b0 = 4, 8, 12, 16, 24
    for g in range(POOL_GROUPS):
        put(col(w_in, g))
    for g in range(PAIRS):
        put(col(w_in, q0 + g))
        put(col(w_in, k0 + g))
        put(col(w_in, v0 + g))
        put(i["w_pool"][0, g][:, None, :])
    for n in range(KT):
        put(col(w_in, a0 + n))
        put(col(w_in, b0 + n))
        put(col(i["w_branch_a"][0], n), col(i["w_branch_b"][0], n))
    for n in range(KT):
        put(col(i["w_out"][0], n))
    f = 0
    for n_f in FF_CHUNKS:
        for t in range(f, f + n_f):
            put(col(i["w_ffn_gate"][0], t))
            put(col(i["w_ffn_up"][0], t))
        for n in range(KT):
            put(col(i["w_ffn_down"][0][f * P:(f + n_f) * P], n))
        f += n_f
    for n in range(KT):
        put(col(i["w_ple_gate"][0], n))
        put(col(i["w_ple_proj"][0], n))
    w_in = i["w_in_2"]
    names = ("r", "k", "v", "wd_ad", "z_a", "c_q", "c_kv", "k_pe", "z_b", "g_a", "g_b")
    widths = (512, 512, 512, 128, 512, 256, 128, ROPE, 512, D, D)
    start = dict(zip(names, np.cumsum((0,) + widths)))
    entry = lambda name, n: tiles(w_in[:, start[name] + n * P:start[name] + (n + 1) * P])
    half = ROPE // 2
    turned = np.r_[half:ROPE, 0:half]
    k_pe = w_in[:, start["k_pe"]:start["k_pe"] + ROPE]
    put(tiles(np.concatenate([np.zeros((D, HD), np.float32), k_pe, k_pe[:, turned]], axis=1)))
    put(entry("c_kv", 0))
    put(entry("c_q", 0))
    put(entry("c_q", 1))
    w_uq = i["w_uq_2"].reshape(2 * P, 2 * PAIRS, HD + ROPE)
    w_ukv = i["w_ukv_2"].reshape(P, 2 * PAIRS, P)
    for g in range(PAIRS):
        put(entry("z_b", g))
        put(*(part for h in (2 * g, 2 * g + 1) for part in
              (tiles(np.concatenate([w_uq[:, h], w_uq[:, h, HD + turned]], axis=1)), tiles(w_ukv[:, h]))))
    put(entry("wd_ad", 0)[:, 0:4])
    put(entry("wd_ad", 0)[:, 4:8])
    for g in range(PAIRS):
        for name in ("r", "k", "v", "z_a"):
            put(entry(name, g))
    for n in range(KT):
        put(entry("g_a", n))
        put(entry("g_b", n))
        put(col(i["w_out_a_2"], n), col(i["w_out_b_2"], n))
    for n in range(KT):
        put(col(i["w_o_2"], n))
    return np.stack(blocks)


def vectors(i):
    v = np.zeros((P, N_VEC), np.float32)

    def put(name, a):
        a = a.reshape(-1, P).T
        v[:, VEC[name]:VEC[name] + a.shape[1]] = a

    for name in ("norm_mix", "norm_ffn", "norm_ple", "norm_final", "pool_scale"):
        put(name, i[name])
    for name in ("g_pre", "g_post", "b_gate", "w0", "a0", "k_k", "k_a", "r_k", "gn_gain", "gn_bias", "g_q", "g_kv"):
        put(name, i[name + "_2"])
    put("mu", i["mu_shift_2"])
    return v


def kernel(**inputs):
    import concourse.bacc as bacc
    from concourse.bass_utils import run_bass_kernel_spmd

    i = {name: np.asarray(a) for name, a in inputs.items()}
    arrays = {"x_t": np.ascontiguousarray(tiles(i["x"][0].T)), "p_t": np.ascontiguousarray(tiles(i["p"][0, 0].T)),
              "w_stream": stream(i), "vec": vectors(i), "const": constants(),
              "pos_t": np.ascontiguousarray(np.broadcast_to(i["positions_2"].astype(np.int32, copy=False), (P, S))),
              "w_up": np.ascontiguousarray(np.concatenate([i["w_decay_up_2"], i["w_iclr_up_2"]]).reshape(P, PAIRS, P).transpose(1, 0, 2))}
    nc = bacc.Bacc("TRN2", target_bir_lowering=False, num_devices=1)
    t = {name: nc.dram_tensor(name, a.shape, mybir.dt.from_np(a.dtype), kind="ExternalInput").ap() for name, a in arrays.items()}
    out = nc.dram_tensor("out_t", (P, KT, S), F32, kind="ExternalOutput").ap()
    with ExitStack() as ctx:
        t["x1_t"] = nc.dram_tensor("x1_t", (P, KT, S), F32, kind="Internal").ap()
        t["branches"] = nc.dram_tensor("branches", (P, 8, S), F32, kind="Internal").ap()
        program(nc, ctx, t, len(arrays["w_stream"]), out)
    got = run_bass_kernel_spmd(nc, [arrays], core_ids=[0]).results[0]["out_t"]
    return np.ascontiguousarray(got.transpose(1, 0, 2).reshape(D, S).T)[None]
```

```python
from contextlib import ExitStack

import numpy as np

import concourse.bass as bass
from concourse import mybir

F32 = mybir.dt.float32
F32R = mybir.dt.float32r
I32 = mybir.dt.int32
ACT = mybir.ActivationFunctionType
ALU = mybir.AluOpType
AX = mybir.AxisListType

P = 128
D = 1024
S = 1024
HALF = 512
KT = D // P
SUB = 8
NEG = -1.0e30
EPS = 1e-6

POOL_GROUPS = 4
WINDOWS = (2, 4, 8, 16)
PAIRS = 4
HD = 64
FF = 2816
FF_TILES = FF // P
FF_CHUNKS = (8, 8, 6)
assert sum(FF_CHUNKS) == FF_TILES

GN_EPS = 64e-5
DECAY = 0.6065306597
CH = 64
NC = HALF // CH
LEVELS = 5
ROPE = 32
ROPE_THETA = 10000.0
MLA_SCALE = (HD + ROPE) ** -0.5
ROUND = 1.5 * 2.0 ** 23
TWO_PI = (6.28125, 1.93500518798828125e-3, 3.0199159819e-07)
PI_BELOW = 3.1415925

CONST = {}
_at = 0
for _name, _width in (("ident", P), ("mean", P), ("headsum", P), ("neg_tri", P), ("neg_ones", P),
                      ("sb_mask", P), ("mla_mask", P), ("pair_ident", HD), ("strict_t", HD), ("strict", HD),
                      ("incl_t", HD), ("lev0", HD), ("lev0_t", HD), ("lev1", HD), ("lev2", HD), ("lev3", HD),
                      ("lev4", HD), ("lev5", HD), ("rope_sum", P), ("pool_count", 64), ("reset", HALF),
                      ("rope", 8)):
    CONST[_name] = (_at, _at + _width)
    _at += _width
N_CONST = _at

VEC = {}
_at = 0
for _name, _width in (("norm_mix", 8), ("norm_ffn", 8), ("norm_ple", 8), ("norm_final", 8), ("pool_scale", 4),
                      ("g_pre", 8), ("g_post", 8), ("b_gate", 16), ("mu", 13), ("w0", 4), ("a0", 4), ("k_k", 4),
                      ("k_a", 4), ("r_k", 4), ("gn_gain", 4), ("gn_bias", 4), ("g_q", 2), ("g_kv", 1)):
    VEC[_name] = _at
    _at += _width
N_VEC = _at

BLK = {"pool": 0}
TILE = {"pool": 0}


def _stage(name, after, blocks, tiles):
    BLK[name] = BLK[after] + blocks
    TILE[name] = TILE[after] + tiles


_stage("sb", "pool", 4, 4)
_stage("merge", "sb", 16, 16)
_stage("out", "merge", 24, 32)
_stage("ffn", "out", 8, 8)
_stage("ple", "ffn", 2 * FF_TILES + KT * len(FF_CHUNKS), 2 * FF_TILES + KT * len(FF_CHUNKS))
_stage("mla", "ple", 16, 16)
_stage("rwkv", "mla", 4 + 2 * 4, 4 + 5 * 4)
_stage("merge2", "rwkv", 2 + 4 * 8, 2 + 10 * 4)
_stage("out2", "merge2", 8, 16)
_stage("end", "out2", 8, 8)


class Core:

    def __init__(self, nc, ctx):
        self.nc, self.ctx, self.sems = nc, ctx, {}
        self.ahead, self.half = {}, {}

    def sem(self, name):
        if name not in self.sems:
            self.sems[name] = self.ctx.enter_context(self.nc.semaphore(name))
        return self.sems[name]

    def at(self, name, offset, shape, dt=F32):
        return self.nc.alloc_sbuf_tensor_at(name, [P, *shape], dt, offset=offset)


def layout(nc, ctx):
    k = Core(nc, ctx)
    kb = 1024
    W = 16512
    K = W + 24 * kb
    H = K + 10 * kb
    X = H + 64 * kb
    C = X + 32 * kb
    V = C + 64 * kb
    k.w_raw = k.at("w_raw", W, [2, SUB, P])
    k.w_hi = k.at("w_hi", W + 8 * kb, [2, SUB, P], F32R)
    k.w_lo = k.at("w_lo", W + 16 * kb, [2, SUB, P], F32R)
    k.const = k.at("const", K, [N_CONST])
    k.vec = k.at("vec", V + 12 * kb, [N_VEC])
    k.one = k.at("one", V + 12 * kb + 4 * N_VEC, [1])
    k.h_hi = k.at("h_hi", H, [KT, S], F32R)
    k.h_lo = k.at("h_lo", H + 32 * kb, [KT, S], F32R)
    k.x = k.at("x_res", X, [KT, S])
    k.inv = k.at("inv", V, [S])
    k.tmp0 = k.at("tmp0", V + 4 * kb, [S])
    k.tmp1 = k.at("tmp1", V + 8 * kb, [S])
    k.tmp = [k.tmp0, k.tmp1]
    k.sq = [k.tmp0, k.tmp1]
    k.sq_ple = [k.at(f"sq_ple{n}", C + (24 + 4 * n) * kb, [S]) for n in range(2)]
    k.sumsq = k.at("sumsq", C + 56 * kb, [S])
    k.std = k.at("std", C + 60 * kb, [S])
    k.u_pad = k.at("u_pad", X, [16 + S])
    k.win = [k.at(f"win{n}", X + (n + 1) * 4160, [16 + S]) for n in range(2)]
    k.pooled = k.at("pooled", X + 3 * 4160, [S])
    k.ya_hi = k.at("ya_hi", C, [4, S], F32R)
    k.ya_lo = k.at("ya_lo", C + 16 * kb, [4, S], F32R)
    k.yb_hi = k.at("yb_hi", C + 32 * kb, [4, S], F32R)
    k.yb_lo = k.at("yb_lo", C + 48 * kb, [4, S], F32R)
    k.sb_q = k.at("sb_q", X, [S])
    k.sb_k = k.at("sb_k", X + 4 * kb, [S])
    k.sb_v = k.at("sb_v", X + 8 * kb, [KT, P])
    k.sb_e = k.at("sb_e", X + 12 * kb, [2, HALF])
    k.sb_sp = k.at("sb_sp", X + 16 * kb, [3, HALF])
    k.sb_acc = k.at("sb_acc", X + 22 * kb, [2, 2, HALF])
    k.sb_o = k.at("sb_o", X + 30 * kb, [4, P])
    k.sb_vt = k.at("sb_vt", V + 4 * kb, [S])
    k.sb_a = k.at("sb_a", V + 8 * kb, [2, HALF])
    k.merged = k.at("merged", X, [KT, S])
    k.x_again = k.at("x_again", C, [KT, S])
    k.hid_hi = k.at("hid_hi", C, [SUB, S], F32R)
    k.hid_lo = k.at("hid_lo", C + 32 * kb, [SUB, S], F32R)
    k.p_raw = k.at("p_raw", C + 16 * kb, [2, S])
    k.p_hi = k.at("p_hi", C, [2, S], F32R)
    k.p_lo = k.at("p_lo", C + 8 * kb, [2, S], F32R)
    k.cq_hi = k.at("cq_hi", X, [2, S], F32R)
    k.cq_lo = k.at("cq_lo", X + 8 * kb, [2, S], F32R)
    k.ckv_hi = k.at("ckv_hi", X + 16 * kb, [1, S], F32R)
    k.ckv_lo = k.at("ckv_lo", X + 20 * kb, [1, S], F32R)
    k.trig = k.at("trig", X + 24 * kb, [S])
    k.inv_q = k.at("inv_q", X + 28 * kb, [S])
    k.inv_kv = k.at("inv_kv", C, [S])
    k.mla_k = k.at("mla_k", C + 4 * kb, [S])
    k.mla_q = k.at("mla_q", C + 8 * kb, [S])
    k.mla_v = k.at("mla_v", C + 12 * kb, [2, KT, HD])
    k.mla_p = k.at("mla_p", C + 16 * kb, [2, S])
    k.mla_o = k.at("mla_o", C + 24 * kb, [KT, P])
    k.mla_gate = k.at("mla_gate", C + 28 * kb, [S])
    k.mla_vt = k.at("mla_vt", V + 4 * kb, [S])
    k.mla_out = k.at("mla_out", C + 32 * kb, [4, S])
    k.mla_pt = k.at("mla_pt", V + 8 * kb, [2, HALF])
    k.latent = k.at("latent", C + 32 * kb, [3, S])
    k.latent_sq = k.at("latent_sq", C + 44 * kb, [3, S])
    k.latent_std = k.at("latent_std", C + 56 * kb, [2, S])
    k.pos = k.at("pos", V + 4 * kb, [S], I32)
    k.angle = k.at("angle", V + 8 * kb, [S])
    k.turns = k.at("turns", X + 16 * kb, [S])
    k.pe_raw = k.at("pe_raw", X + 20 * kb, [S])
    free = V + 12 * kb + 4 * N_VEC + 32
    k.mla_max = k.at("mla_max", free, [2, 2])
    k.mla_sum = k.at("mla_sum", free + 32, [2, 2, KT])
    k.rw_pad = [k.at(f"rw_{name}", X + 4128 * n, [S + 1]) for n, name in enumerate("rkv")]
    k.rw_r, k.rw_k, k.rw_v = (t[:, 1:S + 1] for t in k.rw_pad)
    at = X + 3 * 4128
    k.rw_z = k.at("rw_z", at, [S])
    k.rw_sg = k.at("rw_sg", at + 4 * kb, [S])
    k.rw_b = k.at("rw_b", at + 8 * kb, [S])
    k.rw_kk = k.at("rw_kk", at + 12 * kb, [S])
    k.rw_centred = k.at("rw_centred", at + 16 * kb, [HALF])
    k.rw_s = k.at("rw_s", at + 18 * kb, [HD])
    k.rw_pc = k.at("rw_pc", at + 18 * kb + 256, [S // CH])
    assert at + 18 * kb + 320 <= C
    k.rw_up = k.at("rw_up", K + 4 * N_CONST + 32, [P])
    k.rw_d = k.at("rw_d", V + 4 * kb, [S])
    k.rw_e = k.at("rw_e", V + 8 * kb, [S])
    k.rw_t = [k.at(f"rw_t{n}", V + (4 + 2 * n) * kb, [HALF]) for n in range(3)]
    k.gate_out = k.at("gate_out", V + 4 * kb, [S])
    k.rw_rstd = k.at("rw_rstd", V + 10 * kb, [HALF])
    k.rw_l = k.at("rw_l", C, [S])
    k.rw_wdad = k.at("rw_wdad", C + 4 * kb, [S])
    k.rw_out = k.at("rw_out", C + 8 * kb, [2, HALF])
    at = C + 12 * kb
    for name in ("rp", "kkp", "bq", "kq", "be", "ke", "rkv"):
        k.ahead[name] = [k.at(f"rw_{name}{g}", at + 2 * g * kb, [NC, HD]) for g in range(2)]
        at += 4 * kb
    for name in ("lt", "akt", "xm", "xt", "t1", "arbt", "arkt", "kkp_tm", "v_tm", "be_tm", "ke_tm", "akv"):
        k.half[name] = k.at(f"rw_{name}", at, [NC, HD])
        at += 2 * kb
    assert at <= V
    for name, room in (("w1_t", "lt"), ("u0", "xm"), ("u", "t1"), ("s", "akt"), ("y", "akv")):
        k.half[name] = k.half[room]
    k.back = [k.at(f"back{n}", at, [S]) for n, at in enumerate([X + 4 * n * kb for n in (0, 1, 2, 5, 6)] + [C, C + 4 * kb])]
    k.yb2_hi, k.yb2_lo, k.ya2_hi, k.ya2_lo = (k.at(name, H + 16 * n * kb, [PAIRS, S], F32R)
                                              for n, name in enumerate(("yb2_hi", "yb2_lo", "ya2_hi", "ya2_lo")))
    k.x1_again = k.at("x1_again", C, [KT, S])
    k.dps = nc.alloc_psum_tensor("dps", [P, 2, S], F32)
    k.aps = nc.alloc_psum_tensor("aps", [P, 4, HALF], F32)
    return k


def const(k, name, lo=0, hi=P):
    a, b = CONST[name]
    return k.const[lo:hi, a:b]


def vec(k, name, n):
    return k.vec[:, bass.ds(n + VEC[name], 1)] if not isinstance(n, int) else k.vec[:, VEC[name] + n:VEC[name] + n + 1]


def one(t, n):
    return t[:, n, :] if isinstance(n, int) else t[:, bass.ds(n, 1), :].rearrange("p a t -> p (a t)")


def dense(k, pe, blk, slot, sub, rhs_hi, rhs_lo, n_k, pair, use, done, rows=P, ready=None,
          first=True, last=True):
    pe.wait_ge(k.sem("w_split"), blk + 1)
    if first:
        pe.wait_ge(k.sem(f"pair{pair}_out"), use + 1)
    for t in range(n_k):
        if ready is not None:
            pe.wait_ge(k.sem(ready[0]), ready[1] + t + 1)
        for n, (w, x) in enumerate(((k.w_hi, rhs_hi), (k.w_hi, rhs_lo), (k.w_lo, rhs_hi))):
            for h in range(2):
                mm = k.nc.tensor.matmul(k.dps[0:rows, pair, h * HALF:(h + 1) * HALF], w[:, slot, sub + t, 0:rows],
                                        x(t)[:, h * HALF:(h + 1) * HALF],
                                        start=first and t == 0 and n == 0, stop=last and t == n_k - 1 and n == 2)
    if done is not None:
        mm.then_inc(k.sem(done), 1)


def dense_part(k, pe, blk, slot, pair, use, done, lo, hi):
    if lo == 0:
        pe.wait_ge(k.sem("w_split"), blk + 1)
        pe.wait_ge(k.sem(f"pair{pair}_out"), use + 1)
    for n in range(lo, hi):
        t, h = n // 6, n % 2
        w, x = ((k.w_hi, k.h_hi), (k.w_hi, k.h_lo), (k.w_lo, k.h_hi))[n % 6 // 2]
        mm = k.nc.tensor.matmul(k.dps[:, pair, h * HALF:(h + 1) * HALF], w[:, slot, t, :], x[:, t, h * HALF:(h + 1) * HALF],
                                start=n < 2, stop=n >= 6 * KT - 2, skip_group_check=True)
    if hi == 6 * KT:
        mm.then_inc(k.sem(done), 1)


def stat(k, pe, norm):
    pe.wait_ge(k.sem("sumsq_done"), KT * (norm + 1) + 2)
    for h in range(2):
        mm = k.nc.tensor.matmul(k.aps[:, h, :], const(k, "mean"), k.sumsq[:, h * HALF:(h + 1) * HALF],
                                start=True, stop=True)
    mm.then_inc(k.sem("stat_done"), 1)


def fixed_wait(k, act):
    act.wait_ge(k.sem("vec_loaded"), 16)


def split_act(k, act, n, gain=None, src=None):
    src = k.x if src is None else src
    scale = 1.0 if gain is None else vec(k, gain, n)
    if not isinstance(n, int):
        fixed_wait(k, act)
    k.nc.scalar.activation(one(k.h_hi, n), one(src, n), ACT.Copy, scale=scale).then_inc(k.sem("h_hi_done"), 1)


def split_dve(k, dve, fill, n, gain=None, src=None):
    src = k.x if src is None else src
    dve.wait_ge(k.sem("h_hi_done"), n + (KT * fill + 1))
    if gain is None:
        ins = k.nc.vector.tensor_tensor(one(k.h_lo, n), one(src, n), one(k.h_hi, n).bitcast(F32), ALU.subtract)
    else:
        ins = k.nc.vector.scalar_tensor_tensor(one(k.h_lo, n), one(src, n), vec(k, gain, n),
                                               one(k.h_hi, n).bitcast(F32), ALU.mult, ALU.subtract)
    ins.then_inc(k.sem("h_lo_done"), 1)


def square_wait(k, act, norm, n):
    act.wait_ge(k.sem("sumsq_done"), n + (KT * norm + 1))


def square_act(k, act, norm, n, sq, waited=False):
    if not waited:
        square_wait(k, act, norm, n)
    if not isinstance(n, int) and not waited:
        fixed_wait(k, act)
    k.nc.scalar.activation(sq, one(k.x, n), ACT.Square).then_inc(k.sem("sq_done"), 1)


def sumsq_begin(k, dve, norm):
    if norm:
        dve.wait_ge(k.sem("stat_done"), norm)
    k.nc.vector.memset(k.sumsq[:, :], 0.0).then_inc(k.sem("sumsq_zero"), 1)
    dve.wait_ge(k.sem("sumsq_zero"), norm + 1)


def sumsq_dve(k, dve, norm, n, sq):
    dve.wait_ge(k.sem("sumsq_done"), n + (KT * norm + 2))
    dve.wait_ge(k.sem("sq_done"), n + (KT * norm + 1))
    k.nc.vector.tensor_tensor(k.sumsq[:, :], k.sumsq[:, :], sq, ALU.add).then_inc(k.sem("sumsq_done"), 1)


def inv_act(k, act, norm):
    act.wait_ge(k.sem("stat_done"), norm + 1)
    k.nc.scalar.activation(k.std[:, :], k.aps[:, 0:2, :].rearrange("p a b -> p (a b)"), ACT.Sqrt,
                           bias=EPS).then_inc(k.sem("std_done"), 1)


def inv_dve(k, dve, norm):
    dve.wait_ge(k.sem("std_done"), norm + 1)
    k.nc.vector.reciprocal(k.inv[:, :], k.std[:, :]).then_inc(k.sem("inv_done"), 1)
    dve.wait_ge(k.sem("inv_done"), norm + 1)


def rows(x):
    return lambda t: x[:, t, :]


def entry_act(k, act, x_t):
    for q in range(4):
        act.dma_start(k.x[:, 2 * q:2 * q + 2, :], x_t[:, 2 * q:2 * q + 2, :]).then_inc(k.sem(f"x_loaded{q}"), 16)
    act.wait_ge(k.sem("vec_loaded"), 16)
    for n in range(KT):
        if n % 2 == 0:
            act.wait_ge(k.sem(f"x_loaded{n // 2}"), 16)
        split_act(k, act, n, "norm_mix")
        square_act(k, act, 0, n, k.sq[n % 2][:, :])
    inv_act(k, act, 0)


def entry_dve(k, dve):
    dve.wait_ge(k.sem("vec_loaded"), 16)
    sumsq_begin(k, dve, 0)
    for n in range(KT):
        split_dve(k, dve, 0, n, "norm_mix")
        sumsq_dve(k, dve, 0, n, k.sq[n % 2][:, :])
    inv_dve(k, dve, 0)


def pool_pe(k, pe):
    for g in range(POOL_GROUPS):
        dense(k, pe, BLK["pool"] + g, g % 2, 0, rows(k.h_hi), rows(k.h_lo), KT, g % 2, g // 2, "blk_done",
              ready=("h_lo_done", 0) if g == 0 else None)
        if g == 0:
            pe.wait_ge(k.sem("const_loaded"), 16)
            stat(k, pe, 0)


def pool_dve(k, dve):
    v = k.nc.vector
    dve.wait_ge(k.sem("const_loaded"), 16)
    v.memset(k.u_pad[:, 0:16], 0.0).then_inc(k.sem("u_zero"), 1)
    sums = 0
    for g, w in enumerate(WINDOWS):
        dve.wait_ge(k.sem("blk_done"), BLK["pool"] + g + 1)
        if g == 0:
            dve.wait_ge(k.sem("inv_done"), 1)
            dve.wait_ge(k.sem("u_zero"), 1)
        v.tensor_tensor(k.u_pad[:, 16:], k.dps[:, g % 2, :], k.inv[:, :], ALU.mult).then_inc(k.sem(f"pair{g % 2}_out"), 1)
        dve.wait_ge(k.sem(f"pair{g % 2}_out"), g // 2 + 2)
        src, reach, step = k.u_pad, 1, 1
        while step < w:
            dst = k.win[0] if src is not k.win[0] else k.win[1]
            v.tensor_tensor(dst[:, reach:], src[:, reach:], src[:, reach - step:16 + S - step],
                            ALU.add).then_inc(k.sem("win_done"), 1)
            sums += 1
            dve.wait_ge(k.sem("win_done"), sums)
            src, step = dst, 2 * step
            reach += step
        if g:
            dve.wait_ge(k.sem("pool_hi_done"), g)
        a = CONST["pool_count"][0] + 16 * g
        v.tensor_tensor(k.pooled[:, 0:16], src[:, 16:32], k.const[:, a:a + 16], ALU.mult).then_inc(k.sem("head_done"), 1)
        v.scalar_tensor_tensor(k.pooled[:, 16:], src[:, 32:], 1.0 / w, k.u_pad[:, 32:], ALU.mult,
                               ALU.subtract).then_inc(k.sem("body_done"), 1)
        dve.wait_ge(k.sem("head_done"), g + 1)
        v.tensor_tensor(k.pooled[:, 0:16], k.pooled[:, 0:16], k.u_pad[:, 16:32], ALU.subtract).then_inc(k.sem("pooled_done"), 1)
        dve.wait_ge(k.sem("pool_hi_done"), g + 1)
        v.tensor_tensor(k.ya_lo[:, g, :], k.pooled[:, :], k.ya_hi[:, g, :].bitcast(F32),
                        ALU.subtract).then_inc(k.sem("pool_lo_done"), 1)


def pool_act(k, act):
    for g in range(POOL_GROUPS):
        act.wait_ge(k.sem("body_done"), g + 1)
        act.wait_ge(k.sem("pooled_done"), g + 1)
        k.nc.scalar.activation(k.ya_hi[:, g, :], k.pooled[:, :], ACT.Copy).then_inc(k.sem("pool_hi_done"), 1)


UNITS = [(c, b, h) for c in range(2) for b in range(4 * c + 3, -1, -1) for h in range(2)]
N_UNITS = len(UNITS)
ACC_COUNT = [sum(1 for _, b, _ in UNITS[:u + 1] if b) for u in range(N_UNITS)]
ACCS = ACC_COUNT[-1]
CHUNK_END = [u for u, (c, b, h) in enumerate(UNITS) if b == 0 and h == 1]


def unit(u):
    c, b, h = UNITS[u]
    return c, b, h, max(0, P * b - HALF * c), 4 * c + 3 - b


SB_BANKS = 5


def sb_bank(k, u):
    n = u % SB_BANKS
    return k.aps[:, n, :] if n < 3 else k.dps[:, 0, (n - 3) * HALF:(n - 2) * HALF]


def sb_sums(k, c):
    sums, turned = k.aps[:, 3, :], k.dps[:, 1, HALF:]
    return (sums, turned) if c == 0 else (k.dps[:, 1, 0:HALF], sums)


def sb_pe(k, pe):
    mul, ident = k.nc.tensor.matmul, const(k, "ident")
    with pe.Fori(0, PAIRS) as i:
        blk, use = i * 4 + BLK["sb"], i * 2 + TILE["sb"] // 2
        dense(k, pe, blk, 0, 0, rows(k.h_hi), rows(k.h_lo), KT, 0, use, "blk_done")
        dense(k, pe, blk + 1, 1, 0, rows(k.h_hi), rows(k.h_lo), KT, 1, use, "blk_done")
        dense(k, pe, blk + 2, 0, 0, rows(k.h_hi), rows(k.h_lo), KT, 0, use + 1, "blk_done")
        pe.wait_ge(k.sem("pool_lo_done"), POOL_GROUPS)
        dense(k, pe, blk + 3, 1, 0, lambda t: one(k.ya_hi, i), lambda t: one(k.ya_lo, i), 1, 1, use + 1, "blk_done")
        pe.wait_ge(k.sem("pair0_out"), use + 3)
        for b in range(KT):
            mm = k.nc.tensor.transpose(k.aps[:, b // 4, (b % 4) * P:(b % 4 + 1) * P], k.sb_vt[:, b * P:(b + 1) * P], ident)
        mm.then_inc(k.sem("sb_vtr_done"), 1)
        pe.wait_ge(k.sem("pair1_out"), use + 2)
        pe.wait_ge(k.sem("sb_v_done"), i + 1)
        pe.wait_ge(k.sem("pair1_out"), use + 3)

        def turn(c):
            pe.wait_ge(k.sem("sb_o_done"), i * 2 + (c + 1))
            if c:
                pe.wait_ge(k.sem("sb_y_done"), i * 2 + 1)
            for t in range(4):
                mm = k.nc.tensor.transpose(sb_sums(k, c)[1][:, t * P:(t + 1) * P], k.sb_o[:, t, :], ident)
            mm.then_inc(k.sem("sb_ot_done"), 1)

        for s in range(N_UNITS + 4):
            if s < N_UNITS:
                c, b, h, lo, n = unit(s)
                head = slice(h * HD, (h + 1) * HD)
                bank = sb_bank(k, s)
                if s >= SB_BANKS:
                    pe.wait_ge(k.sem("sb_a_done"), i * N_UNITS + (s - SB_BANKS + 1))
                mm = mul(bank[:, lo:HALF], k.sb_k[head, b * P:(b + 1) * P], k.sb_q[head, c * HALF + lo:(c + 1) * HALF],
                         start=True, stop=False, skip_group_check=True)
                if b >= 4 * c:
                    mm = mul(bank[:, lo:lo + P], ident, const(k, "sb_mask"), start=False, stop=False, skip_group_check=True)
                mm.then_inc(k.sem("sb_z_done"), 1)
            if s == CHUNK_END[0] + 6:
                turn(0)
            if s >= 4:
                c, b, h, lo, n = unit(s - 4)
                pe.wait_ge(k.sem("sb_a_done"), i * N_UNITS + (s - 3))
                for t in range(lo // P, 4):
                    mm = mul(sb_sums(k, c)[0][:, t * P + h * HD:t * P + (h + 1) * HD], k.sb_a[:, (s - 4) % 2, t * P:(t + 1) * P],
                             k.sb_v[:, b, h * HD:(h + 1) * HD], start=n == 0 and h == 0 and t == lo // P, stop=b == 0,
                             skip_group_check=True)
                mm.then_inc(k.sem("sb_pv_done"), 1)
            if 2 <= s < N_UNITS + 2:
                c, b, h, lo, n = unit(s - 2)
                bank = sb_bank(k, s - 2)
                pe.wait_ge(k.sem("sb_sp_done"), i * N_UNITS + (s - 1))
                mm = mul(bank[:, lo:HALF], const(k, "neg_tri"), k.sb_sp[:, (s - 2) % 3, lo:HALF], start=False, stop=n == 0, skip_group_check=True)
                if n:
                    seen = lo + P if b >= 4 * c else lo
                    pe.wait_ge(k.sem("sb_acc_done"), i * ACCS + ACC_COUNT[s - 4])
                    mm = mul(bank[:, seen:HALF], const(k, "neg_ones"), k.sb_acc[:, h, n % 2, seen:HALF], start=False, stop=True, skip_group_check=True)
                mm.then_inc(k.sem("sb_r_done"), 1)
        turn(1)


def sb_dve(k, dve):
    v = k.nc.vector

    def result(i, c):
        dve.wait_ge(k.sem("sb_yb_hi_done"), i * 2 + (c + 1))
        v.tensor_tensor(one(k.yb_lo, i)[:, c * HALF:(c + 1) * HALF], sb_sums(k, c)[1],
                        one(k.yb_hi, i)[:, c * HALF:(c + 1) * HALF].bitcast(F32), ALU.subtract).then_inc(k.sem("sb_y_done"), 1)

    with dve.Fori(0, PAIRS) as i:
        blk, use = i * 4 + BLK["sb"], i * 2 + TILE["sb"] // 2
        dve.wait_ge(k.sem("blk_done"), blk + 1)
        v.scalar_tensor_tensor(k.sb_q[:, :], k.dps[:, 0, :], HD ** -0.5, k.inv[:, :], ALU.mult, ALU.mult).then_inc(k.sem("pair0_out"), 1)
        dve.wait_ge(k.sem("blk_done"), blk + 2)
        v.tensor_tensor(k.sb_k[:, :], k.dps[:, 1, :], k.inv[:, :], ALU.mult).then_inc(k.sem("pair1_out"), 1)
        dve.wait_ge(k.sem("blk_done"), blk + 3)
        v.tensor_tensor(k.sb_vt[:, :], k.dps[:, 0, :], k.inv[:, :], ALU.mult).then_inc(k.sem("pair0_out"), 1)
        dve.wait_ge(k.sem("sb_ya_hi_done"), i + 1)
        v.scalar_tensor_tensor(one(k.ya_lo, i), k.dps[:, 1, :], vec(k, "pool_scale", i), one(k.ya_hi, i).bitcast(F32),
                               ALU.mult, ALU.subtract).then_inc(k.sem("pair1_out"), 1)
        for u in range(N_UNITS):
            c, b, h, lo, n = unit(u)
            dve.wait_ge(k.sem("sb_ln_done"), i * N_UNITS + (u + 1))
            if u >= 3:
                dve.wait_ge(k.sem("sb_r_done"), i * N_UNITS + (u - 2))
            v.scalar_tensor_tensor(k.sb_sp[:, u % 3, lo:], sb_bank(k, u)[:, lo:HALF], 0.0, k.sb_e[:, u % 2, lo:],
                                   ALU.max, ALU.add).then_inc(k.sem("sb_sp_done"), 1)
            if b:
                dve.wait_ge(k.sem("sb_sp_done"), i * N_UNITS + (u + 1))
                if u >= 2:
                    dve.wait_ge(k.sem("sb_r_done"), i * N_UNITS + (u - 1))
                seen = lo + P if b >= 4 * c else lo
                if seen > lo:
                    last = v.tensor_copy(k.sb_acc[:, h, (n + 1) % 2, lo:seen], k.sb_sp[:, u % 3, lo:seen])
                if n:
                    dve.wait_ge(k.sem("sb_acc_done"), i * ACCS + ACC_COUNT[u - 2])
                    last = v.tensor_tensor(k.sb_acc[:, h, (n + 1) % 2, seen:], k.sb_acc[:, h, n % 2, seen:],
                                           k.sb_sp[:, u % 3, seen:], ALU.add)
                last.then_inc(k.sem("sb_acc_done"), 1)
            if u == CHUNK_END[0] + 8:
                result(i, 0)
        result(i, 1)


def sb_act(k, act):
    a = k.nc.scalar

    def take(i, c):
        act.wait_ge(k.sem("sb_pv_done"), i * N_UNITS + (CHUNK_END[c] + 1))
        a.activation(k.sb_o[:, :, :].rearrange("p a b -> p (a b)"), sb_sums(k, c)[0], ACT.Copy).then_inc(k.sem("sb_o_done"), 1)

    def upper(i, c):
        act.wait_ge(k.sem("sb_ot_done"), i * 2 + (c + 1))
        fixed_wait(k, act)
        a.activation(one(k.yb_hi, i)[:, c * HALF:(c + 1) * HALF], sb_sums(k, c)[1], ACT.Copy).then_inc(k.sem("sb_yb_hi_done"), 1)

    a.preload_act_table_set("natural_log_exp_and_others")
    with act.Fori(0, PAIRS) as i:
        act.wait_ge(k.sem("blk_done"), i * 4 + (BLK["sb"] + 4))
        fixed_wait(k, act)
        a.activation(one(k.ya_hi, i), k.dps[:, 1, :], ACT.Copy, scale=vec(k, "pool_scale", i)).then_inc(k.sem("sb_ya_hi_done"), 1)
        act.wait_ge(k.sem("sb_vtr_done"), i + 1)
        a.activation(k.sb_v[:, :, :].rearrange("p a b -> p (a b)"), k.aps[:, 0:2, :].rearrange("p a b -> p (a b)"),
                     ACT.Copy).then_inc(k.sem("sb_v_done"), 1)
        for s in range(N_UNITS + 2):
            if s < N_UNITS:
                c, b, h, lo, n = unit(s)
                e = k.sb_e[:, s % 2, lo:]
                act.wait_ge(k.sem("sb_z_done"), i * N_UNITS + (s + 1))
                if s >= 2:
                    act.wait_ge(k.sem("sb_sp_done"), i * N_UNITS + (s - 1))
                a.activation(e, sb_bank(k, s)[:, lo:HALF], ACT.Abs).then_inc(k.sem("sb_abs_done"), 1)
                act.wait_ge(k.sem("sb_abs_done"), i * N_UNITS + (s + 1))
                a.activation(e, e, ACT.Exp, scale=-1.0).then_inc(k.sem("sb_exp_done"), 1)
                act.wait_ge(k.sem("sb_exp_done"), i * N_UNITS + (s + 1))
                a.activation(e, e, ACT.Ln, bias=1.0).then_inc(k.sem("sb_ln_done"), 1)
            if s >= 2:
                u = s - 2
                c, b, h, lo, n = unit(u)
                act.wait_ge(k.sem("sb_r_done"), i * N_UNITS + (u + 1))
                if u >= 2:
                    act.wait_ge(k.sem("sb_pv_done"), i * N_UNITS + (u - 1))
                a.activation(k.sb_a[:, u % 2, lo:], sb_bank(k, u)[:, lo:HALF], ACT.Exp).then_inc(k.sem("sb_a_done"), 1)
            if s == CHUNK_END[0] + 5:
                take(i, 0)
            if s == CHUNK_END[0] + 7:
                upper(i, 0)
        take(i, 1)
        upper(i, 1)


def merge_pe(k, pe, blk0, use0, ready=None):
    def gates(i, j):
        blk, use = i * 6 + (blk0 + 3 * j), [i * 4 + (use0[g] + 2 * j) for g in range(2)]
        for g in range(2):
            dense(k, pe, blk + g, (j + g) % 2, 0, rows(k.h_hi), rows(k.h_lo), KT, g, use[g], "blk_done")

    def branches(i, j):
        blk, use = i * 6 + (blk0 + 3 * j), [i * 4 + (use0[g] + 2 * j) for g in range(2)]
        dense(k, pe, blk + 2, j, 0, rows(k.ya_hi), rows(k.ya_lo), 4, 0, use[0] + 1, "branch_a_done")
        dense(k, pe, blk + 2, j, 4, rows(k.yb_hi), rows(k.yb_lo), 4, 1, use[1] + 1, "blk_done")

    if ready is None:
        gates(0, 0)
    else:
        pe.wait_ge(k.sem(ready[0]), ready[1])
    with pe.Fori(0, KT // 2 - 1) as i:
        for j in range(2):
            branches(i, j)
            gates(i + j, 1 - j)
    branches(KT // 2 - 1, 0)
    gates(KT // 2 - 1, 1)
    branches(KT // 2 - 1, 1)


def merge_dve(k, dve, blk0, use0, call):
    v = k.nc.vector
    with dve.Fori(0, KT // 2) as i:
        for j in range(2):
            n, blk, use = i * 2 + j, i * 6 + (blk0 + 3 * j), [i * 4 + (use0[g] + 2 * j) for g in range(2)]
            for g in range(2):
                dve.wait_ge(k.sem("blk_done"), blk + (g + 1))
                v.tensor_tensor(k.tmp[g][:, :], k.dps[:, g, :], k.inv[:, :], ALU.mult).then_inc(k.sem(f"pair{g}_out"), 1)
            dve.wait_ge(k.sem("branch_a_done"), i * 2 + (KT * call + j + 1))
            dve.wait_ge(k.sem("gate_done"), i * 4 + (2 * KT * call + 2 * j + 1))
            v.tensor_tensor(one(k.merged, n), k.dps[:, 0, :], k.tmp0[:, :], ALU.mult).then_inc(k.sem("pair0_out"), 1)
            dve.wait_ge(k.sem("blk_done"), blk + 3)
            dve.wait_ge(k.sem("gate_done"), i * 4 + (2 * KT * call + 2 * j + 2))
            v.tensor_tensor(k.tmp1[:, :], k.dps[:, 1, :], k.tmp1[:, :], ALU.mult).then_inc(k.sem("pair1_out"), 1)
            dve.wait_ge(k.sem("pair0_out"), use[0] + 3)
            dve.wait_ge(k.sem("pair1_out"), use[1] + 3)
            v.tensor_tensor(one(k.merged, n), one(k.merged, n), k.tmp1[:, :], ALU.add).then_inc(k.sem("merged_done"), 1)
            dve.wait_ge(k.sem("merged_done"), i * 2 + (KT * call + j + 1))


def merge_act(k, act, use0, bias):
    with act.Fori(0, KT // 2) as i:
        for j in range(2):
            for g in range(2):
                act.wait_ge(k.sem(f"pair{g}_out"), i * 4 + (use0[g] + 2 * j + 2))
                if bias is not None:
                    fixed_wait(k, act)
                b = 0.0 if bias is None else vec(k, bias, i * 2 + (j + KT * g))
                k.nc.scalar.activation(k.tmp[g][:, :], k.tmp[g][:, :], ACT.Sigmoid, bias=b).then_inc(k.sem("gate_done"), 1)


def merged_split_act(k, act, blk_end, call):
    act.wait_ge(k.sem("blk_done"), blk_end)
    act.wait_ge(k.sem("merged_done"), KT * (call + 1))
    for n in range(KT):
        split_act(k, act, n, src=k.merged)


def merged_split_dve(k, dve, fill, call):
    dve.wait_ge(k.sem("merged_done"), KT * (call + 1))
    for n in range(KT):
        split_dve(k, dve, fill, n, src=k.merged)


def out_pe(k, pe):
    with pe.Fori(0, KT // 2) as i:
        for j in range(2):
            dense(k, pe, i * 2 + (BLK["out"] + j), j, 0, rows(k.h_hi), rows(k.h_lo), KT, j, i + TILE["out"] // 2, "blk_done",
                  ready=("h_lo_done", KT) if j == 0 else None)
    stat(k, pe, 1)


def out_dve(k, dve):
    sumsq_begin(k, dve, 1)
    dve.wait_ge(k.sem("x_again_loaded"), 16)
    with dve.Fori(0, KT // 2) as i:
        for j in range(2):
            n = i * 2 + j
            dve.wait_ge(k.sem("blk_done"), i * 2 + (BLK["out"] + j + 1))
            k.nc.vector.tensor_tensor(one(k.x, n), k.dps[:, j, :], one(k.x_again, n), ALU.add).then_inc(k.sem(f"pair{j}_out"), 1)
            sumsq_dve(k, dve, 1, n, k.sq[j][:, :])
    for n in range(KT):
        split_dve(k, dve, 2, n, "norm_ffn")
    inv_dve(k, dve, 1)


def out_act(k, act, x_t):
    act.wait_ge(k.sem("blk_done"), BLK["out"])
    act.dma_start(k.x_again[:, :, :], x_t).then_inc(k.sem("x_again_loaded"), 16)
    merged_split_act(k, act, BLK["out"], 0)
    with act.Fori(0, KT // 2) as i:
        for j in range(2):
            act.wait_ge(k.sem(f"pair{j}_out"), i + (TILE["out"] // 2 + 2))
            square_act(k, act, 1, i * 2 + j, k.sq[j][:, :])
    act.wait_ge(k.sem("blk_done"), BLK["ffn"])
    for n in range(KT):
        split_act(k, act, n, "norm_ffn")
    inv_act(k, act, 1)


def ffn_places():
    before, blk, tile = 0, BLK["ffn"], TILE["ffn"]
    for c, n in enumerate(FF_CHUNKS):
        yield c, n, before, blk, tile, blk + 2 * n, tile + 2 * n
        before, blk, tile = before + n, blk + 2 * n + KT, tile + 2 * n + KT


def ffn_pe(k, pe):
    for c, n_f, before, blk, tile, blk_d, tile_d in ffn_places():
        with pe.Fori(0, n_f) as i:
            dense(k, pe, i * 2 + blk, 0, 0, rows(k.h_hi), rows(k.h_lo), KT, 0, i + tile // 2, "blk_done",
                  ready=("h_lo_done", 2 * KT) if c == 0 else None)
            dense(k, pe, i * 2 + (blk + 1), 1, 0, rows(k.h_hi), rows(k.h_lo), KT, 1, i + tile // 2, "blk_done")
        with pe.Fori(0, KT // 2) as i:
            for j in range(2):
                dense(k, pe, i * 2 + (blk_d + j), j, 0, rows(k.hid_hi), rows(k.hid_lo), n_f, j, i + tile_d // 2, "blk_done",
                      ready=("hid_lo_done", before) if j == 0 else None)
    stat(k, pe, 2)


def ffn_dve(k, dve):
    v = k.nc.vector
    for c, n_f, before, blk, tile, blk_d, tile_d in ffn_places():
        with dve.Fori(0, n_f) as i:
            dve.wait_ge(k.sem("blk_done"), i * 2 + (blk + 1))
            v.tensor_tensor(k.tmp0[:, :], k.dps[:, 0, :], k.inv[:, :], ALU.mult).then_inc(k.sem("pair0_out"), 1)
            dve.wait_ge(k.sem("blk_done"), i * 2 + (blk + 2))
            v.tensor_tensor(k.tmp1[:, :], k.dps[:, 1, :], k.inv[:, :], ALU.mult).then_inc(k.sem("pair1_out"), 1)
            dve.wait_ge(k.sem("silu_done"), i + (before + 1))
            dve.wait_ge(k.sem("pair1_out"), i + (tile // 2 + 2))
            v.tensor_tensor(k.tmp1[:, :], k.tmp1[:, :], k.tmp0[:, :], ALU.mult).then_inc(k.sem("hid_done"), 1)
            dve.wait_ge(k.sem("hid_hi_done"), i + (before + 1))
            v.tensor_tensor(one(k.hid_lo, i), k.tmp1[:, :], one(k.hid_hi, i).bitcast(F32), ALU.subtract).then_inc(k.sem("hid_lo_done"), 1)
            dve.wait_ge(k.sem("hid_lo_done"), i + (before + 1))
        last = c == len(FF_CHUNKS) - 1
        if last:
            sumsq_begin(k, dve, 2)
        with dve.Fori(0, KT // 2) as i:
            for j in range(2):
                n = i * 2 + j
                dve.wait_ge(k.sem("blk_done"), i * 2 + (blk_d + j + 1))
                v.tensor_tensor(one(k.x, n), k.dps[:, j, :], one(k.x, n), ALU.add).then_inc(k.sem(f"pair{j}_out"), 1)
                if last:
                    split_dve(k, dve, 3, n, "norm_ple")
                    sumsq_dve(k, dve, 2, n, k.sq[j][:, :])
    inv_dve(k, dve, 2)


def ffn_act(k, act):
    a = k.nc.scalar
    for c, n_f, before, blk, tile, blk_d, tile_d in ffn_places():
        with act.Fori(0, n_f) as i:
            act.wait_ge(k.sem("pair0_out"), i + (tile // 2 + 2))
            a.activation(k.tmp0[:, :], k.tmp0[:, :], ACT.Silu).then_inc(k.sem("silu_done"), 1)
            act.wait_ge(k.sem("hid_done"), i + (before + 1))
            fixed_wait(k, act)
            a.activation(one(k.hid_hi, i), k.tmp1[:, :], ACT.Copy).then_inc(k.sem("hid_hi_done"), 1)
        if c == len(FF_CHUNKS) - 1:
            with act.Fori(0, KT // 2) as i:
                for j in range(2):
                    act.wait_ge(k.sem(f"pair{j}_out"), i + (tile_d // 2 + 2))
                    square_wait(k, act, 2, i * 2 + j)
                    split_act(k, act, i * 2 + j, "norm_ple")
                    square_act(k, act, 2, i * 2 + j, k.sq[j][:, :], waited=True)
    inv_act(k, act, 2)


def ple_pe(k, pe):
    with pe.Fori(0, KT // 2) as i:
        for j in range(2):
            blk, use = i * 4 + (BLK["ple"] + 2 * j), i * 2 + (TILE["ple"] // 2 + j)
            dense(k, pe, blk, 0, 0, rows(k.h_hi), rows(k.h_lo), KT, 0, use, "blk_done",
                  ready=("h_lo_done", 3 * KT) if j == 0 else None)
            dense(k, pe, blk + 1, 1, 0, rows(k.p_hi), rows(k.p_lo), 2, 1, use, "blk_done",
                  ready=("p_lo_done", 0) if j == 0 else None)
    stat(k, pe, 3)


def ple_dve(k, dve):
    v = k.nc.vector
    for t in range(2):
        dve.wait_ge(k.sem("p_hi_done"), t + 1)
        v.tensor_tensor(k.p_lo[:, t, :], k.p_raw[:, t, :], k.p_hi[:, t, :].bitcast(F32), ALU.subtract).then_inc(k.sem("p_lo_done"), 1)
    sumsq_begin(k, dve, 3)
    with dve.Fori(0, KT // 2) as i:
        for j in range(2):
            n, blk, use = i * 2 + j, i * 4 + (BLK["ple"] + 2 * j), i * 2 + (TILE["ple"] // 2 + j)
            dve.wait_ge(k.sem("blk_done"), blk + 1)
            v.tensor_tensor(k.tmp[j][:, :], k.dps[:, 0, :], k.inv[:, :], ALU.mult).then_inc(k.sem("pair0_out"), 1)
            dve.wait_ge(k.sem("blk_done"), blk + 2)
            dve.wait_ge(k.sem("ple_gate_done"), n + 1)
            v.tensor_tensor(k.tmp[j][:, :], k.dps[:, 1, :], k.tmp[j][:, :], ALU.mult).then_inc(k.sem("pair1_out"), 1)
            dve.wait_ge(k.sem("pair1_out"), use + 2)
            v.tensor_tensor(one(k.x, n), one(k.x, n), k.tmp[j][:, :], ALU.add).then_inc(k.sem("ple_x_done"), 1)
            sumsq_dve(k, dve, 3, n, k.sq_ple[j][:, :])
    inv_dve(k, dve, 3)


def ple_act(k, act, p_t):
    a = k.nc.scalar
    act.wait_ge(k.sem("blk_done"), BLK["ple"])
    act.dma_start(k.p_raw[:, :, :], p_t).then_inc(k.sem("p_loaded"), 16)
    act.wait_ge(k.sem("p_loaded"), 16)
    for t in range(2):
        a.activation(k.p_hi[:, t, :], k.p_raw[:, t, :], ACT.Copy).then_inc(k.sem("p_hi_done"), 1)
    with act.Fori(0, KT // 2) as i:
        for j in range(2):
            n, use = i * 2 + j, i * 2 + (TILE["ple"] // 2 + j)
            act.wait_ge(k.sem("pair0_out"), use + 2)
            a.activation(k.tmp[j][:, :], k.tmp[j][:, :], ACT.Sigmoid).then_inc(k.sem("ple_gate_done"), 1)
            act.wait_ge(k.sem("ple_x_done"), n + 1)
            square_act(k, act, 3, n, k.sq_ple[j][:, :])
    inv_act(k, act, 3)



def bridge_dve(k, dve):
    sumsq_begin(k, dve, 4)
    for n in range(KT + 1):
        if n < KT:
            k.nc.vector.scalar_tensor_tensor(k.x[:, n, :], k.x[:, n, :], vec(k, "norm_final", n), k.inv[:, :],
                                             ALU.mult, ALU.mult).then_inc(k.sem("x1_done"), 1)
        if n:
            split_dve(k, dve, 4, n - 1, "g_pre")
            sumsq_dve(k, dve, 4, n - 1, k.sq[(n - 1) % 2][:, :])
    inv_dve(k, dve, 4)


def bridge_act(k, act, x1_t, pos_t):
    for n in range(KT):
        act.wait_ge(k.sem("x1_done"), n + 1)
        split_act(k, act, n, "g_pre")
        square_act(k, act, 4, n, k.sq[n % 2][:, :])
        if n % 2:
            act.dma_start(x1_t[:, n - 1:n + 1, :], k.x[:, n - 1:n + 1, :]).then_inc(k.sem("x1_spilled"), 16)
    inv_act(k, act, 4)
    act.wait_ge(k.sem("sumsq_done"), KT * 5 + 2)
    act.dma_start(k.pos[:, :], pos_t).then_inc(k.sem("pos_loaded"), 16)


LATENT_USE = TILE["mla"] // 2


def latent_pe(k, pe):
    b = BLK["mla"]
    mul = k.nc.tensor.matmul
    dense(k, pe, b, 0, 0, rows(k.h_hi), rows(k.h_lo), KT, 0, LATENT_USE, "blk_done", ready=("h_lo_done", 4 * KT))
    stat(k, pe, 4)
    dense(k, pe, b + 1, 1, 0, rows(k.h_hi), rows(k.h_lo), KT, 1, LATENT_USE, "blk_done")
    dense(k, pe, b + 2, 0, 0, rows(k.h_hi), rows(k.h_lo), KT, 0, LATENT_USE + 1, "blk_done")
    dense(k, pe, b + 3, 1, 0, rows(k.h_hi), rows(k.h_lo), KT, 1, LATENT_USE + 1, "blk_done")
    pe.wait_ge(k.sem("pe_rot_done"), 1)
    for h in range(2):
        mm = mul(k.aps[:, h, :], const(k, "rope_sum", HD, P), k.pe_raw[HD:P, h * HALF:(h + 1) * HALF], start=True, stop=True)
    mm.then_inc(k.sem("pe_sum_done"), 1)
    pe.wait_ge(k.sem("latent_sq_done"), 1)
    for h in range(2):
        mm = mul(k.aps[:, 2 + h, :], const(k, "mean"), k.latent_sq[:, 2, h * HALF:(h + 1) * HALF], start=True, stop=True)
    mm.then_inc(k.sem("latent_stat_done"), 1)
    pe.wait_ge(k.sem("latent_sq_done"), 3)
    pe.wait_ge(k.sem("pe_key_done"), 1)
    for h in range(2):
        for n in range(2):
            mm = mul(k.aps[:, h, :], const(k, "mean"), k.latent_sq[:, n, h * HALF:(h + 1) * HALF], start=n == 0, stop=n == 1)
    mm.then_inc(k.sem("latent_stat_done"), 1)


def latent_dve(k, dve):
    v = k.nc.vector
    r = CONST["rope"][0]
    col = lambda n: k.const[:, r + n:r + n + 1]
    dve.wait_ge(k.sem("pos_loaded"), 16)
    dve.wait_ge(k.sem("x1_spilled"), 64)
    steps = (lambda: v.tensor_scalar(k.angle[:, :], k.pos[:, :], col(0), None, ALU.mult),
             lambda: v.tensor_scalar(k.turns[:, :], k.angle[:, :], 0.5 / np.pi, col(1), ALU.mult, ALU.add),
             lambda: v.tensor_scalar(k.turns[:, :], k.turns[:, :], ROUND, -ROUND, ALU.add, ALU.add),
             lambda: v.scalar_tensor_tensor(k.angle[:, :], k.turns[:, :], -TWO_PI[0], k.angle[:, :], ALU.mult, ALU.add),
             lambda: v.scalar_tensor_tensor(k.angle[:, :], k.turns[:, :], -TWO_PI[1], k.angle[:, :], ALU.mult, ALU.add),
             lambda: v.scalar_tensor_tensor(k.angle[:, :], k.turns[:, :], -TWO_PI[2], k.angle[:, :], ALU.mult, ALU.add),
             lambda: v.tensor_scalar(k.angle[:, :], k.angle[:, :], col(2), PI_BELOW, ALU.add, ALU.min),
             lambda: v.tensor_scalar(k.angle[:, :], k.angle[:, :], -PI_BELOW, None, ALU.max))
    for n, step in enumerate(steps):
        step().then_inc(k.sem("angle_done"), 1)
        dve.wait_ge(k.sem("angle_done"), n + 1)
    dve.wait_ge(k.sem("blk_done"), BLK["mla"] + 1)
    v.tensor_tensor(k.pe_raw[HD:P, :], k.dps[HD:P, 0, :], k.inv[HD:P, :], ALU.mult).then_inc(k.sem("pair0_out"), 1)
    for n, (pair, use) in enumerate(((1, LATENT_USE), (0, LATENT_USE + 1), (1, LATENT_USE + 1))):
        dve.wait_ge(k.sem("blk_done"), BLK["mla"] + n + 2)
        v.tensor_tensor(k.latent[:, (n + 2) % 3, :], k.dps[:, pair, :], k.inv[:, :], ALU.mult).then_inc(k.sem(f"pair{pair}_out"), 1)
        if n == 0:
            dve.wait_ge(k.sem("sin_done"), 1)
            v.tensor_scalar(k.trig[:, :], k.trig[:, :], col(3), None, ALU.mult).then_inc(k.sem("trig_done"), 1)
            dve.wait_ge(k.sem("trig_done"), 1)
            dve.wait_ge(k.sem("pair0_out"), LATENT_USE + 2)
            v.tensor_tensor(k.pe_raw[HD:P, :], k.pe_raw[HD:P, :], k.trig[HD:P, :], ALU.mult).then_inc(k.sem("pe_rot_done"), 1)
    dve.wait_ge(k.sem("latent_std_done"), 1)
    v.reciprocal(k.inv_kv[:, :], k.latent_std[:, 0, :]).then_inc(k.sem("latent_inv_done"), 1)
    dve.wait_ge(k.sem("latent_hi_done"), 1)
    v.scalar_tensor_tensor(k.ckv_lo[:, 0, :], k.latent[:, 2, :], vec(k, "g_kv", 0), k.ckv_hi[:, 0, :].bitcast(F32),
                           ALU.mult, ALU.subtract).then_inc(k.sem("latent_lo_done"), 1)
    for n in range(2):
        dve.wait_ge(k.sem("latent_hi_done"), n + 2)
        v.scalar_tensor_tensor(k.cq_lo[:, n, :], k.latent[:, n, :], vec(k, "g_q", n), k.cq_hi[:, n, :].bitcast(F32),
                               ALU.mult, ALU.subtract).then_inc(k.sem("latent_lo_done"), 1)
    dve.wait_ge(k.sem("latent_std_done"), 2)
    v.reciprocal(k.inv_q[:, :], k.latent_std[:, 1, :]).then_inc(k.sem("latent_inv_done"), 1)
    dve.wait_ge(k.sem("latent_inv_done"), 2)


def latent_act(k, act):
    a = k.nc.scalar
    act.wait_ge(k.sem("angle_done"), 8)
    a.activation(k.trig[:, :], k.angle[:, :], ACT.Sin).then_inc(k.sem("sin_done"), 1)
    act.wait_ge(k.sem("pair1_out"), LATENT_USE + 2)
    a.activation(k.latent_sq[:, 2, :], k.latent[:, 2, :], ACT.Square).then_inc(k.sem("latent_sq_done"), 1)
    act.wait_ge(k.sem("pe_sum_done"), 1)
    a.activation(k.mla_k[HD:P, :], k.aps[HD:P, 0:2, :].rearrange("p a b -> p (a b)"), ACT.Copy).then_inc(k.sem("pe_key_done"), 1)
    a.activation(k.ckv_hi[:, 0, :], k.latent[:, 2, :], ACT.Copy, scale=vec(k, "g_kv", 0)).then_inc(k.sem("latent_hi_done"), 1)
    for n in range(2):
        act.wait_ge(k.sem(f"pair{n}_out"), LATENT_USE + 3)
        a.activation(k.latent_sq[:, n, :], k.latent[:, n, :], ACT.Square).then_inc(k.sem("latent_sq_done"), 1)
        a.activation(k.cq_hi[:, n, :], k.latent[:, n, :], ACT.Copy, scale=vec(k, "g_q", n)).then_inc(k.sem("latent_hi_done"), 1)
    for n, (bank, width) in enumerate(((2, 128), (0, 256))):
        act.wait_ge(k.sem("latent_stat_done"), n + 1)
        a.activation(k.latent_std[:, n, :], k.aps[:, bank:bank + 2, :].rearrange("p a b -> p (a b)"), ACT.Sqrt, bias=EPS,
                     scale=D / width).then_inc(k.sem("latent_std_done"), 1)


MLA_USE0 = LATENT_USE + 2
MLA_USES = 5
MLA_USE1 = LATENT_USE + 2
GROUPS = [(b, g, min(4, b + 1 - g)) for b in range(KT) for g in range(0, b + 1, 4)]
N_GROUPS = len(GROUPS)


def mla_pe(k, pe):
    mla_queries_pe(k, pe, 0, 0)
    mla_keys_pe(k, pe, 0, 0)
    with pe.Fori(0, PAIRS - 1) as i:
        mla_pair_pe(k, pe, i, False)
    mla_pair_pe(k, pe, PAIRS - 1, True)


def mla_block(i):
    return i * 2 + (BLK["mla"] + 4)


def mla_use(i, h):
    return i * MLA_USES + (MLA_USE0 + 2 * h)


def mla_queries_pe(k, pe, i, h):
    if h == 0:
        pe.wait_ge(k.sem("latent_lo_done"), 3)
    dense(k, pe, mla_block(i), 0, 3 * h, rows(k.cq_hi), rows(k.cq_lo), 2, 0, mla_use(i, h), "mla_proj_done")


def mla_keys_pe(k, pe, i, h):
    dense(k, pe, mla_block(i), 0, 3 * h + 2, rows(k.ckv_hi), rows(k.ckv_lo), 1, 0, mla_use(i, h) + 1, "blk_done" if h else "mla_proj_done")


def mla_pair_pe(k, pe, i, end):
    mul, ident = k.nc.tensor.matmul, const(k, "ident")
    for h in range(2):
        def scores(b):
            n = i * 16 + (8 * h + b + 1)
            r = b % 2
            if b >= 2:
                pe.wait_ge(k.sem("mla_exp_done"), n - 2)
            for lo in range(0, (b + 1) * P, HALF):
                hi = min(lo + HALF, (b + 1) * P)
                mm = mul(k.aps[:, 2 * r + lo // HALF, 0:hi - lo], k.mla_q[:, b * P:(b + 1) * P], k.mla_k[:, lo:hi],
                         start=True, stop=False, skip_group_check=True)
            at = b * P % HALF
            mm = mul(k.aps[:, 2 * r + b * P // HALF, at:at + P], ident, const(k, "mla_mask"), start=False, stop=True, skip_group_check=True)
            mm.then_inc(k.sem("mla_s_done"), 1)

        def turn(g):
            b, first, n = GROUPS[g]
            c = i * 2 * N_GROUPS + (N_GROUPS * h + g)
            pe.wait_ge(k.sem("mla_exp_done"), i * 16 + (8 * h + b + 1))
            if g:
                pe.wait_ge(k.sem("mla_pt_done"), c)
            for t in range(n):
                mm = k.nc.tensor.transpose(k.dps[:, 1, t * P:(t + 1) * P], k.mla_p[:, b % 2, (first + t) * P:(first + t + 1) * P], ident)
            mm.then_inc(k.sem("mla_t_done"), 1)

        def values(g):
            b, first, n = GROUPS[g]
            pe.wait_ge(k.sem("mla_pt_done"), i * 2 * N_GROUPS + (N_GROUPS * h + g + 1))
            for t in range(n):
                mm = mul(k.dps[:, 1, HALF + b * HD:HALF + (b + 1) * HD], k.mla_pt[:, g % 2, t * P:(t + 1) * P],
                         k.mla_v[:, h, first + t, :], start=g == 0 and t == 0, stop=first + t == b, skip_group_check=True)
            mm.then_inc(k.sem("mla_pv_done"), 1)

        def ahead(step):
            if h == 0:
                step(k, pe, i, 1)
            elif not end:
                step(k, pe, i + 1, 0)

        pe.wait_ge(k.sem("pair0_out"), mla_use(i, h) + 3)
        for b in range(KT):
            mm = mul(k.dps[:, 1, b * HD:(b + 1) * HD], k.mla_vt[HD:P, b * P:(b + 1) * P], const(k, "ident", HD, P)[:, HD:P],
                     start=True, stop=True)
        mm.then_inc(k.sem("mla_vtr_done"), 1)
        pe.wait_ge(k.sem("mla_q_done"), i * 2 + (h + 1))
        scores(0)
        if h == 0:
            pe.wait_ge(k.sem("mla_out_done"), i + 1)
        scores(1)
        pe.wait_ge(k.sem("mla_v_done"), i * 2 + (h + 1))
        if h:
            pe.wait_ge(k.sem("mla_o_done"), i * 2 + 1)
        g = 0
        for s in range(2, KT + 2):
            if s < KT:
                scores(s)
            elif s == KT:
                ahead(mla_queries_pe)
            else:
                ahead(mla_keys_pe)
            while g < N_GROUPS and GROUPS[g][0] == s - 2:
                turn(g)
                if g:
                    values(g - 1)
                g += 1
        values(N_GROUPS - 1)
        if h == 0:
            dense(k, pe, mla_block(i) + 1, 1, 0, rows(k.h_hi), rows(k.h_lo), KT, 0, i * MLA_USES + (MLA_USE0 + 4), "blk_done")
    pe.wait_ge(k.sem("mla_o_done"), i * 2 + 2)
    for b in range(KT):
        mm = k.nc.tensor.transpose(k.aps[:, 2 + b // 4, b % 4 * P:(b % 4 + 1) * P], k.mla_o[:, b, :], ident)
    mm.then_inc(k.sem("mla_yt_done"), 1)


def mla_dve(k, dve):
    dve.sem_inc(k.sem("mla_out_done"), 1)
    mla_proj_dve(k, dve, 0, 0)
    with dve.Fori(0, PAIRS - 1) as i:
        mla_pair_dve(k, dve, i, False)
    mla_pair_dve(k, dve, PAIRS - 1, True)


def mla_proj_dve(k, dve, i, h):
    v = k.nc.vector
    use = mla_use(i, h)
    dve.wait_ge(k.sem("mla_proj_done"), i * 3 + (2 * h + 1))
    v.tensor_tensor(k.mla_q[:, :], k.dps[:, 0, :], k.inv_q[:, :], ALU.mult).then_inc(k.sem("pair0_out"), 1)
    dve.wait_ge(k.sem("pair0_out"), use + 2)
    v.tensor_tensor(k.mla_q[HD:P, :], k.mla_q[HD:P, :], k.trig[HD:P, :], ALU.mult).then_inc(k.sem("mla_q_done"), 1)
    if h:
        dve.wait_ge(k.sem("blk_done"), mla_block(i) + 1)
    else:
        dve.wait_ge(k.sem("mla_proj_done"), i * 3 + 2)
    v.tensor_tensor(k.mla_k[0:HD, :], k.dps[0:HD, 0, :], k.inv_kv[0:HD, :], ALU.mult).then_inc(k.sem("mla_k_done"), 1)
    v.tensor_tensor(k.mla_vt[HD:P, :], k.dps[HD:P, 0, :], k.inv_kv[HD:P, :], ALU.mult).then_inc(k.sem("pair0_out"), 1)


def mla_pair_dve(k, dve, i, end):
    v = k.nc.vector
    for h in range(2):
        for b in range(KT):
            n = i * 16 + (8 * h + b + 1)
            r = b % 2
            dve.wait_ge(k.sem("mla_s_done"), n)
            v.tensor_reduce(k.mla_max[:, r, 0:1], k.aps[:, 2 * r:2 * r + 2, :].rearrange("p a b -> p (a b)")[:, 0:(b + 1) * P],
                            AX.X, ALU.max).then_inc(k.sem("mla_max_done"), 1)
            dve.wait_ge(k.sem("mla_max_done"), n)
            v.tensor_scalar(k.mla_max[:, r, 1:2], k.mla_max[:, r, 0:1], -MLA_SCALE, None, ALU.mult).then_inc(k.sem("mla_neg_done"), 1)
        if h == 0:
            mla_proj_dve(k, dve, i, 1)
        elif not end:
            mla_proj_dve(k, dve, i + 1, 0)
        dve.wait_ge(k.sem("mla_exp_done"), i * 16 + 8 * (h + 1))
        v.reciprocal(k.mla_sum[:, 1, h, :], k.mla_sum[:, 0, h, :]).then_inc(k.sem("mla_rsum_done"), 1)
        dve.wait_ge(k.sem("mla_rsum_done"), i * 2 + (h + 1))
        dve.wait_ge(k.sem("mla_pv_done"), i * 2 * N_GROUPS + N_GROUPS * (h + 1))
        v.tensor_tensor(k.mla_o[:, :, h * HD:(h + 1) * HD], k.dps[:, 1, HALF:2 * HALF].rearrange("p (a b) -> p a b", a=KT),
                        k.mla_sum[:, 1, h, :].rearrange("p (a b) -> p a b", b=1).to_broadcast([P, KT, HD]), ALU.mult).then_inc(k.sem("mla_o_done"), 1)
        if h == 0:
            dve.wait_ge(k.sem("blk_done"), mla_block(i) + 2)
            v.tensor_tensor(k.mla_gate[:, :], k.dps[:, 0, :], k.inv[:, :], ALU.mult).then_inc(k.sem("pair0_out"), 1)
    dve.wait_ge(k.sem("mla_yt_done"), i + 1)
    dve.wait_ge(k.sem("mla_gate_done"), i + 1)
    v.tensor_tensor(one(k.mla_out, i), k.aps[:, 2:4, :].rearrange("p a b -> p (a b)"), k.mla_gate[:, :], ALU.mult).then_inc(k.sem("mla_out_done"), 1)
    dve.wait_ge(k.sem("mla_out_done"), i + 2)


def mla_act(k, act):
    a = k.nc.scalar
    with act.Fori(0, PAIRS) as i:
        for h in range(2):
            act.wait_ge(k.sem("mla_vtr_done"), i * 2 + (h + 1))
            a.activation(k.mla_v[:, h, :, :].rearrange("p a b -> p (a b)"), k.dps[:, 1, 0:HALF], ACT.Copy).then_inc(k.sem("mla_v_done"), 1)
            g = 0
            for s in range(KT + 2):
                while g < N_GROUPS and GROUPS[g][0] == s - 2:
                    c = i * 2 * N_GROUPS + (N_GROUPS * h + g)
                    act.wait_ge(k.sem("mla_t_done"), c + 1)
                    if g >= 2:
                        act.wait_ge(k.sem("mla_pv_done"), c - 1)
                    w = GROUPS[g][2] * P
                    a.activation(k.mla_pt[:, g % 2, 0:w], k.dps[:, 1, 0:w], ACT.Copy).then_inc(k.sem("mla_pt_done"), 1)
                    g += 1
                if s < KT:
                    n = i * 16 + (8 * h + s + 1)
                    r = s % 2
                    act.wait_ge(k.sem("mla_neg_done"), n)
                    a.activation(k.mla_p[:, r, 0:(s + 1) * P], k.aps[:, 2 * r:2 * r + 2, :].rearrange("p a b -> p (a b)")[:, 0:(s + 1) * P],
                                 ACT.Exp, bias=k.mla_max[:, r, 1:2], scale=MLA_SCALE, accum_out=k.mla_sum[:, 0, h, s:s + 1]).then_inc(k.sem("mla_exp_done"), 1)
            if h == 0:
                act.wait_ge(k.sem("pair0_out"), i * MLA_USES + (MLA_USE0 + 6))
                a.activation(k.mla_gate[:, :], k.mla_gate[:, :], ACT.Silu).then_inc(k.sem("mla_gate_done"), 1)


LEVEL_STEPS = range(1, LEVELS + 1)


class Steps:

    def __init__(self, sem, names):
        self.sem, self.names = sem, names


LEVEL_NAMES = [f"{n}{l}" for l in LEVEL_STEPS for n in ("t", "x", "xt") if (n, l) != ("x", LEVELS)]
AHEAD = Steps("rw_ahead", ["rp", "kkp", "bq", "kq", "l_rel", "be", "ke", "rk"])
EXPS = Steps("rw_exps", ["p", "pp", "q", "e"])
PRODUCTS = Steps("rw_product", ["rk", "lt", "l", "ak_t", "rb_t", "rk_t", "kkp_tm", "v_tm", "akv", "be_tm", "ke_tm"] + LEVEL_NAMES
                 + ["u0", "w1_t"] + [f"{n}{c}" for c in range(NC) for n in ("w1s", "ds")])
VALUES = Steps("rw_value", ["rkv", "lt", "xt_part", "xt0", "x_part", "x0", "ak_t", "rb_t", "rk_t"] + LEVEL_NAMES
               + ["s_in"] + [f"{n}{c}" for c in range(NC) for n in ("u", "s")])
COPIES = Steps("rw_copy", ["kkp_tm", "v_tm", "akv", "be_tm", "ke_tm", "u0", "w1_t"])
Y_PRODUCTS = Steps("rw_y_product", ["y", "mean", "var"])
Y_VALUES = Steps("rw_y_value", ["centred"] + [f"rstd{n}" for n in range(4)] + ["normed", "gained", "summed"])
Y_COPIES = Steps("rw_y_copy", ["y", "sq", "std"])
TAKEN_BY = {"rk": (VALUES, "rkv"), "lt": (VALUES, "xt_part"), "l": (VALUES, "x_part"), **{n: (VALUES, n) for n in ["ak_t", "rb_t", "rk_t"] + LEVEL_NAMES},
            **{n: (COPIES, n) for n in COPIES.names}}
RW_BLOCKS = 8
RW_USES = 5
GATES = 4
GATE_BLOCK = (3, 5, 6, 7)
GATE_PAIR = (1, 1, 0, 1)
GATE_USE = (2, 3, 4, 4)
BANKS = 3
RW_USE0 = MLA_USE0 + MLA_USES * PAIRS
RW_USE1 = MLA_USE1


def rw_block(i):
    return i * RW_BLOCKS + (BLK["rwkv"] + 2)


class Half:

    def __init__(self, k, i, g):
        self.k, self.i, self.g = k, i, g
        self.tokens = slice(g * HALF, (g + 1) * HALF)

    def at(self, steps, name):
        n = len(steps.names)
        return self.i * (2 * n) + (self.g * n + steps.names.index(name) + 1)

    def wait(self, engine, steps, name):
        engine.wait_ge(self.k.sem(steps.sem), self.at(steps, name))


def bank(k, name):
    return k.aps[:, PRODUCTS.names.index(name) % BANKS, :]


def chunks(ap):
    return ap.rearrange("p (c t) -> p c t", c=NC)


def flat(t):
    return t[:, :, :].rearrange("p a b -> p (a b)")


HEADS = tuple(slice(h * HD, (h + 1) * HD) for h in range(2))


def masked(k, name):
    return const(k, name).rearrange("p (a b) -> p a b", a=1).to_broadcast([P, NC, HD])


def both(k, out, lhs, rhs, start=True, stop=True):
    for head in HEADS:
        mm = k.nc.tensor.matmul(out[head], lhs[head], rhs[head], start=start, stop=stop, skip_group_check=True)
    return mm


def rw_pe(k, pe):
    mul = k.nc.tensor.matmul
    second = lambda x: lambda t: x[:, t + 4, :]
    dense(k, pe, BLK["rwkv"], 0, 0, rows(k.h_hi), rows(k.h_lo), 4, 0, RW_USE0, "blk_done", last=False)
    dense(k, pe, BLK["rwkv"] + 1, 1, 0, second(k.h_hi), second(k.h_lo), 4, 0, RW_USE0, "blk_done", first=False)
    for n, use in enumerate((RW_USE0 + 1, RW_USE1)):
        dense(k, pe, BLK["rwkv"] + (2 + n), n, 0, rows(k.h_hi), rows(k.h_lo), KT, n, use, "blk_done")
    pe.wait_ge(k.sem("rw_tanh_done"), 1)
    rw_pair_pe(k, pe, 0, None)
    with pe.Fori(1, PAIRS - 1) as i:
        rw_pair_pe(k, pe, i, Half(k, i - 1, 1))
    rw_pair_pe(k, pe, PAIRS - 1, Half(k, PAIRS - 2, 1))
    for name in ("mean", "var"):
        rw_result_pe(k, pe, Half(k, PAIRS - 1, 1), name)


def rw_pair_pe(k, pe, i, before):
    mul = k.nc.tensor.matmul
    blk, use0, use1 = rw_block(i), i * RW_USES + (RW_USE0 + 1), i * RW_USES + RW_USE1
    pe.wait_ge(k.sem("rw_up_loaded"), i * 16 + 16)
    for n, (use, done) in enumerate(((use0, "rw_w_done"), (use1, "rw_a_done"))):
        pe.wait_ge(k.sem(f"pair{n}_out"), use + 2)
        for h in range(2):
            mm = mul(k.dps[:, n, h * HALF:(h + 1) * HALF], k.rw_up[HEADS[n], :], k.rw_wdad[HEADS[n], h * HALF:(h + 1) * HALF],
                     start=True, stop=True)
        mm.then_inc(k.sem(done), 1)
    pe.wait_ge(k.sem("rw_kk_sq_done"), i + 1)
    for h in range(2):
        mm = mul(k.aps[:, h, :], const(k, "headsum"), k.rw_e[:, h * HALF:(h + 1) * HALF], start=True, stop=True)
    mm.then_inc(k.sem("rw_kk_norm_done"), 1)
    dense(k, pe, blk + 2, 0, 0, rows(k.h_hi), rows(k.h_lo), KT, 0, use0 + 2, "blk_done")
    dense(k, pe, blk + 3, 1, 0, rows(k.h_hi), rows(k.h_lo), KT, 1, use1 + 2, "blk_done")
    first, last = Half(k, i, 0), Half(k, i, 1)
    ahead = ((blk + 8, 0, 0, use0 + 5), (blk + 9, 1, 1, use1 + 5)) if before is None or not isinstance(i, int) else ()
    rw_half_pe(k, pe, first, before, ((blk + 4, 0, 0, use0 + 3), (blk + 5, 1, 1, use1 + 3), (blk + 6, 0, 0, use0 + 4)))
    rw_half_pe(k, pe, last, first, ((blk + 7, 1, 1, use1 + 4), *ahead))


FILL_FIRST, FILL_LEVEL, FILL_WAIT, FILL_START, FILL_U, FILL_S, FILL_Y = 1, 2, 4, 4, 3, 5, 1


def rw_half_pe(k, pe, u, before, tiles):
    product = k.sem("rw_product")
    made = {name: t[u.g] for name, t in k.ahead.items()}
    m = k.half
    filled = 0

    def fill(n):
        nonlocal filled
        for at in range(filled, min(filled + n, 6 * KT * len(tiles))):
            lo = at % (6 * KT)
            dense_part(k, pe, *tiles[at // (6 * KT)], "blk_done", lo, lo + 1)
        filled = min(filled + n, 6 * KT * len(tiles))

    def free(name):
        u.wait(pe, *TAKEN_BY[PRODUCTS.names[PRODUCTS.names.index(name) - BANKS]])

    def each_chunk(name, lhs, rhs, beside=FILL_FIRST):
        fill(beside)
        for c in range(NC):
            mm = both(k, bank(k, name)[:, c * CH:(c + 1) * CH], lhs[:, c, :], rhs[:, c, :])
        mm.then_inc(product, 1)

    def turned(name, lhs):
        ident = const(k, "pair_ident")
        fill(1)
        for c in range(NC):
            mm = both(k, bank(k, name)[:, c * CH:(c + 1) * CH], lhs[:, c, :], ident)
        mm.then_inc(product, 1)

    u.wait(pe, AHEAD, "rk")
    k.nc.tensor.matmul(bank(k, "rk"), const(k, "headsum"), flat(made["rkv"]), start=True, stop=True).then_inc(product, 1)
    if before is not None:
        before.wait(pe, VALUES, f"s{NC - 1}")
    each_chunk("lt", made["bq"], made["kkp"])
    each_chunk("l", made["kkp"], made["bq"])
    if before is not None:
        rw_result_pe(k, pe, before, "mean")
    free("ak_t")
    each_chunk("ak_t", made["kq"], made["kkp"])
    free("rb_t")
    each_chunk("rb_t", made["bq"], made["rp"])
    free("rk_t")
    each_chunk("rk_t", made["kq"], made["rp"])
    free("kkp_tm")
    turned("kkp_tm", made["kkp"])
    free("v_tm")
    fill(1)
    for c in range(NC):
        t = slice(u.g * HALF + c * CH, u.g * HALF + (c + 1) * CH)
        mm = both(k, bank(k, "v_tm")[:, c * CH:(c + 1) * CH], k.rw_v[:, t], const(k, "pair_ident"))
    mm.then_inc(product, 1)
    if before is not None:
        rw_result_pe(k, pe, before, "var")
    free("akv")
    u.wait(pe, COPIES, "v_tm")
    each_chunk("akv", m["akt"], m["v_tm"])
    free("be_tm")
    turned("be_tm", made["be"])
    free("ke_tm")
    turned("ke_tm", made["ke"])
    for l in LEVEL_STEPS:
        free(f"t{l}")
        u.wait(pe, VALUES, "x0" if l == 1 else f"x{l - 1}")
        each_chunk(f"t{l}", m["lt"], m["xm"], FILL_LEVEL)
        fill(FILL_WAIT)
        u.wait(pe, VALUES, f"t{l}")
        if l < LEVELS:
            free(f"x{l}")
            each_chunk(f"x{l}", m["xt"], m["t1"], FILL_LEVEL)
        free(f"xt{l}")
        each_chunk(f"xt{l}", m["t1"], m["xt"], FILL_LEVEL)
    free("u0")
    u.wait(pe, VALUES, f"xt{LEVELS}")
    u.wait(pe, COPIES, "akv")
    each_chunk("u0", m["xt"], m["akv"], FILL_LEVEL)
    free("w1_t")
    each_chunk("w1_t", m["kkp_tm"], m["xt"], FILL_LEVEL)
    assert filled >= 6 * KT
    fill(FILL_START)
    u.wait(pe, COPIES, "w1_t")
    for c in range(NC):
        at = slice(c % 2 * HD, (c % 2 + 1) * HD)
        u.wait(pe, VALUES, f"s{c - 1}" if c else "s_in")
        fill(FILL_S)
        both(k, k.aps[:, 0, at], m["w1_t"][:, c, :], m["s"][:, c, :]).then_inc(product, 1)
        both(k, k.aps[:, 1, at], m["ke_tm"][:, c, :], m["v_tm"][:, c, :], stop=False)
        u.wait(pe, VALUES, f"u{c}")
        fill(FILL_U)
        both(k, k.aps[:, 1, at], m["be_tm"][:, c, :], m["u"][:, c, :], start=False).then_inc(product, 1)
    if before is not None:
        before.wait(pe, Y_COPIES, "std")
    for c in range(NC):
        t = slice(c * CH, (c + 1) * CH)
        fill(FILL_Y)
        both(k, k.aps[:, 3, t], m["s"][:, c, :], made["rp"][:, c, :], stop=False)
        both(k, k.aps[:, 3, t], m["v_tm"][:, c, :], m["arkt"][:, c, :], start=False, stop=False)
        mm = both(k, k.aps[:, 3, t], m["u"][:, c, :], m["arbt"][:, c, :], start=False)
    mm.then_inc(k.sem("rw_y_product"), 1)
    fill(6 * KT * len(tiles))


def rw_result_pe(k, pe, u, name):
    src, wait = {"mean": (flat(k.half["y"]), (Y_COPIES, "y")), "var": (k.rw_out[:, u.g, :], (Y_COPIES, "sq"))}[name]
    u.wait(pe, *wait)
    k.nc.tensor.matmul(k.aps[:, 3, :], const(k, "headsum"), src, start=True, stop=True).then_inc(k.sem("rw_y_product"), 1)


def rw_dve(k, dve):
    v = k.nc.vector
    dve.wait_ge(k.sem("yb_spilled"), 16)
    for n in range(3):
        zeroed = v.memset(k.rw_pad[n][:, 0:1], 0.0)
    zeroed.then_inc(k.sem("rw_zeroed"), 1)
    dve.wait_ge(k.sem("rw_zeroed"), 1)
    dve.wait_ge(k.sem("blk_done"), BLK["rwkv"] + 2)
    v.tensor_tensor(k.rw_r, k.dps[:, 0, :], k.inv[:, :], ALU.mult).then_inc(k.sem("pair0_out"), 1)
    dve.wait_ge(k.sem("pair0_out"), RW_USE0 + 2)
    rw_shift(k, dve, 1, k.rw_r, k.rw_pad[0], k.rw_wdad[:, :], vec(k, "mu", 12))
    rw_pair_dve(k, dve, 0, None)
    with dve.Fori(1, PAIRS - 1) as i:
        rw_pair_dve(k, dve, i, Half(k, i - 1, 1))
    rw_pair_dve(k, dve, PAIRS - 1, Half(k, PAIRS - 2, 1))
    for step in Y_VALUES.names + ["gated"]:
        rw_result_dve(k, dve, Half(k, PAIRS - 1, 1), step)
    dve.wait_ge(k.sem("branch_hi_done"), BACK + 1)
    v.tensor_tensor(k.ya2_lo[:, PAIRS - 1, :], k.rw_out[:, :, :].rearrange("p a b -> p (a b)"),
                    k.ya2_hi[:, PAIRS - 1, :].bitcast(F32), ALU.subtract).then_inc(k.sem("last_lo_done"), 1)


def rw_shift(k, dve, n, seq, pad, out, mu):
    v = k.nc.vector
    v.tensor_tensor(k.rw_d[:, :], pad[:, 0:S], seq, ALU.subtract).then_inc(k.sem("rw_diff_done"), 1)
    dve.wait_ge(k.sem("rw_diff_done"), n)
    v.scalar_tensor_tensor(out, k.rw_d[:, :], mu, seq, ALU.mult, ALU.add).then_inc(k.sem("rw_mix_done"), 1)
    dve.wait_ge(k.sem("rw_mix_done"), n)


def rw_pair_dve(k, dve, i, before):
    v = k.nc.vector
    blk, use = rw_block(i), (i * RW_USES + (RW_USE0 + 1), i * RW_USES + RW_USE1)

    def take(n, seq, pair, nth):
        dve.wait_ge(k.sem("blk_done"), blk + (n + 1))
        v.tensor_tensor(seq, k.dps[:, pair, :], k.inv[:, :], ALU.mult).then_inc(k.sem(f"pair{pair}_out"), 1)
        dve.wait_ge(k.sem(f"pair{pair}_out"), use[pair] + (nth + 2))

    if before is not None:
        before.wait(dve, VALUES, f"s{NC - 1}")
        dve.wait_ge(k.sem("gate_spilled"), i * (16 * GATES))
    v.memset(k.rw_s[:, :], 0.0).then_inc(k.sem("rw_s_zero"), 1)
    take(0, k.rw_r, 0, 0)
    take(1, k.rw_k, 1, 0)
    rw_shift(k, dve, i * 3 + 2, k.rw_k, k.rw_pad[1], k.rw_k, vec(k, "mu", i + 4))
    v.tensor_scalar(k.rw_kk[:, :], k.rw_k, vec(k, "k_k", i), None, ALU.mult).then_inc(k.sem("rw_kk_done"), 1)
    rw_shift(k, dve, i * 3 + 3, k.rw_r, k.rw_pad[0], k.rw_r, vec(k, "mu", i))
    dve.wait_ge(k.sem("pair0_out"), use[0] + 3)
    for h in range(2):
        t = slice(h * HALF, (h + 1) * HALF)
        v.tensor_tensor_scan(k.rw_l[:, t], const(k, "reset"), k.rw_sg[:, t], 0.0, ALU.mult, ALU.add).then_inc(k.sem("rw_l_done"), 1)
    dve.wait_ge(k.sem("rw_l_done"), i * 2 + 2)
    v.tensor_tensor(k.rw_sg[:, :], k.rw_l[:, :], k.rw_sg[:, :], ALU.subtract).then_inc(k.sem("rw_lp_done"), 1)
    dve.wait_ge(k.sem("rw_kk_root_done"), i + 1)
    dve.wait_ge(k.sem("pair1_out"), use[1] + 3)
    v.tensor_scalar(k.rw_e[:, :], k.rw_b[:, :], -1.0, vec(k, "k_a", i), ALU.add, ALU.mult).then_inc(k.sem("rw_rate_done"), 1)
    steps = (lambda: v.tensor_scalar(k.rw_d[:, :], k.rw_d[:, :], 1e-12, None, ALU.max),
             lambda: v.reciprocal(k.rw_d[:, :], k.rw_d[:, :]),
             lambda: v.tensor_tensor(k.rw_kk[:, :], k.rw_kk[:, :], k.rw_d[:, :], ALU.mult),
             lambda: v.tensor_tensor(k.rw_b[:, :], k.rw_b[:, :], k.rw_kk[:, :], ALU.mult))
    for n, step in enumerate(steps):
        step().then_inc(k.sem("rw_unit_done"), 1)
        dve.wait_ge(k.sem("rw_unit_done"), i * 4 + (n + 1))
    dve.wait_ge(k.sem("rw_rate_done"), i + 1)
    v.scalar_tensor_tensor(k.rw_k, k.rw_e[:, :], 1.0, k.rw_k, ALU.add, ALU.mult).then_inc(k.sem("rw_in_done"), 1)
    dve.wait_ge(k.sem("rw_in_done"), i + 1)
    dve.wait_ge(k.sem("rw_s_zero"), i + 1)
    first, last = Half(k, i, 0), Half(k, i, 1)
    rw_ahead_dve(k, dve, first, range(0, 8))
    take(2, k.rw_v, 0, 2)
    rw_shift(k, dve, i * 3 + 4, k.rw_v, k.rw_pad[2], k.rw_v, vec(k, "mu", i + 8))
    rw_half_dve(k, dve, first, before)
    take(4, k.rw_z[:, :], 0, 3)
    rw_ahead_dve(k, dve, last, range(0, 5))
    rw_chunks_dve(k, dve, first)
    rw_ahead_dve(k, dve, last, range(5, 8))
    rw_half_dve(k, dve, last, first)
    rw_chunks_dve(k, dve, last)


def rw_ahead_dve(k, dve, u, steps):
    v = k.nc.vector
    ts = u.tokens
    p, pp, q = k.rw_t
    l_half = chunks(k.rw_l[:, ts])
    out = {name: flat(t[u.g]) for name, t in k.ahead.items()}
    mul = lambda name, x, y: v.tensor_tensor(out[name], x, y, ALU.mult)
    for n in steps:
        name = AHEAD.names[n]
        if name == "rp":
            u.wait(dve, EXPS, "p")
            ins = mul("rp", k.rw_r[:, ts], p[:, :])
        elif name == "kkp":
            u.wait(dve, EXPS, "pp")
            ins = mul("kkp", k.rw_kk[:, ts], pp[:, :])
        elif name == "bq":
            u.wait(dve, EXPS, "q")
            ins = mul("bq", k.rw_b[:, ts], q[:, :])
        elif name == "kq":
            ins = mul("kq", k.rw_k[:, ts], q[:, :])
        elif name == "l_rel":
            u.wait(dve, AHEAD, "rp")
            ins = v.tensor_tensor(chunks(p[:, :]), l_half, l_half[:, :, CH - 1:CH].to_broadcast([P, NC, CH]), ALU.subtract)
        elif name == "be":
            u.wait(dve, EXPS, "e")
            ins = mul("be", k.rw_b[:, ts], p[:, :])
        elif name == "ke":
            ins = mul("ke", k.rw_k[:, ts], p[:, :])
        else:
            ins = v.scalar_tensor_tensor(out["rkv"], k.rw_r[:, ts], vec(k, "r_k", u.i), k.rw_k[:, ts], ALU.mult, ALU.mult)
        ins.then_inc(k.sem("rw_ahead"), 1)


def rw_half_dve(k, dve, u, before):
    v = k.nc.vector
    made = k.sem("rw_value")
    m = k.half
    taken = lambda name: chunks(bank(k, name))
    rest = iter(Y_VALUES.names + ["gated"])

    def result_step():
        if before is not None:
            step = next(rest, None)
            if step is not None:
                rw_result_dve(k, dve, before, step)
            return step
        return None

    def mask(out, name, which):
        return v.tensor_tensor(m[out][:, :, :], taken(name), masked(k, which), ALU.mult)

    u.wait(dve, PRODUCTS, "rk")
    rkv = flat(k.ahead["rkv"][u.g])
    v.tensor_tensor(rkv, bank(k, "rk"), k.rw_v[:, u.tokens], ALU.mult).then_inc(made, 1)
    u.wait(dve, PRODUCTS, "lt")
    mask("lt", "lt", "strict_t").then_inc(made, 1)
    for first, which, out, part in (("lt", "lev0_t", "xt", "xt_part"), ("l", "lev0", "xm", "x_part")):
        u.wait(dve, PRODUCTS, first)
        mask(out, first, which).then_inc(made, 1)
        u.wait(dve, VALUES, part)
        v.tensor_tensor(m[out][:, :, :], masked(k, "pair_ident"), m[out][:, :, :], ALU.subtract).then_inc(made, 1)
    result_step()
    for name, out, which in (("ak_t", "akt", "strict_t"), ("rb_t", "arbt", "incl_t"), ("rk_t", "arkt", "incl_t")):
        u.wait(dve, PRODUCTS, name)
        mask(out, name, which).then_inc(made, 1)
    for l in LEVEL_STEPS:
        u.wait(dve, PRODUCTS, f"t{l}")
        mask("t1", f"t{l}", f"lev{l}").then_inc(made, 1)
        result_step()
        for n, out in (("x", "xm"), ("xt", "xt")):
            if (n, l) != ("x", LEVELS):
                u.wait(dve, PRODUCTS, f"{n}{l}")
                v.tensor_tensor(m[out][:, :, :], m[out][:, :, :], taken(f"{n}{l}"), ALU.subtract).then_inc(made, 1)
        result_step()
    while result_step() is not None:
        pass


def rw_chunks_dve(k, dve, u):
    v = k.nc.vector
    made = k.sem("rw_value")
    m = k.half
    v.tensor_copy(m["s"][:, 0, :], k.rw_s[:, :]).then_inc(made, 1)
    u.wait(dve, VALUES, "s_in")
    u.wait(dve, COPIES, "u0")
    for c in range(NC):
        at = slice(c % 2 * HD, (c % 2 + 1) * HD)
        u.wait(dve, PRODUCTS, f"w1s{c}")
        v.scalar_tensor_tensor(m["u"][:, c, :], k.aps[:, 0, at], -1.0, m["u0"][:, c, :], ALU.mult, ALU.subtract).then_inc(made, 1)
        u.wait(dve, PRODUCTS, f"ds{c}")
        if c:
            u.wait(dve, VALUES, f"s{c - 1}")
        pc = k.rw_pc[:, u.g * NC + c:u.g * NC + c + 1]
        out = m["s"][:, c + 1, :] if c < NC - 1 else k.rw_s[:, :]
        v.scalar_tensor_tensor(out, m["s"][:, c, :], pc, k.aps[:, 1, at], ALU.mult, ALU.add).then_inc(made, 1)


def rw_result_dve(k, dve, u, step):
    v = k.nc.vector
    made = k.sem("rw_y_value")
    y = k.rw_centred
    if step == "centred":
        u.wait(dve, Y_PRODUCTS, "mean")
        v.scalar_tensor_tensor(y[:, :], k.aps[:, 3, :], -1.0 / HD, flat(k.half["y"]), ALU.mult, ALU.add).then_inc(made, 1)
    elif step.startswith("rstd"):
        part = slice(int(step[-1]) * P, (int(step[-1]) + 1) * P)
        u.wait(dve, Y_COPIES, "std")
        v.reciprocal(k.rw_rstd[:, part], k.rw_rstd[:, part]).then_inc(made, 1)
    elif step == "normed":
        u.wait(dve, Y_VALUES, "rstd3")
        v.tensor_tensor(y[:, :], y[:, :], k.rw_rstd[:, :], ALU.mult).then_inc(made, 1)
    elif step == "gained":
        u.wait(dve, Y_VALUES, "normed")
        v.tensor_scalar(y[:, :], y[:, :], vec(k, "gn_gain", u.i), vec(k, "gn_bias", u.i), ALU.mult, ALU.add).then_inc(made, 1)
    elif step == "summed":
        u.wait(dve, Y_VALUES, "gained")
        v.tensor_tensor(y[:, :], y[:, :], flat(k.ahead["rkv"][u.g]), ALU.add).then_inc(made, 1)
    else:
        u.wait(dve, Y_VALUES, "summed")
        dve.wait_ge(k.sem("rw_silu_done"), u.i + 1)
        v.tensor_tensor(k.rw_out[:, u.g, :], y[:, :], k.rw_z[:, u.tokens], ALU.mult).then_inc(k.sem("rw_gated"), 1)
        dve.wait_ge(k.sem("rw_gated"), u.i * 2 + (u.g + 1))


def rw_act(k, act, w_up, branches, gates):
    a = k.nc.scalar
    act.wait_ge(k.sem("mla_out_done"), PAIRS + 1)
    act.dma_start(branches[:, PAIRS - 1:2 * PAIRS - 1, :], k.mla_out[:, :, :]).then_inc(k.sem("yb_spilled"), 16)
    act.wait_ge(k.sem("rw_mix_done"), 1)
    a.activation(k.rw_wdad[0:HD, :], k.rw_wdad[0:HD, :], ACT.Tanh).then_inc(k.sem("rw_tanh_done"), 1)
    rw_pair_act(k, act, 0, None, w_up, branches, gates)
    with act.Fori(1, PAIRS - 1) as i:
        rw_pair_act(k, act, i, Half(k, i - 1, 1), w_up, branches, gates)
    rw_pair_act(k, act, PAIRS - 1, Half(k, PAIRS - 2, 1), w_up, branches, gates)
    last = Half(k, PAIRS - 1, 1)
    for step in ("sq", "std"):
        rw_result_act(k, act, last, step)
    act.wait_ge(k.sem("rw_gated"), 2 * PAIRS)
    a.activation(k.ya2_hi[:, PAIRS - 1, :], k.rw_out[:, :, :].rearrange("p a b -> p (a b)"), ACT.Copy).then_inc(k.sem("branch_hi_done"), 1)
    gate_load(k, act, 0, 1, gates)


def rw_pair_act(k, act, i, before, w_up, branches, gates):
    a = k.nc.scalar
    use0, use1 = i * RW_USES + (RW_USE0 + 1), i * RW_USES + RW_USE1
    act.dma_start(k.rw_up[:, :], w_up[bass.ds(i, 1)].rearrange("a p n -> p (a n)")).then_inc(k.sem("rw_up_loaded"), 16)
    act.wait_ge(k.sem("rw_kk_done"), i + 1)
    a.activation(k.rw_e[:, :], k.rw_kk[:, :], ACT.Square).then_inc(k.sem("rw_kk_sq_done"), 1)
    act.wait_ge(k.sem("rw_w_done"), i + 1)
    fixed_wait(k, act)
    a.activation(k.rw_sg[:, :], k.dps[:, 0, :], ACT.Sigmoid, bias=vec(k, "w0", i)).then_inc(k.sem("pair0_out"), 1)
    act.wait_ge(k.sem("rw_a_done"), i + 1)
    fixed_wait(k, act)
    a.activation(k.rw_b[:, :], k.dps[:, 1, :], ACT.Sigmoid, bias=vec(k, "a0", i)).then_inc(k.sem("pair1_out"), 1)
    act.wait_ge(k.sem("rw_kk_norm_done"), i + 1)
    act.wait_ge(k.sem("rw_mix_done"), i * 3 + 3)
    a.activation(k.rw_d[:, :], k.aps[:, 0:2, :].rearrange("p a b -> p (a b)"), ACT.Sqrt).then_inc(k.sem("rw_kk_root_done"), 1)
    act.wait_ge(k.sem("rw_l_done"), i * 2 + 2)
    a.activation(k.rw_pc[:, :], k.rw_l[:, :].rearrange("p (c t) -> p c t", t=CH)[:, :, CH - 1:CH].rearrange("p c t -> p (c t)"),
                 ACT.Exp, scale=-DECAY).then_inc(k.sem("rw_pc_done"), 1)
    act.wait_ge(k.sem("rw_in_done"), i + 1)
    first, last = Half(k, i, 0), Half(k, i, 1)
    rw_exps_act(k, act, first)
    rw_e_act(k, act, first)
    rw_half_act(k, act, first, before, last, branches, gates)
    rw_half_act(k, act, last, first, None, branches, gates)


def rw_spill(k, act, u, branches):
    act.wait_ge(k.sem("rw_gated"), u.i * 2 + (u.g + 1))
    act.dma_start(branches[:, bass.ds(u.i, 1), u.tokens].rearrange("p a t -> p (a t)"), k.rw_out[:, u.g, :]).then_inc(k.sem(f"rw_spilled{u.g}"), 16)


def rw_exps_act(k, act, u):
    a = k.nc.scalar
    for n, (src, sign) in enumerate(((k.rw_l, -1), (k.rw_sg, -1), (k.rw_l, 1))):
        a.activation(k.rw_t[n][:, :], src[:, u.tokens], ACT.Exp, scale=sign * DECAY).then_inc(k.sem("rw_exps"), 1)


def rw_e_act(k, act, u):
    u.wait(act, AHEAD, "l_rel")
    k.nc.scalar.activation(k.rw_t[0][:, :], k.rw_t[0][:, :], ACT.Exp, scale=DECAY).then_inc(k.sem("rw_exps"), 1)


def rw_gate_act(k, act, u, n, gates):
    pair = GATE_PAIR[n]
    act.wait_ge(k.sem("blk_done"), rw_block(u.i) + (GATE_BLOCK[n] + 1))
    if n < 2:
        u.wait(act, AHEAD, "ke")
        if n == 0:
            act.wait_ge(k.sem("rw_mix_done"), u.i * 3 + 4)
    else:
        rw_gate_spilled(k, act, u, n - 1)
    k.nc.scalar.activation(k.gate_out[:, :], k.dps[:, pair, :], ACT.Copy).then_inc(k.sem(f"pair{pair}_out"), 1)
    act.wait_ge(k.sem(f"pair{pair}_out"), u.i * RW_USES + ((RW_USE0 + 1, RW_USE1)[pair] + GATE_USE[n] + 2))
    act.dma_start(one(gates, u.i * GATES + n), k.gate_out[:, :]).then_inc(k.sem("gate_spilled"), 16)


def rw_gate_spilled(k, act, u, n):
    act.wait_ge(k.sem("gate_spilled"), u.i * (16 * GATES) + 16 * (n + 1))


def rw_half_act(k, act, u, before, after, branches, gates):
    a = k.nc.scalar
    m = k.half
    end = after is None and isinstance(u.i, int) and u.i == PAIRS - 1

    def copy(name):
        u.wait(act, PRODUCTS, name)
        a.activation(flat(m[name]), bank(k, name), ACT.Copy).then_inc(k.sem("rw_copy"), 1)

    rw_gate_act(k, act, u, 0 if after is not None else 1, gates)
    copy("kkp_tm")
    if before is not None:
        rw_result_act(k, act, before, "sq")
    copy("v_tm")
    if before is not None:
        rw_result_act(k, act, before, "std")
    copy("akv")
    copy("be_tm")
    copy("ke_tm")
    if after is None:
        for n in (2, 3):
            rw_gate_act(k, act, u, n, gates)
        if end:
            back_load(k, act, u, branches, gates)
    else:
        rw_gate_spilled(k, act, u, 0)
        u.wait(act, AHEAD, "ke")
        rw_exps_act(k, act, after)
    copy("u0")
    copy("w1_t")
    if end:
        back_act(k, act)
    elif before is not None:
        rw_spill(k, act, before, branches)
    if after is not None:
        act.wait_ge(k.sem("pair0_out"), u.i * RW_USES + (RW_USE0 + 6))
        a.activation(k.rw_z[:, :], k.rw_z[:, :], ACT.Silu).then_inc(k.sem("rw_silu_done"), 1)
        rw_e_act(k, act, after)
    rw_result_act(k, act, u, "y")


def rw_result_act(k, act, u, step):
    a = k.nc.scalar
    done = k.sem("rw_y_copy")
    if step == "y":
        u.wait(act, Y_PRODUCTS, "y")
        a.activation(flat(k.half["y"]), k.aps[:, 3, :], ACT.Copy).then_inc(done, 1)
    elif step == "sq":
        u.wait(act, Y_VALUES, "centred")
        act.wait_ge(k.sem(f"rw_spilled{u.g}"), u.i * 16 + 16)
        a.activation(k.rw_out[:, u.g, :], k.rw_centred[:, :], ACT.Square).then_inc(done, 1)
    else:
        u.wait(act, Y_PRODUCTS, "var")
        a.activation(k.rw_rstd[:, :], k.aps[:, 3, :], ACT.Sqrt, bias=GN_EPS, scale=1.0 / HD).then_inc(done, 1)


MERGE2_USE = (RW_USE0 + 1 + RW_USES * PAIRS, RW_USE1 + RW_USES * PAIRS)
OUT2_USE = tuple(n + KT for n in MERGE2_USE)


BACK = 2 * PAIRS - 1


def back_tile(k, n):
    hi, lo = (k.yb2_hi, k.yb2_lo) if n < PAIRS else (k.ya2_hi, k.ya2_lo)
    return hi[:, n % PAIRS, :], lo[:, n % PAIRS, :]


def back_load(k, act, u, branches, gates):
    u.wait(act, VALUES, "rk_t")
    act.wait_ge(k.sem("yb_spilled"), 16)
    for g in range(2):
        act.wait_ge(k.sem(f"rw_spilled{g}"), PAIRS * 16)
    for n in range(BACK):
        act.dma_start(k.back[n][:, :], branches[:, (n + PAIRS - 1) % BACK, :]).then_inc(k.sem(f"branch_loaded{n}"), 16)
    act.wait_ge(k.sem("gate_spilled"), 16 * GATES * PAIRS)
    gate_load(k, act, 0, 0, gates)


def back_act(k, act):
    act.wait_ge(k.sem("blk_done"), BLK["merge2"])
    for n in range(BACK):
        act.wait_ge(k.sem(f"branch_loaded{n}"), 16)
        k.nc.scalar.activation(back_tile(k, n)[0], k.back[n][:, :], ACT.Copy).then_inc(k.sem("branch_hi_done"), 1)


def back_pool(k, pool):
    for n in range(BACK):
        hi, lo = back_tile(k, n)
        pool.wait_ge(k.sem("branch_hi_done"), n + 1)
        k.nc.gpsimd.tensor_tensor(lo, k.back[n][:, :], hi.bitcast(F32), ALU.subtract).then_inc(k.sem("branch_lo_done"), 1)


def merge2_pe(k, pe):
    b = BLK["merge2"]

    def second(n, slot):
        dense(k, pe, n + b, slot, 4, rows(k.yb2_hi), rows(k.yb2_lo), 4, 1, n + MERGE2_USE[1], "branch_b_done")

    def tile(n, slot):
        second(n, slot)
        dense(k, pe, n + b, slot, 0, rows(k.ya2_hi), rows(k.ya2_lo), 4, 0, n + MERGE2_USE[0], "blk_done")

    pe.wait_ge(k.sem("branch_lo_done"), PAIRS)
    second(0, 0)
    pe.wait_ge(k.sem("branch_lo_done"), BACK)
    dense(k, pe, b, 0, 0, rows(k.ya2_hi), rows(k.ya2_lo), PAIRS - 1, 0, MERGE2_USE[0], None, last=False)
    pe.wait_ge(k.sem("last_lo_done"), 1)
    end = lambda x: lambda t: x[:, PAIRS - 1, :]
    dense(k, pe, b, 0, PAIRS - 1, end(k.ya2_hi), end(k.ya2_lo), 1, 0, MERGE2_USE[0], "blk_done", first=False)
    with pe.Fori(0, KT // 2 - 1) as i:
        for j in range(2):
            tile(i * 2 + (1 + j), 1 - j)
    tile(KT - 1, 1)


def merge2_dve(k, dve):
    v = k.nc.vector

    def scale(n, g):
        dve.wait_ge(k.sem(f"gate{g}_loaded"), n * 16 + 16)
        v.tensor_tensor(k.tmp[g][:, :], k.tmp[g][:, :], k.inv[:, :], ALU.mult).then_inc(k.sem(f"gate{g}_scaled"), 1)

    for g in range(2):
        scale(0, g)
    def tile(n):
        dve.wait_ge(k.sem("branch_b_done"), n + 1)
        dve.wait_ge(k.sem("gate_done"), n * 2 + (2 * KT + 2))
        v.tensor_tensor(k.tmp1[:, :], k.dps[:, 1, :], k.tmp1[:, :], ALU.mult).then_inc(k.sem("pair1_out"), 1)
        dve.wait_ge(k.sem("blk_done"), n + (BLK["merge2"] + 1))
        v.tensor_tensor(one(k.merged, n), k.dps[:, 0, :], k.tmp0[:, :], ALU.mult).then_inc(k.sem("pair0_out"), 1)
        dve.wait_ge(k.sem("pair0_out"), n + (MERGE2_USE[0] + 2))
        dve.wait_ge(k.sem("pair1_out"), n + (MERGE2_USE[1] + 2))
        v.tensor_tensor(one(k.merged, n), one(k.merged, n), k.tmp1[:, :], ALU.add).then_inc(k.sem("merged_done"), 1)

    with dve.Fori(0, KT - 1) as n:
        tile(n)
        for g in range(2):
            scale(n + 1, g)
    tile(KT - 1)


def merge2_act(k, act, gates):
    def sigmoids(n):
        for g in range(2):
            act.wait_ge(k.sem(f"gate{g}_scaled"), n + 1)
            fixed_wait(k, act)
            k.nc.scalar.activation(k.tmp[g][:, :], k.tmp[g][:, :], ACT.Sigmoid, bias=vec(k, "b_gate", n + KT * g)).then_inc(k.sem("gate_done"), 1)

    with act.Fori(0, KT - 1) as n:
        sigmoids(n)
        act.wait_ge(k.sem("pair0_out"), n + (MERGE2_USE[0] + 2))
        gate_load(k, act, n + 1, 0, gates)
        act.wait_ge(k.sem("merged_done"), n + (KT + 1))
        gate_load(k, act, n + 1, 1, gates)
    sigmoids(KT - 1)


def gate_load(k, act, n, g, gates):
    act.dma_start(k.tmp[g][:, :], one(gates, n * 2 + g)).then_inc(k.sem(f"gate{g}_loaded"), 16)


def out2_pe(k, pe):
    with pe.Fori(0, KT // 2) as i:
        for j in range(2):
            dense(k, pe, i * 2 + (BLK["out2"] + j), j, 0, rows(k.h_hi), rows(k.h_lo), KT, j, i + OUT2_USE[j], "blk_done",
                  ready=("h_lo_done", 5 * KT) if j == 0 else None)
    stat(k, pe, 5)


def out2_act(k, act, x1_t):
    act.wait_ge(k.sem("blk_done"), BLK["out2"])
    act.dma_start(k.x1_again[:, :, :], x1_t).then_inc(k.sem("x1_again_loaded"), 16)
    merged_split_act(k, act, BLK["out2"], 1)
    with act.Fori(0, KT // 2) as i:
        for j in range(2):
            act.wait_ge(k.sem(f"pair{j}_out"), i + (OUT2_USE[j] + 2))
            square_act(k, act, 5, i * 2 + j, k.sq[j][:, :])
    inv_act(k, act, 5)


def out2_dve(k, dve):
    v = k.nc.vector
    sumsq_begin(k, dve, 5)
    with dve.Fori(0, KT // 2) as i:
        for j in range(2):
            n = i * 2 + j
            dve.wait_ge(k.sem("blk_done"), i * 2 + (BLK["out2"] + j + 1))
            v.tensor_copy(one(k.x, n), k.dps[:, j, :]).then_inc(k.sem(f"pair{j}_out"), 1)
            sumsq_dve(k, dve, 5, n, k.sq[j][:, :])
    inv_dve(k, dve, 5)
    dve.wait_ge(k.sem("x1_again_loaded"), 16)
    for n in range(KT):
        v.scalar_tensor_tensor(k.x[:, n, :], k.x[:, n, :], vec(k, "g_post", n), k.inv[:, :], ALU.mult,
                               ALU.mult).then_inc(k.sem("post_done"), 1)
        dve.wait_ge(k.sem("post_done"), n + 1)
        v.tensor_tensor(k.x1_again[:, n, :], k.x1_again[:, n, :], k.x[:, n, :], ALU.add).then_inc(k.sem("result_done"), 1)


def store_sync(k, sp, out):
    for n in range(KT):
        sp.wait_ge(k.sem("result_done"), n + 1)
        sp.dma_start(out[:, n, :], k.x1_again[:, n, :]).then_inc(k.sem("stored"), 16)
    sp.wait_ge(k.sem("stored"), KT * 16)


def stream_sync(k, sp, w_stream, n_blk, consts):
    for s in range(2):
        sp.dma_start(k.w_raw[:, s], w_stream[s]).then_inc(k.sem(f"w_loaded{s}"), 16)
    sp.dma_start(k.const[:, :], consts).then_inc(k.sem("const_loaded"), 16)
    with sp.Fori(1, n_blk // 2) as i:
        for s in range(2):
            sp.wait_ge(k.sem("w_split"), i * 2 + (s - 1))
            sp.dma_start(k.w_raw[:, s], w_stream[bass.ds(i * 2 + s, 1)].rearrange("a p k n -> p (a k) n")).then_inc(k.sem(f"w_loaded{s}"), 16)


def stream_pool(k, pool, n_blk):
    g = k.nc.gpsimd
    g.memset(k.one[:, :], 1.0).then_inc(k.sem("one_done"), 1)
    pool.wait_ge(k.sem("one_done"), 1)
    ones = k.one[:, 0:1].to_broadcast([P, SUB * P]).rearrange("p (a b) -> p a b", a=SUB)

    def split(i, s, first):
        pool.wait_ge(k.sem(f"w_loaded{s}"), i * 16 + 16)
        if not first:
            pool.wait_ge(k.sem("blk_done"), i * 2 + (s - 1))
        g.tensor_tensor(k.w_hi[:, s], k.w_raw[:, s], ones, ALU.mult).then_inc(k.sem("w_hi_done"), 1)
        pool.wait_ge(k.sem("w_hi_done"), i * 2 + (s + 1))
        g.tensor_tensor(k.w_lo[:, s], k.w_raw[:, s], k.w_hi[:, s].bitcast(F32), ALU.subtract).then_inc(k.sem("w_split"), 1)

    for s in range(2):
        split(0, s, True)
    stop = BLK["merge2"] // 2 + 1
    with pool.Fori(1, stop) as i:
        for s in range(2):
            split(i, s, False)
    back_pool(k, pool)
    with pool.Fori(stop, n_blk // 2) as i:
        for s in range(2):
            split(i, s, False)


def program(nc, ctx, t, n_blk, out):
    k = layout(nc, ctx)
    block = ctx.enter_context(nc.Block())

    @block.sync
    def _(sp):
        sp.dma_start(k.vec[:, :], t["vec"]).then_inc(k.sem("vec_loaded"), 16)
        stream_sync(k, sp, t["w_stream"], n_blk, t["const"])
        store_sync(k, sp, out)

    @block.gpsimd
    def _(pool):
        stream_pool(k, pool, n_blk)

    @block.tensor
    def _(pe):
        pool_pe(k, pe)
        sb_pe(k, pe)
        merge_pe(k, pe, BLK["merge"], (TILE["merge"] // 2,) * 2)
        out_pe(k, pe)
        ffn_pe(k, pe)
        ple_pe(k, pe)
        latent_pe(k, pe)
        mla_pe(k, pe)
        rw_pe(k, pe)
        merge2_pe(k, pe)
        out2_pe(k, pe)

    @block.scalar
    def _(act):
        entry_act(k, act, t["x_t"])
        pool_act(k, act)
        sb_act(k, act)
        merge_act(k, act, (TILE["merge"] // 2,) * 2, None)
        out_act(k, act, t["x_t"])
        ffn_act(k, act)
        ple_act(k, act, t["p_t"])
        bridge_act(k, act, t["x1_t"], t["pos_t"])
        latent_act(k, act)
        mla_act(k, act)
        rw_act(k, act, t["w_up"], t["branches"], t["gates"])
        merge2_act(k, act, t["gates"])
        out2_act(k, act, t["x1_t"])

    @block.vector
    def _(dve):
        dve.sem_inc(k.sem("pair0_out"), 1)
        dve.sem_inc(k.sem("pair1_out"), 1)
        dve.sem_inc(k.sem("sumsq_done"), 2)
        for g in range(2):
            dve.sem_inc(k.sem(f"rw_spilled{g}"), 16)
        entry_dve(k, dve)
        pool_dve(k, dve)
        sb_dve(k, dve)
        merge_dve(k, dve, BLK["merge"], (TILE["merge"] // 2,) * 2, 0)
        merged_split_dve(k, dve, 1, 0)
        out_dve(k, dve)
        ffn_dve(k, dve)
        ple_dve(k, dve)
        bridge_dve(k, dve)
        latent_dve(k, dve)
        mla_dve(k, dve)
        rw_dve(k, dve)
        merge2_dve(k, dve)
        merged_split_dve(k, dve, 5, 1)
        out2_dve(k, dve)


def constants():
    c = np.zeros((P, N_CONST), np.float32)
    p = np.arange(P)[:, None]
    q = np.arange(P)[None, :]
    put = lambda name, a: c.__setitem__((slice(None), slice(*CONST[name])), a)
    put("ident", p == q)
    put("mean", 1.0 / D)
    put("headsum", p // HD == q // HD)
    put("neg_tri", -1.0 * (p >= q))
    put("neg_ones", -1.0)
    put("sb_mask", np.where(p >= q, NEG, 0.0))
    put("mla_mask", np.where(q > p, NEG, 0.0))
    r, f = p % HD, np.arange(HD)[None, :]
    put("pair_ident", r == f)
    put("strict_t", r < f)
    put("strict", r > f)
    put("incl_t", r <= f)
    for n in range(6):
        b = 1 << n
        put(f"lev{n}", (r // (2 * b) == f // (2 * b)) & (r // b > f // b))
    put("lev0_t", (r // 2 == f // 2) & (r < f))
    for g, w in enumerate(WINDOWS):
        a = CONST["pool_count"][0] + 16 * g
        c[:, a:a + 16] = 1.0 / np.minimum(np.arange(16) + 1, w)
    put("reset", (np.arange(HALF) % CH != 0)[None, :])
    put("rope_sum", (p >= HD) & (q >= HD) & (p % ROPE == q % ROPE))
    half = ROPE // 2
    freq = ROPE_THETA ** (-np.arange(0, ROPE, 2, dtype=np.float32) / np.float32(ROPE))
    a = CONST["rope"][0]
    c[HD:, a] = freq[np.arange(HD) % half]
    c[HD:HD + ROPE, a + 1] = 0.25
    c[HD:HD + ROPE, a + 2] = np.pi / 2
    c[HD:, a + 3] = 1.0
    c[HD + ROPE:HD + ROPE + half, a + 3] = -1.0
    return c


def tiles(w):
    return w.reshape(w.shape[0] // P, P, w.shape[1]).transpose(1, 0, 2)


def stream(i):
    blocks = []

    def put(*parts):
        b, at = np.zeros((P, SUB, P), np.float32), 0
        for a in parts:
            b[:, at:at + a.shape[1], :a.shape[2]] = a
            at += a.shape[1]
        blocks.append(b)

    col = lambda w, n: tiles(w)[:, :, n * P:(n + 1) * P]
    w_in = i["w_in"][0]
    q0, k0, v0, a0, b0 = 4, 8, 12, 16, 24
    for g in range(POOL_GROUPS):
        put(col(w_in, g))
    for g in range(PAIRS):
        put(col(w_in, q0 + g))
        put(col(w_in, k0 + g))
        put(col(w_in, v0 + g))
        put(i["w_pool"][0, g][:, None, :])
    for n in range(KT):
        put(col(w_in, a0 + n))
        put(col(w_in, b0 + n))
        put(col(i["w_branch_a"][0], n), col(i["w_branch_b"][0], n))
    for n in range(KT):
        put(col(i["w_out"][0], n))
    f = 0
    for n_f in FF_CHUNKS:
        for t in range(f, f + n_f):
            put(col(i["w_ffn_gate"][0], t))
            put(col(i["w_ffn_up"][0], t))
        for n in range(KT):
            put(col(i["w_ffn_down"][0][f * P:(f + n_f) * P], n))
        f += n_f
    for n in range(KT):
        put(col(i["w_ple_gate"][0], n))
        put(col(i["w_ple_proj"][0], n))
    w_in = i["w_in_2"]
    names = ("r", "k", "v", "wd_ad", "z_a", "c_q", "c_kv", "k_pe", "z_b", "g_a", "g_b")
    widths = (512, 512, 512, 128, 512, 256, 128, ROPE, 512, D, D)
    start = dict(zip(names, np.cumsum((0,) + widths)))
    entry = lambda name, n: tiles(w_in[:, start[name] + n * P:start[name] + (n + 1) * P])
    half = ROPE // 2
    turned = np.r_[half:ROPE, 0:half]
    k_pe = w_in[:, start["k_pe"]:start["k_pe"] + ROPE]
    put(tiles(np.concatenate([np.zeros((D, HD), np.float32), k_pe, k_pe[:, turned]], axis=1)))
    put(entry("c_kv", 0))
    put(entry("c_q", 0))
    put(entry("c_q", 1))
    w_uq = i["w_uq_2"].reshape(2 * P, 2 * PAIRS, HD + ROPE)
    w_ukv = i["w_ukv_2"].reshape(P, 2 * PAIRS, P)
    for g in range(PAIRS):
        put(*(part for h in (2 * g, 2 * g + 1) for part in
              (tiles(np.concatenate([w_uq[:, h], w_uq[:, h, HD + turned]], axis=1)), tiles(w_ukv[:, h]))))
        put(entry("z_b", g))
    put(entry("wd_ad", 0)[:, 0:4])
    put(entry("wd_ad", 0)[:, 4:8])
    for g in range(PAIRS):
        for name in ("r", "k", "v", 0, "z_a", 1, 2, 3):
            put(entry(name, g) if isinstance(name, str) else entry(("g_a", "g_b")[name % 2], (4 * g + name) // 2))
    for n in range(KT):
        put(col(i["w_out_a_2"], n), col(i["w_out_b_2"], n))
    for n in range(KT):
        put(col(i["w_o_2"], n))
    return np.stack(blocks)


def vectors(i):
    v = np.zeros((P, N_VEC), np.float32)

    def put(name, a):
        a = a.reshape(-1, P).T
        v[:, VEC[name]:VEC[name] + a.shape[1]] = a

    for name in ("norm_mix", "norm_ffn", "norm_ple", "norm_final", "pool_scale"):
        put(name, i[name])
    for name in ("g_pre", "g_post", "b_gate", "w0", "a0", "k_k", "k_a", "r_k", "gn_gain", "gn_bias", "g_q", "g_kv"):
        put(name, i[name + "_2"])
    put("mu", i["mu_shift_2"])
    return v


def kernel(**inputs):
    import concourse.bacc as bacc
    from concourse.bass_utils import run_bass_kernel_spmd

    i = {name: np.asarray(a) for name, a in inputs.items()}
    arrays = {"x_t": np.ascontiguousarray(tiles(i["x"][0].T)), "p_t": np.ascontiguousarray(tiles(i["p"][0, 0].T)),
              "w_stream": stream(i), "vec": vectors(i), "const": constants(),
              "pos_t": np.ascontiguousarray(np.broadcast_to(i["positions_2"].astype(np.int32, copy=False), (P, S))),
              "w_up": np.ascontiguousarray(np.concatenate([i["w_decay_up_2"], i["w_iclr_up_2"]]).reshape(P, PAIRS, P).transpose(1, 0, 2))}
    nc = bacc.Bacc("TRN2", target_bir_lowering=False, num_devices=1)
    t = {name: nc.dram_tensor(name, a.shape, mybir.dt.from_np(a.dtype), kind="ExternalInput").ap() for name, a in arrays.items()}
    out = nc.dram_tensor("out_t", (P, KT, S), F32, kind="ExternalOutput").ap()
    with ExitStack() as ctx:
        t["x1_t"] = nc.dram_tensor("x1_t", (P, KT, S), F32, kind="Internal").ap()
        t["gates"] = nc.dram_tensor("gates", (P, 2 * KT, S), F32, kind="Internal").ap()
        t["branches"] = nc.dram_tensor("branches", (P, BACK, S), F32, kind="Internal").ap()
        program(nc, ctx, t, len(arrays["w_stream"]), out)
    got = run_bass_kernel_spmd(nc, [arrays], core_ids=[0]).results[0]["out_t"]
    return np.ascontiguousarray(got.transpose(1, 0, 2).reshape(D, S).T)[None]
```
